# Optimizing a Trainium2 kernel written in Bass

```python
import math
import jax, jax.numpy as jnp
from jax import lax
import numpy as np

D_MODEL = 1024
BATCH = 1
SEQ = 256
DEPTH = 1

N_HEADS = 8
N_KV = 2
HEAD_DIM = 64
HPG = N_HEADS // N_KV
NSA_WIDTH = N_HEADS * HEAD_DIM
KV_WIDTH = N_KV * HEAD_DIM
ROPE_DIM = HEAD_DIM // 4
ROPE_THETA = 500000.0
CMP_BLOCK = 32
CMP_STRIDE = 16
SLC_BLOCK = 64
N_SLC = 16
WINDOW = 512
Q_BLOCK = 128
PHI_HIDDEN = 256
N_BRANCH = 3
LRU_WIDTH = D_MODEL
LRU_BLOCKS = 8
LRU_BD = LRU_WIDTH // LRU_BLOCKS
LRU_C = 8.0
CONV_W = 4
D_FF = 4 * D_MODEL
EPS = 1e-6
NEG = -1e30
FORCE_SCORE = 1e4
COL_WIDTHS = (NSA_WIDTH,) + (KV_WIDTH,) * 6 + (N_BRANCH * N_HEADS, LRU_WIDTH, LRU_WIDTH, 2 * D_MODEL)
IN_COLS = sum(COL_WIDTHS)


def rmsnorm(x, w):
    xf = x.astype(jnp.float32)
    y = xf * lax.rsqrt(jnp.mean(xf * xf, axis=-1, keepdims=True) + EPS)
    return (y * w.astype(jnp.float32)).astype(x.dtype)

def rope_partial(x, pos):
    half = ROPE_DIM // 2
    inv = ROPE_THETA ** (-jnp.arange(half, dtype=jnp.float32) / half)
    ang = pos.astype(jnp.float32)[:, None] * inv[None, :]
    cos, sin = jnp.cos(ang), jnp.sin(ang)
    xr = x[..., :ROPE_DIM].astype(jnp.float32)
    x1, x2 = xr[..., :half], xr[..., half:]
    rot = jnp.concatenate([x1 * cos - x2 * sin, x2 * cos + x1 * sin], axis=-1).astype(x.dtype)
    return jnp.concatenate([rot, x[..., ROPE_DIM:]], axis=-1)

def kv_heads(t):
    b, s, _ = t.shape
    return t.reshape(b, s, N_KV, HEAD_DIM).transpose(0, 2, 1, 3)

def compress_mlp(blocks, pos_emb, w1, w2):
    z = (blocks + pos_emb).reshape(blocks.shape[:3] + (CMP_BLOCK * HEAD_DIM,))
    return jax.nn.gelu(z @ w1) @ w2

def nsa_mixer(q_raw, kc_raw, vc_raw, ks_raw, vs_raw, kw_raw, vw_raw, g_raw,
              q_norm_w, k_norm_w, phi_k_pos, phi_k_w1, phi_k_w2, phi_v_pos, phi_v_w1, phi_v_w2):
    B, S, _ = q_raw.shape
    dt = q_raw.dtype
    scale = HEAD_DIM ** -0.5
    t = jnp.arange(S, dtype=jnp.int32)
    nqb = S // Q_BLOCK

    q = q_raw.reshape(B, S, N_KV, HPG, HEAD_DIM).transpose(0, 2, 3, 1, 4)
    q = rope_partial(rmsnorm(q, q_norm_w), t)

    n_cmp = (S - CMP_BLOCK) // CMP_STRIDE + 1
    cmp_idx = jnp.arange(n_cmp)[:, None] * CMP_STRIDE + jnp.arange(CMP_BLOCK)[None, :]
    cmp_end = cmp_idx[:, -1]
    kc = compress_mlp(kv_heads(kc_raw)[:, :, cmp_idx], phi_k_pos, phi_k_w1, phi_k_w2)
    vc = compress_mlp(kv_heads(vc_raw)[:, :, cmp_idx], phi_v_pos, phi_v_w1, phi_v_w2)
    kc = rope_partial(rmsnorm(kc, k_norm_w[0]), cmp_end)
    s_c = jnp.einsum('bghsd,bgnd->bghsn', q, kc).astype(jnp.float32) * scale
    mask_c = cmp_end[None, :] <= t[:, None]
    p_c = jax.nn.softmax(jnp.where(mask_c, s_c, NEG), axis=-1)
    p_c = jnp.where((t >= CMP_BLOCK - 1)[:, None], p_c, 0.0)
    o_cmp = jnp.einsum('bghsn,bgnd->bghsd', p_c.astype(dt), vc)

    n_slc = S // SLC_BLOCK
    n_sel = min(N_SLC, n_slc)
    blk = jnp.arange(n_slc)
    slc_lo = blk * SLC_BLOCK
    overlap = ((cmp_idx[:, 0][:, None] <= (slc_lo + SLC_BLOCK - 1)[None, :]) &
               (cmp_end[:, None] >= slc_lo[None, :])).astype(jnp.float32)
    imp = jnp.einsum('bghsn,nj->bgsj', p_c, overlap)
    cur = t // SLC_BLOCK
    forced = (blk[None, :] == 0) | (blk[None, :] == cur[:, None]) | (blk[None, :] == cur[:, None] - 1)
    causal_ok = blk[None, :] <= cur[:, None]
    score = jnp.where(causal_ok, jnp.where(forced, FORCE_SCORE, imp), NEG)
    _, sel = lax.top_k(score, n_sel)

    k_s = rope_partial(rmsnorm(kv_heads(ks_raw), k_norm_w[1]), t)
    v_s = kv_heads(vs_raw)
    b_ix = jnp.arange(B)[:, None, None]
    g_ix = jnp.arange(N_KV)[None, :, None]
    q_blk = q.reshape(B, N_KV, HPG, nqb, Q_BLOCK, HEAD_DIM).transpose(3, 0, 1, 2, 4, 5)
    sel_blk = sel.reshape(B, N_KV, nqb, Q_BLOCK, n_sel).transpose(2, 0, 1, 3, 4)
    t_blk = t.reshape(nqb, Q_BLOCK)

    def attend_selected(args):
        qb, sb, tb = args
        tok = sb[..., None] * SLC_BLOCK + jnp.arange(SLC_BLOCK)
        tok = tok.reshape(B, N_KV, Q_BLOCK * n_sel * SLC_BLOCK)
        kg = k_s[b_ix, g_ix, tok].reshape(B, N_KV, Q_BLOCK, n_sel * SLC_BLOCK, HEAD_DIM)
        vg = v_s[b_ix, g_ix, tok].reshape(B, N_KV, Q_BLOCK, n_sel * SLC_BLOCK, HEAD_DIM)
        s = jnp.einsum('bghqd,bgqkd->bghqk', qb, kg).astype(jnp.float32) * scale
        m = tok.reshape(B, N_KV, Q_BLOCK, n_sel * SLC_BLOCK) <= tb[None, None, :, None]
        p = jax.nn.softmax(jnp.where(m[:, :, None], s, NEG), axis=-1)
        return jnp.einsum('bghqk,bgqkd->bghqd', p.astype(dt), vg)

    o_slc = lax.map(attend_selected, (q_blk, sel_blk, t_blk))
    o_slc = o_slc.transpose(1, 2, 3, 0, 4, 5).reshape(B, N_KV, HPG, S, HEAD_DIM)

    k_w = rope_partial(rmsnorm(kv_heads(kw_raw), k_norm_w[2]), t)
    v_w = kv_heads(vw_raw)
    win_pos = jnp.arange(nqb)[:, None] * Q_BLOCK + jnp.arange(WINDOW + Q_BLOCK)[None, :] - WINDOW
    safe = jnp.clip(win_pos, 0, S - 1)
    kb = k_w[:, :, safe]
    vb = v_w[:, :, safe]
    qw = q.reshape(B, N_KV, HPG, nqb, Q_BLOCK, HEAD_DIM)
    s_w = jnp.einsum('bghnqd,bgnkd->bghnqk', qw, kb).astype(jnp.float32) * scale
    kp = win_pos[:, None, :]
    tq = t_blk[:, :, None]
    mask_w = (kp <= tq) & (kp > tq - WINDOW) & (kp >= 0)
    p_w = jax.nn.softmax(jnp.where(mask_w, s_w, NEG), axis=-1)
    o_win = jnp.einsum('bghnqk,bgnkd->bghnqd', p_w.astype(dt), vb).reshape(B, N_KV, HPG, S, HEAD_DIM)

    g = jax.nn.sigmoid(g_raw).reshape(B, S, N_BRANCH, N_KV, HPG).transpose(2, 0, 3, 4, 1)[..., None]
    o = g[0] * o_cmp + g[1] * o_slc + g[2] * o_win
    return o.transpose(0, 3, 1, 2, 4).reshape(B, S, NSA_WIDTH)

def rglru_mixer(xr, yr, conv_w, conv_b, lru_wa, lru_ba, lru_wx, lru_bx, lru_lambda):
    B, S, W = xr.shape
    xp = jnp.pad(xr, ((0, 0), (CONV_W - 1, 0), (0, 0)))
    xc = conv_b + sum(xp[:, j:j + S] * conv_w[j] for j in range(CONV_W))
    xb = xc.reshape(B, S, LRU_BLOCKS, LRU_BD)
    r = jax.nn.sigmoid(jnp.einsum('bsnd,nde->bsne', xb, lru_wa) + lru_ba).reshape(B, S, W)
    i_g = jax.nn.sigmoid(jnp.einsum('bsnd,nde->bsne', xb, lru_wx) + lru_bx).reshape(B, S, W)
    log_a = -LRU_C * jax.nn.softplus(-lru_lambda.astype(jnp.float32)) * r.astype(jnp.float32)
    a = jnp.exp(log_a)
    bterm = jnp.sqrt(-jnp.expm1(2.0 * log_a)) * (i_g.astype(jnp.float32) * xc.astype(jnp.float32))

    def combine(left, right):
        a1, b1 = left
        a2, b2 = right
        return a1 * a2, a2 * b1 + b2

    _, h = lax.associative_scan(combine, (a, bterm), axis=1)
    return h.astype(xr.dtype) * jax.nn.gelu(yr)

def first_inputs(seed: int = 0) -> dict:
    key = jax.random.key(seed)
    ks = jax.random.split(key, 24)
    L = DEPTH

    def nrm(k, shape, scale):
        return jax.random.normal(k, shape, jnp.float32) * scale

    u = jax.random.uniform(ks[17], (L, LRU_WIDTH), jnp.float32, 0.9, 0.999)
    a0 = u ** (1.0 / LRU_C)
    return {
        "x": nrm(ks[0], (BATCH, SEQ, D_MODEL), 1.0),
        "norm1_w": 1.0 + nrm(ks[1], (L, D_MODEL), 0.02),
        "w_in": nrm(ks[2], (L, D_MODEL, IN_COLS), D_MODEL ** -0.5),
        "q_norm_w": 1.0 + nrm(ks[3], (L, HEAD_DIM), 0.02),
        "k_norm_w": 1.0 + nrm(ks[4], (L, N_BRANCH, HEAD_DIM), 0.02),
        "phi_k_pos": nrm(ks[5], (L, CMP_BLOCK, HEAD_DIM), 0.02),
        "phi_k_w1": nrm(ks[6], (L, CMP_BLOCK * HEAD_DIM, PHI_HIDDEN), (CMP_BLOCK * HEAD_DIM) ** -0.5),
        "phi_k_w2": nrm(ks[7], (L, PHI_HIDDEN, HEAD_DIM), PHI_HIDDEN ** -0.5),
        "phi_v_pos": nrm(ks[8], (L, CMP_BLOCK, HEAD_DIM), 0.02),
        "phi_v_w1": nrm(ks[9], (L, CMP_BLOCK * HEAD_DIM, PHI_HIDDEN), (CMP_BLOCK * HEAD_DIM) ** -0.5),
        "phi_v_w2": nrm(ks[10], (L, PHI_HIDDEN, HEAD_DIM), PHI_HIDDEN ** -0.5),
        "conv_w": nrm(ks[11], (L, CONV_W, LRU_WIDTH), CONV_W ** -0.5),
        "conv_b": nrm(ks[12], (L, LRU_WIDTH), 0.01),
        "lru_wa": nrm(ks[13], (L, LRU_BLOCKS, LRU_BD, LRU_BD), LRU_BD ** -0.5),
        "lru_ba": nrm(ks[14], (L, LRU_BLOCKS, LRU_BD), 0.01),
        "lru_wx": nrm(ks[15], (L, LRU_BLOCKS, LRU_BD, LRU_BD), LRU_BD ** -0.5),
        "lru_bx": nrm(ks[16], (L, LRU_BLOCKS, LRU_BD), 0.01),
        "lru_lambda": jnp.log(a0) - jnp.log1p(-a0),
        "w_nsa_up": nrm(ks[18], (L, NSA_WIDTH, D_MODEL), NSA_WIDTH ** -0.5),
        "w_lru_up": nrm(ks[19], (L, LRU_WIDTH, D_MODEL), LRU_WIDTH ** -0.5),
        "w_o": nrm(ks[20], (L, D_MODEL, D_MODEL), D_MODEL ** -0.5),
        "norm2_w": 1.0 + nrm(ks[21], (L, D_MODEL), 0.02),
        "w_ff1": nrm(ks[22], (L, D_MODEL, D_FF), D_MODEL ** -0.5),
        "w_ff2": nrm(ks[23], (L, D_FF, D_MODEL), D_FF ** -0.5),
    }

def first_block(x, norm1_w, w_in, q_norm_w, k_norm_w, phi_k_pos, phi_k_w1, phi_k_w2,
              phi_v_pos, phi_v_w1, phi_v_w2, conv_w, conv_b, lru_wa, lru_ba, lru_wx, lru_bx,
              lru_lambda, w_nsa_up, w_lru_up, w_o, norm2_w, w_ff1, w_ff2):
    h = x
    for l in range(DEPTH):
        xn = rmsnorm(h, norm1_w[l])
        proj = xn @ w_in[l]
        parts = []
        off = 0
        for wdt in COL_WIDTHS:
            parts.append(proj[..., off:off + wdt])
            off += wdt
        q_raw, kc_raw, vc_raw, ks_raw, vs_raw, kw_raw, vw_raw, g_nsa, xr, yr, g_merge = parts

        o_nsa = nsa_mixer(q_raw, kc_raw, vc_raw, ks_raw, vs_raw, kw_raw, vw_raw, g_nsa,
                          q_norm_w[l], k_norm_w[l], phi_k_pos[l], phi_k_w1[l], phi_k_w2[l],
                          phi_v_pos[l], phi_v_w1[l], phi_v_w2[l])
        o_lru = rglru_mixer(xr, yr, conv_w[l], conv_b[l], lru_wa[l], lru_ba[l], lru_wx[l],
                            lru_bx[l], lru_lambda[l])
        gate = jax.nn.sigmoid(g_merge)
        merged = gate[..., :D_MODEL] * (o_nsa @ w_nsa_up[l]) + gate[..., D_MODEL:] * (o_lru @ w_lru_up[l])
        h = h + merged @ w_o[l]

        hn = rmsnorm(h, norm2_w[l])
        h = h + jnp.square(jax.nn.relu(hn @ w_ff1[l])) @ w_ff2[l]
    return h


DEPTH_2 = 2

D_FF_2 = 2816
D_MIX = D_MODEL
N_KV_HEADS = 2
GROUP = N_HEADS // N_KV_HEADS
ATTN_W = N_HEADS * HEAD_DIM
KV_W = N_KV_HEADS * HEAD_DIM
CONV_CH = D_MIX - ATTN_W
CONV_WIDTH = 31
WINDOW_2 = 128
BLOCK = 128
ROT_DIM = HEAD_DIM // 4
PLE_DIM = 256
IN_W = ATTN_W + 2 * KV_W + 2 * CONV_CH
SPLITS = (ATTN_W, ATTN_W + KV_W, ATTN_W + 2 * KV_W, ATTN_W + 2 * KV_W + CONV_CH)


def _rms_norm(x, g):
    xf = x.astype(jnp.float32)
    y = xf * lax.rsqrt(jnp.mean(xf * xf, axis=-1, keepdims=True) + EPS)
    return (y * g.astype(jnp.float32)).astype(x.dtype)

def _layer_norm(x, g, b):
    xf = x.astype(jnp.float32)
    mu = jnp.mean(xf, axis=-1, keepdims=True)
    xc = xf - mu
    y = xc * lax.rsqrt(jnp.mean(xc * xc, axis=-1, keepdims=True) + EPS)
    return (y * g.astype(jnp.float32) + b.astype(jnp.float32)).astype(x.dtype)

def _swiglu_ffn(x, w_gate_up, w_down):
    g, u = jnp.split(x @ w_gate_up, 2, axis=-1)
    return (jax.nn.silu(g) * u) @ w_down

def _partial_rope(x, positions):
    half = ROT_DIM // 2
    inv_freq = ROPE_THETA ** (-jnp.arange(0, ROT_DIM, 2, dtype=jnp.float32) / ROT_DIM)
    ang = positions.astype(jnp.float32)[..., None] * inv_freq
    cos = jnp.cos(ang)[:, :, None, :]
    sin = jnp.sin(ang)[:, :, None, :]
    xr = x[..., :ROT_DIM].astype(jnp.float32)
    x1, x2 = xr[..., :half], xr[..., half:]
    rot = jnp.concatenate([x1 * cos - x2 * sin, x2 * cos + x1 * sin], axis=-1).astype(x.dtype)
    return jnp.concatenate([rot, x[..., ROT_DIM:]], axis=-1)

def _sliding_window_attention(q, k, v, sinks):
    B, S, _, hd = q.shape
    nb = S // BLOCK
    qb = q.reshape(B, nb, BLOCK, N_KV_HEADS, GROUP, hd)
    kb = k.reshape(B, nb, BLOCK, N_KV_HEADS, hd)
    vb = v.reshape(B, nb, BLOCK, N_KV_HEADS, hd)
    pad = ((0, 0), (1, 0), (0, 0), (0, 0), (0, 0))
    kk = jnp.concatenate([jnp.pad(kb, pad)[:, :-1], kb], axis=2)
    vv = jnp.concatenate([jnp.pad(vb, pad)[:, :-1], vb], axis=2)
    s = jnp.einsum('bnqkgd,bnskd->bnkgqs', qb, kk).astype(jnp.float32) * (hd ** -0.5)
    qi = jnp.arange(BLOCK)[:, None] + BLOCK
    kj = jnp.arange(2 * BLOCK)[None, :]
    rel = qi - kj
    band = (rel >= 0) & (rel < WINDOW_2)
    valid = (jnp.arange(nb)[:, None, None] > 0) | (kj[None] >= BLOCK)
    mask = band[None] & valid
    s = jnp.where(mask[None, :, None, None], s, -1e30)
    sink = sinks.astype(jnp.float32).reshape(N_KV_HEADS, GROUP)[None, None, :, :, None, None]
    m = jnp.maximum(jnp.max(s, axis=-1, keepdims=True), sink)
    e = jnp.exp(s - m)
    probs = (e / (jnp.sum(e, axis=-1, keepdims=True) + jnp.exp(sink - m))).astype(v.dtype)
    o = jnp.einsum('bnkgqs,bnskd->bnqkgd', probs, vv)
    return o.reshape(B, S, N_HEADS * hd)

def _conformer_conv(a, g, w_dw, b_dw, ln_g, ln_b):
    u = a * jax.nn.sigmoid(g)
    y = lax.conv_general_dilated(
        u, w_dw[:, None, :].astype(u.dtype), window_strides=(1,),
        padding=[(CONV_WIDTH - 1, 0)],
        dimension_numbers=('NWC', 'WIO', 'NWC'),
        feature_group_count=CONV_CH) + b_dw
    return jax.nn.silu(_layer_norm(y, ln_g, ln_b))

def second_inputs(seed: int = 0) -> dict:
    key = jax.random.key(seed)
    ks = jax.random.split(key, 24)
    f32 = jnp.float32

    def w(k, shape, fan_in, scale=1.0):
        return jax.random.normal(k, shape, f32) * (scale * fan_in ** -0.5)

    def gain(k, shape):
        return 1.0 + 0.02 * jax.random.normal(k, shape, f32)

    L = DEPTH_2
    x = jax.random.normal(ks[0], (BATCH, SEQ, D_MODEL), f32)
    p = jax.random.normal(ks[1], (DEPTH_2, BATCH, SEQ, PLE_DIM), f32)
    offsets = jax.random.randint(ks[2], (BATCH, 1), 0, 1024, dtype=jnp.int32)
    positions = offsets + jnp.arange(SEQ, dtype=jnp.int32)[None, :]
    return {
        "x": x,
        "p": p,
        "positions": positions,
        "ffn1_norm": gain(ks[3], (L, D_MODEL)),
        "ffn1_w_gate_up": w(ks[4], (L, D_MODEL, 2 * D_FF_2), D_MODEL),
        "ffn1_w_down": w(ks[5], (L, D_FF_2, D_MODEL), D_FF_2),
        "mix_norm": gain(ks[6], (L, D_MODEL)),
        "w_in": w(ks[7], (L, D_MODEL, IN_W), D_MODEL),
        "sinks": 0.5 * jax.random.normal(ks[8], (L, N_HEADS), f32),
        "conv_w": w(ks[9], (L, CONV_WIDTH, CONV_CH), CONV_WIDTH),
        "conv_b": 0.02 * jax.random.normal(ks[10], (L, CONV_CH), f32),
        "conv_ln_g": gain(ks[11], (L, CONV_CH)),
        "conv_ln_b": 0.02 * jax.random.normal(ks[12], (L, CONV_CH), f32),
        "attn_out_norm": gain(ks[13], (L, ATTN_W)),
        "conv_out_norm": gain(ks[14], (L, CONV_CH)),
        "w_out": w(ks[15], (L, D_MIX, D_MODEL), D_MIX),
        "ffn2_norm": gain(ks[16], (L, D_MODEL)),
        "ffn2_w_gate_up": w(ks[17], (L, D_MODEL, 2 * D_FF_2), D_MODEL),
        "ffn2_w_down": w(ks[18], (L, D_FF_2, D_MODEL), D_FF_2),
        "w_ple": w(ks[19], (L, PLE_DIM, D_MODEL), PLE_DIM),
        "ple_norm": gain(ks[20], (L, D_MODEL)),
        "w_ple_gate": w(ks[21], (L, D_MODEL, D_MODEL), D_MODEL),
        "final_norm": gain(ks[22], (D_MODEL,)),
    }

def second_block(x, p, positions, ffn1_norm, ffn1_w_gate_up, ffn1_w_down, mix_norm, w_in,
              sinks, conv_w, conv_b, conv_ln_g, conv_ln_b, attn_out_norm, conv_out_norm,
              w_out, ffn2_norm, ffn2_w_gate_up, ffn2_w_down, w_ple, ple_norm, w_ple_gate,
              final_norm):
    B, S, _ = x.shape
    h = x
    for i in range(DEPTH_2):
        h = h + 0.5 * _swiglu_ffn(_rms_norm(h, ffn1_norm[i]), ffn1_w_gate_up[i], ffn1_w_down[i])
        u = _rms_norm(h, mix_norm[i])
        q, k, v, ca, cg = jnp.split(u @ w_in[i], SPLITS, axis=-1)
        q = _partial_rope(q.reshape(B, S, N_HEADS, HEAD_DIM), positions)
        k = _partial_rope(k.reshape(B, S, N_KV_HEADS, HEAD_DIM), positions)
        v = v.reshape(B, S, N_KV_HEADS, HEAD_DIM)
        attn = _sliding_window_attention(q, k, v, sinks[i])
        conv = _conformer_conv(ca, cg, conv_w[i], conv_b[i], conv_ln_g[i], conv_ln_b[i])
        mixed = jnp.concatenate([_rms_norm(attn, attn_out_norm[i]),
                                 _rms_norm(conv, conv_out_norm[i])], axis=-1)
        h = h + mixed @ w_out[i]
        h = h + 0.5 * _swiglu_ffn(_rms_norm(h, ffn2_norm[i]), ffn2_w_gate_up[i], ffn2_w_down[i])
        e = _rms_norm(p[i] @ w_ple[i], ple_norm[i])
        h = h + jax.nn.sigmoid(h @ w_ple_gate[i]) * e
    return _rms_norm(h, final_norm)


def setup_inputs(seed=0):
    out = dict(first_inputs(seed))
    for name, value in second_inputs(seed + 1).items():
        if name != "x":
            out[name + "_2"] = value
    return out


def reference(
    x, norm1_w, w_in, q_norm_w, k_norm_w, phi_k_pos, phi_k_w1, phi_k_w2, phi_v_pos, phi_v_w1,
    phi_v_w2, conv_w, conv_b, lru_wa, lru_ba, lru_wx, lru_bx, lru_lambda, w_nsa_up, w_lru_up,
    w_o, norm2_w, w_ff1, w_ff2, p_2, positions_2, ffn1_norm_2, ffn1_w_gate_up_2, ffn1_w_down_2,
    mix_norm_2, w_in_2, sinks_2, conv_w_2, conv_b_2, conv_ln_g_2, conv_ln_b_2, attn_out_norm_2,
    conv_out_norm_2, w_out_2, ffn2_norm_2, ffn2_w_gate_up_2, ffn2_w_down_2, w_ple_2, ple_norm_2,
    w_ple_gate_2, final_norm_2,
):
    x = first_block(
        x, norm1_w, w_in, q_norm_w, k_norm_w, phi_k_pos, phi_k_w1, phi_k_w2, phi_v_pos,
        phi_v_w1, phi_v_w2, conv_w, conv_b, lru_wa, lru_ba, lru_wx, lru_bx, lru_lambda,
        w_nsa_up, w_lru_up, w_o, norm2_w, w_ff1, w_ff2,
    )
    return second_block(
        x, p_2, positions_2, ffn1_norm_2, ffn1_w_gate_up_2, ffn1_w_down_2, mix_norm_2, w_in_2,
        sinks_2, conv_w_2, conv_b_2, conv_ln_g_2, conv_ln_b_2, attn_out_norm_2, conv_out_norm_2,
        w_out_2, ffn2_norm_2, ffn2_w_gate_up_2, ffn2_w_down_2, w_ple_2, ple_norm_2,
        w_ple_gate_2, final_norm_2,
    )


_drawn_inputs = setup_inputs


def setup_inputs(seed=0):
    import zlib

    import numpy as np

    out = dict(_drawn_inputs(seed))
    spreads = {}
    factors = {'norm1_w': 6.987,
     'q_norm_w': 8.0,
     'k_norm_w': 8.0,
     'phi_k_pos': 8.0,
     'phi_v_pos': 64.0,
     'conv_b': 3.979,
     'lru_ba': 22.187,
     'lru_bx': 8.0,
     'norm2_w': 3.159,
     'ffn1_norm_2': 8.0,
     'mix_norm_2': 3.561,
     'sinks_2': 44.008,
     'conv_ln_g_2': 37.936,
     'conv_ln_b_2': 43.544,
     'attn_out_norm_2': 46.048,
     'conv_out_norm_2': 48.432,
     'ffn2_norm_2': 8.0,
     'ple_norm_2': 59.728,
     'final_norm_2': 8.677,
     'conv_b_2': 8.0}
    for name, (base, spread) in spreads.items():
        noise = np.random.default_rng([zlib.crc32(name.encode()), seed]).standard_normal(out[name].shape)
        drawn = base * np.exp(spread * noise) if base else spread * noise
        out[name] = __import__('jax').numpy.asarray(drawn.astype(out[name].dtype))
    for name, factor in factors.items():
        out[name] = (out[name] * factor).astype(out[name].dtype)
    return out
```

```python
from contextlib import ExitStack

import numpy as np

import concourse.bass as bass
from concourse import mybir

F32 = mybir.dt.float32
F32R = mybir.dt.float32r
I32 = mybir.dt.int32
ALU = mybir.AluOpType
ACT = mybir.ActivationFunctionType
AX_X = mybir.AxisListType.X

P = 128
S = 256
TT = S // P
D = 1024
KD = D // P
COLS = 512
UNIT_K = 2
EPS = 1e-6
NEG = -1e30
HEADS, HD, KV = 8, 64, 2
PAIRS = HEADS // 2
ROT = HD // 4
HALF = ROT // 2
THETA = 500000.0
CMP_BLOCK, CMP_STRIDE = 32, 16
NCMP = (S - CMP_BLOCK) // CMP_STRIDE + 1
ROWS_C = KV * NCMP
KPHI = CMP_BLOCK * HD // P
PHI = 256
TAPS1 = 4
FF1 = 4096
KF1 = FF1 // P
OFF_KV, OFF_KW, OFF_XR, OFF_YR, OFF_GM = 512, 1024, 1304, 2328, 3352
W_KW = OFF_XR - OFF_KW
LAYERS = 2
FF2 = 2816
KF2 = FF2 // P
TAPS2 = 31
CONV = 512
KC = CONV // P
WINDOW = 128
PLE = 256
KPLE = PLE // P
HALFW = COLS // 2
UPS = FF2 // HALFW

STAGE, SPLIT = 8, 4

V1 = dict(norm1=0, norm2=8, conv_w=16, conv_b=48, ba=56, bx=64, lam=72, pos_k=80, pos_v=96)
NV1 = 112
V2 = dict(ffn1=0, mix=8, ffn2=16, attn=24, conv=28, conv_b=32, ln_g=36, ln_b=40)
NV2 = 44

C_ID, C_M1, C_M2, C_ROPE, C_ROPEC, C_CMASK, C_ROWOK, C_INV, C_SEL, C_SELM, C_EPS, C_END = np.cumsum(
    [0, P, S, S, TT * 2 * ROT, 2 * ROT, TT * NCMP, TT, HALF, HEADS * NCMP, HEADS, 1]).tolist()


class Count:

    def __init__(self, const, terms=()):
        self.const, self.terms = const, [t for t in terms if t[0] is not None and t[1]]

    def __add__(self, n):
        return Count(self.const + n, self.terms)

    def slot(self, n):
        assert all(c % n == 0 for _, c in self.terms)
        return self.const % n

    def lap(self, n):
        assert all(c % n == 0 for _, c in self.terms)
        return Count(self.const // n, [(r, c // n) for r, c in self.terms])

    def value(self, times=1):
        v = self.const * times
        for r, c in self.terms:
            v = r * (c * times) + v
        return v


def wait(eng, sem, count, times=1):
    v = count.value(times)
    if not isinstance(v, int) or v > 0:
        eng.wait_ge(sem, v)


class Plan:

    def __init__(self, before, layer):
        self.start, n = {}, 0
        for name, k in before:
            self.start[name] = (n, False)
            n += k
        self.per_layer = 0
        for name, k in layer:
            self.start[name] = (n + self.per_layer, True)
            self.per_layer += k

    def at(self, name, k=0, layer=None, step=None, per_step=0):
        n, looped = self.start[name]
        assert looped == (layer is not None), name
        return Count(n + k, [(layer, self.per_layer), (step, per_step)])


def units_of(k_tiles, per=UNIT_K):
    return k_tiles // per


U = units_of(KD)
NF = FF1 // COLS
_FIRST = ["xr0", "xr1", "q", "ks", "kw", "yr0", "yr1"]
_U1 = ([(n, U) for n in _FIRST] + [("phi_k", units_of(KPHI)), ("phi_v", units_of(KPHI))]
       + [(f"gm{i}", U) for i in range(4)]
       + [("nsa0", units_of(4)), ("lru0", U), ("nsa1", units_of(4)), ("lru1", U), ("o0", U), ("o1", U)]
       + [(f"f{i}", U) for i in range(NF)] + [("d0", units_of(KF1)), ("d1", units_of(KF1))])
_U2 = ([(f"a_up{i}", U) for i in range(UPS)] + [("a_dn0", units_of(KF2)), ("a_dn1", units_of(KF2))]
       + [(n, U) for n in ("ca", "cg", "q", "kv", "out0", "out1")]
       + [(f"b_up{i}", U) for i in range(UPS)] + [("b_dn0", units_of(KF2)), ("b_dn1", units_of(KF2))]
       + [("ple0", units_of(KPLE, 1)), ("ple1", units_of(KPLE, 1)), ("gate0", U), ("gate1", U)])
_U2 = [("L" + n, k) for n, k in _U2]
N_UNITS = dict(_U1 + _U2)
UNITS = Plan(_U1, _U2)
CHUNKS = Plan([(n, 1) for n, _ in _U1 if not n.startswith("phi")], [(n, 1) for n, _ in _U2])
TURNS = Plan([("norm1", 4), ("xr", 4), ("q", 2), ("k", 2), ("z", 2), ("hid", 1), ("kc", 1), ("pc", 1),
              ("yr", 4), ("slc", 8), ("win", 8), ("nsa", 2), ("merged", 4), ("norm2", 4), ("ff", 2 * NF)],
             [("La_norm", 4), ("La_hid", UPS), ("Lmix", 4), ("Lu", 2), ("Lq", 2), ("Lk", 1), ("Latt", 8),
              ("Lmixed", 2), ("Lb_norm", 4), ("Lb_hid", UPS), ("Lp", 1), ("Lraw", 4)])
HI_TURNS = Plan([("norm1", 4), ("nsa", 2), ("merged", 4), ("norm2", 4), ("ff", 2 * NF)],
                [("La_norm", 4), ("La_hid", UPS), ("Lmix", 4), ("Lmixed", 2), ("Lb_norm", 4), ("Lb_hid", UPS),
                 ("Lp", 1), ("Lraw", 4)])
NORMS = Plan([("norm1", 1), ("norm2", 1)], [("La_norm", 1), ("Lmix", 1), ("Lmixed", 1), ("Lb_norm", 1)])
ROOTS = Plan([("qk", 1), ("lru", 1), ("kc", 1)], [("Lple", 1)])
HIDDEN = Plan([("ff", NF)], [("La_hid", UPS), ("Lb_hid", UPS)])
RESIDUAL = Plan([("o", 2), ("d", 2)], [("La_dn", 2), ("Lout", 2), ("Lb_dn", 2), ("Lgate", 2)])
SCORES = Plan([("vec", 2), ("gates", 4), ("hid", 1), ("cmp", 1), ("slc", 8), ("win", 8)],
              [("Latt", 8), ("Lsum", 3)])
OUTS = Plan([("vec", 2), ("gates", 4), ("kvc", 1), ("vb", 1), ("cmp", TT), ("slc", 8), ("win", 8)],
            [("Latt", 8)])
HEAD_PAIRS = Plan([("slc", 8), ("win", 8)], [("Latt", 8)])

DVE_LINKS = 73
ACT_LINKS = 4
POOL_LINKS = 2 * TAPS2 - 1


class Chain:

    def __init__(self, eng, sem, per_layer):
        self.eng, self.sem, self.per_layer = eng, sem, per_layer
        self.n, self.layer, self.first = 0, None, 0

    def enter(self, layer):
        self.layer, self.first = layer, self.n

    def leave(self, layers):
        assert self.n - self.first == self.per_layer, (self.n - self.first, self.per_layer)
        self.n, self.layer = self.first + layers * self.per_layer, None

    def link(self, ins):
        self.n += 1
        ins.then_inc(self.sem, 1)
        wait(self.eng, self.sem, Count(self.n, [(self.layer, self.per_layer)]))


def heads_of(x, p):
    return x.rearrange("q (g a i d) -> q g i a d", g=KV, a=2, i=2)[:, p // 2, p % 2, :, :]


def constants():
    c = np.zeros((P, C_END), np.float32)
    i, j = np.arange(P)[:, None], np.arange(P)[None, :]
    c[:, C_ID:C_ID + P] = i == j
    causal = np.where(j <= i, 0.0, NEG)
    c[:, C_M1 + P:C_M1 + S] = causal
    c[:, C_M2:C_M2 + P] = np.where(i + P - j < WINDOW, 0.0, NEG)
    c[:, C_M2 + P:C_M2 + S] = causal
    inv = (THETA ** (-np.arange(HALF, dtype=np.float64) / HALF)).astype(np.float32)

    def rope(pos):
        ang = (pos.astype(np.float32)[:, None] * inv[None, :]).astype(np.float64)
        return np.concatenate([np.cos(ang), np.cos(ang), -np.sin(ang), np.sin(ang)], 1)

    ends = np.arange(NCMP) * CMP_STRIDE + CMP_BLOCK - 1
    for t in range(TT):
        tok = t * P + np.arange(P)
        c[:, C_ROPE + t * 2 * ROT:C_ROPE + (t + 1) * 2 * ROT] = rope(tok)
        c[:, C_CMASK + t * NCMP:C_CMASK + (t + 1) * NCMP] = np.where(ends[None, :] <= tok[:, None], 0.0, NEG)
        c[:, C_ROWOK + t] = tok >= CMP_BLOCK - 1
    c[:ROWS_C, C_ROPEC:C_ROPEC + 2 * ROT] = np.tile(rope(ends), (KV, 1))
    c[:, C_INV:C_INV + HALF] = inv
    for head in range(HEADS):
        for n in range(NCMP):
            c[(head // (HEADS // KV)) * NCMP + n, C_SEL + head * NCMP + n] = 1.0
            c[head * NCMP + n, C_SELM + head] = 1.0
    c[:, C_EPS] = EPS
    return c


def build(nc, a, consts, out, layers=LAYERS):
    ctx = ExitStack()
    with ctx:
        def sb(name, shape, dt=F32, stack=ctx):
            return stack.enter_context(nc.sbuf_tensor(name, shape, dt))

        def sem(name):
            return ctx.enter_context(nc.semaphore(name))

        def overlay(stack, *groups):
            made, free, least = [], nc.sbuf_bytes_remaining, nc.sbuf_bytes_remaining
            for group in groups:
                with ExitStack() as own:
                    made += [sb(*spec, stack=own) for spec in group]
                    least = min(least, nc.sbuf_bytes_remaining)
            sb(f"room_{groups[0][0][0]}", [P, -(-(free - least) // 4)], stack=stack)
            return made

        stage = sb("stage", [P, STAGE, UNIT_K, COLS])
        w_hi = sb("w_hi", [P, SPLIT, UNIT_K, COLS], F32R)
        w_lo = sb("w_lo", [P, SPLIT, UNIT_K, COLS], F32R)
        x_hi = sb("x_hi", [P, KD, S], F32R)
        x_lo = sb("x_lo", [P, KD, S], F32R)
        h = sb("h", [P, TT, D])
        xs = sb("xs", [P, TT, D])
        ct = sb("ct", [P, C_END])
        stat = sb("stat", [P, 12])
        vec1 = sb("vec1", [P, NV1])
        vec2 = sb("vec2", [P, LAYERS, NV2])
        taps2 = sb("taps2", [P, LAYERS, TAPS2 * KC])
        sinks = sb("sinks", [P, LAYERS, HEADS])
        vcur = sb("vcur", [P, NV2])
        tcur = sb("tcur", [P, TAPS2 * KC])
        scur = sb("scur", [P, HEADS])
        pos_i = sb("pos_i", [P, TT], I32)
        pos_f = sb("pos_f", [P, TT])
        ang = sb("ang", [P, 3, TT, HALF])
        rope2 = sb("rope2", [P, TT, 2 * ROT])
        mx = sb("mx", [P, 2, 2])
        negm = sb("negm", [P, 2, 2])
        den = sb("den", [P, 2, 2])
        esink = sb("esink", [P, 2, 2])
        coef = sb("coef", [P, 2])
        ident, eps = ct[:, C_ID:C_ID + P], ct[:, C_EPS:C_EPS + 1]

        attn, mixer, mlp, lay = ExitStack(), ExitStack(), ExitStack(), ExitStack()
        qk = sb("qk", [P, TT, 12, HD], stack=attn)
        vv = sb("vv", [P, TT, 2, P], stack=attn)
        kd = sb("kd", [P, TT, 4, 2, HD], stack=attn)
        q_t = sb("q_t", [P, PAIRS, S], stack=attn)
        k_t = sb("k_t", [P, 4, S], stack=attn)
        sm = sb("sm", [P, 2, 2, S], stack=attn)
        p_t = sb("p_t", [P, 2, TT, P], stack=attn)
        ropet = sb("ropet", [P, TT, 12, ROT], stack=attn)
        tmpo = sb("tmpo", [P, 2, HD], stack=attn)
        mixo, z = overlay(attn, [("mixo", [P, TT, 512])], [("z", [P, 4, S])])
        x_rt, gy, raw1, raw2, rawt, gate = overlay(
            mixer, [("x_rt", [P, KD, TAPS1 - 1 + S]), ("gy", [P, TT, D])],
            [("raw1", [NV1, P]), ("raw2", [LAYERS * NV2, P]), ("rawt", [TAPS2 * KC, LAYERS, P])],
            [("gate", [P, TT, 2 * D])])
        lru_r, lru_i, lru_hi, lru_lo = overlay(
            mixer, [("lru_r", [P, KD, S]), ("lru_i", [P, KD, S])],
            [("lru_hi", [P, KD, S], F32R), ("lru_lo", [P, KD, S], F32R)])
        w_gates, nsa_hi, nsa_lo = overlay(
            mixer, [("w_gates", [P, 2, KD, P])], [("nsa_hi", [P, 4, S], F32R), ("nsa_lo", [P, 4, S], F32R)])
        xc = sb("xc", [P, KD, S], stack=mixer)
        cd = sb("cd", [P, TT, 4, 2, HD], stack=mixer)
        zj_hi = sb("zj_hi", [P, 2, KPHI, ROWS_C], F32R, stack=mixer)
        zj_lo = sb("zj_lo", [P, 2, KPHI, ROWS_C], F32R, stack=mixer)
        zj, pc, pc_t = overlay(mixer, [("zj", [P, KPHI, KV, NCMP])],
                               [("pc", [P, TT, HEADS, NCMP]), ("pc_t", [HEADS * NCMP, S])])
        gsig = sb("gsig", [P, TT, 3, HEADS], stack=mixer)
        softp = sb("softp", [P, 9, KD], stack=mixer)
        qk_ss = sb("qk_ss", [P, TT * 12], stack=mixer)
        w_phi2 = sb("w_phi2", [P, 2, 2, HD], stack=mixer)
        ghid = sb("ghid", [ROWS_C, 2 * PHI], stack=mixer)
        ghid_t = sb("ghid_t", [P, 4, ROWS_C], stack=mixer)
        kvc = sb("kvc", [ROWS_C, 2, HD], stack=mixer)
        kcs = sb("kcs", [ROWS_C, HD], stack=mixer)
        kcd = sb("kcd", [ROWS_C, 2, HD], stack=mixer)
        kcr = sb("kcr", [ROWS_C, ROT + 1], stack=mixer)
        knw = sb("knw", [P, HD], stack=mixer)
        qkw = sb("qkw", [P, 12, HD], stack=mixer)
        kb = sb("kb", [P, KV, 2, NCMP], stack=mixer)
        vb = sb("vb", [HEADS * NCMP, HEADS, HD], stack=mixer)
        pcs = sb("pcs", [P, 2, TT, HEADS], stack=mixer)
        mixer.close()
        u = sb("u", [P, TT, CONV], stack=attn)
        y = sb("y", [P, KC, S], stack=attn)
        ysq = sb("ysq", [P, KC, S], stack=attn)
        attn.close()
        f_hi = sb("f_hi", [P, KF1, S], F32R, stack=mlp)
        f_lo = sb("f_lo", [P, KF1, S], F32R, stack=mlp)
        hid1 = sb("hid1", [P, 2, TT, COLS], stack=mlp)
        relu = sb("relu", [P, 2, TT, COLS], stack=mlp)
        mlp.close()
        g_hi = sb("g_hi", [P, KF2, S], F32R, stack=lay)
        g_lo = sb("g_lo", [P, KF2, S], F32R, stack=lay)
        hid2 = sb("hid2", [P, 2, TT, HALFW], stack=lay)
        silu = sb("silu", [P, 2, TT, HALFW], stack=lay)
        sig = sb("sig", [P, TT, COLS], stack=lay)
        u_t = sb("u_t", [P, KC, TAPS2 - 1 + S], stack=lay)
        pin = sb("pin", [P, LAYERS, TT, PLE], stack=lay)
        pcur = sb("pcur", [P, TT, PLE], stack=lay)
        pl_hi = sb("pl_hi", [P, KPLE, S], F32R, stack=lay)
        pl_lo = sb("pl_lo", [P, KPLE, S], F32R, stack=lay)
        e_ple = sb("e_ple", [P, TT, D], stack=lay)
        gn = sb("gn", [P, LAYERS + 1, D], stack=lay)
        mean = sb("mean", [P, P], stack=lay)
        lay.close()
        merged, sq, th = xs, xs[:, :, 0:12 * HD], x_rt[:, :, 0:S]
        den2 = xs[:, :, :].rearrange("p t (f s) -> p (t f) s", s=S)

        acc = [ctx.enter_context(nc.psum_tensor(f"acc{i}", [P, TT, COLS], F32)) for i in range(2)]
        turn = [ctx.enter_context(nc.psum_tensor(f"turn{i}", [P, 512], F32)) for i in range(2)]
        score = ctx.enter_context(nc.psum_tensor("score", [P, 512], F32))
        outp = ctx.enter_context(nc.psum_tensor("outp", [P, 512], F32))

        s_x = sem("s_x")
        s_table = sem("s_table")
        s_const = sem("s_const")
        s_vecs2 = sem("s_vecs2")
        s_small = sem("s_small")
        s_late = sem("s_late")
        s_zero = sem("s_zero")
        s_pcur = sem("s_pcur")
        landed = [sem(f"landed{i}") for i in range(STAGE)]
        hi_done = sem("hi_done")
        lo_done = sem("lo_done")
        unit_used = sem("unit_used")
        acc_free = [sem(f"acc_free{i}") for i in range(2)]
        turn_done = sem("turn_done")
        turn_hi = sem("turn_hi")
        turn_free = [sem(f"turn_free{i}") for i in range(2)]
        score_done, score_free = sem("score_done"), sem("score_free")
        out_done, out_free = sem("out_done"), sem("out_free")
        dve_chain, act_chain, pool_chain = sem("dve_chain"), sem("act_chain"), sem("pool_chain")
        s_rms = sem("s_rms")
        s_xs = sem("s_xs")
        s_sums, s_roots = sem("s_sums"), sem("s_roots")
        s_h = sem("s_h")
        s_vec = sem("s_vec")
        s_lam = sem("s_lam")
        s_elam = sem("s_elam")
        s_soft = sem("s_soft")
        s_xc = sem("s_xc")
        s_ab = sem("s_ab")
        s_olru = sem("s_olru")
        s_lruhi = sem("s_lruhi")
        s_lrulo = sem("s_lrulo")
        s_qk = sem("s_qk")
        s_kd = sem("s_kd")
        s_zj = sem("s_zj")
        s_zjhi = sem("s_zjhi")
        s_zjlo = sem("s_zjlo")
        s_kcd = sem("s_kcd")
        s_pcm = sem("s_pcm")
        s_pce = sem("s_pce")
        s_negm = sem("s_negm")
        s_exp = sem("s_exp")
        s_mixo = sem("s_mixo")
        s_merged = sem("s_merged")
        s_rl = sem("s_rl")
        s_hid = sem("s_hid")
        s_ang = sem("s_ang")
        s_rope2 = sem("s_rope2")
        s_cur = sem("s_cur")
        s_y = sem("s_y")
        s_ypool = sem("s_ypool")
        s_ysq = sem("s_ysq")
        s_yn = sem("s_yn")
        s_silu = sem("s_silu")
        s_convhi = sem("s_convhi")
        s_convlo = sem("s_convlo")
        s_ple = sem("s_ple")
        s_result = sem("s_result")
        s_out = sem("s_out")

        def rows(w):
            return w.rearrange("(k p) n -> p k n", p=P)

        def layer_rows(w):
            return w.rearrange("l (k p) n -> l p k n", p=P)

        win1 = rows(a["w_in"][0])
        FIRST_COL = {"xr0": OFF_XR, "xr1": OFF_XR + COLS, "q": 0, "ks": OFF_KV, "kw": OFF_KW, "yr0": OFF_YR,
                     "yr1": OFF_YR + COLS, **{f"gm{i}": OFF_GM + i * COLS for i in range(4)}}
        view1 = {"nsa": rows(a["w_nsa_up"][0]), "lru": rows(a["w_lru_up"][0]), "o": rows(a["w_o"][0]),
                 "d": rows(a["w_ff2"][0])}
        phi1 = {"phi_k": rows(a["phi_k_w1"][0]), "phi_v": rows(a["phi_v_w1"][0])}
        ff1 = rows(a["w_ff1"][0])
        win2, wout2 = layer_rows(a["w_in_2"]), layer_rows(a["w_out_2"])
        win2_flat = a["w_in_2"].rearrange("l (k p) n -> p (l k) n", p=P)
        up2 = {"a": layer_rows(a["ffn1_w_gate_up_2"]), "b": layer_rows(a["ffn2_w_gate_up_2"])}
        dn2 = {"a": layer_rows(a["ffn1_w_down_2"]), "b": layer_rows(a["ffn2_w_down_2"])}
        wple, wpleg = layer_rows(a["w_ple_2"]), layer_rows(a["w_ple_gate_2"])
        L_COL = {"Lkv": HEADS * HD, "Lca": HEADS * HD + 2 * KV * HD,
                 "Lcg": HEADS * HD + 2 * KV * HD + CONV}

        def width(name):
            return W_KW if name == "kw" else 2 * KV * HD if name == "Lkv" else PHI if name in phi1 else COLS

        def tiles_of(name):
            return 1 if name.startswith("Lple") else UNIT_K

        def evacuated(eng, name, layer=None):
            n = CHUNKS.at(name, 0, layer)
            wait(eng, acc_free[n.slot(2)], n.lap(2) + 1)

        def turn_read(eng, name, k, layer=None):
            n = TURNS.at(name, k, layer)
            wait(eng, turn_free[n.slot(2)], n.lap(2) + 1)

        def turns_read(eng, name, count, layer=None):
            for k in range(max(0, count - 2), count):
                turn_read(eng, name, k, layer)

        block = ctx.enter_context(nc.Block())

        @block.sync
        def _(sp):
            def load(name, source, layer=None, step=None, per_step=0, k=0):
                for i in range(N_UNITS[name]):
                    n = UNITS.at(name, i + k, layer, step, per_step)
                    t = tiles_of(name)
                    src = source(i * t, t)
                    if n.const >= STAGE:
                        wait(sp, lo_done, n + (1 - STAGE))
                    sp.dma_start(stage[:, n.slot(STAGE), 0:t, 0:width(name)],
                                 src).then_inc(landed[n.slot(STAGE)], 16)

            def plain(view, c0, w=COLS):
                return lambda k0, t: view[:, k0:k0 + t, c0:c0 + w]

            def of_layer(view, layer, c0, w=COLS):
                return lambda k0, t: view[bass.ds(layer, 1), :, k0:k0 + t, c0:c0 + w].rearrange(
                    "o p k n -> (o p) k n")

            for t in range(TT):
                sp.dma_start(h[:, t, :], a["x"][0, t * P:(t + 1) * P, :]).then_inc(s_x, 16)
            for name in _FIRST:
                load(name, plain(win1, FIRST_COL[name], width(name)))
            for name in phi1:
                load(name, plain(phi1[name], 0, PHI))
            for i in range(4):
                load(f"gm{i}", plain(win1, FIRST_COL[f"gm{i}"]))
            for name in ["nsa0", "lru0", "nsa1", "lru1", "o0", "o1"]:
                load(name, plain(view1[name[:-1]], int(name[-1]) * COLS))
            with sp.Fori(0, NF // 2) as j:
                for i in range(2):
                    load("f0", lambda k0, t: ff1[:, k0:k0 + t, bass.ds(j * (2 * COLS) + i * COLS, COLS)],
                         step=j, per_step=2 * U, k=i * U)
            for name in ["d0", "d1"]:
                load(name, plain(view1["d"], int(name[-1]) * COLS))

            def swiglu_loads(f, layer):
                load(f"L{f}_up0", of_layer(up2[f], layer, 0), layer)
                with sp.Fori(0, (UPS - 1) // 2) as j:
                    for i in range(2):
                        load(f"L{f}_up1", lambda k0, t: up2[f][bass.ds(layer, 1), :, k0:k0 + t,
                             bass.ds(j * (2 * COLS) + (1 + i) * COLS, COLS)].rearrange("o p k n -> (o p) k n"),
                             layer, step=j, per_step=2 * U, k=i * U)
                for c in range(2):
                    load(f"L{f}_dn{c}", of_layer(dn2[f], layer, c * COLS), layer)

            with sp.Fori(0, layers) as layer:
                swiglu_loads("a", layer)
                for name in ["Lca", "Lcg"]:
                    load(name, of_layer(win2, layer, L_COL[name]), layer)
                load("Lq", lambda k0, t: win2_flat[:, bass.ds(layer * KD + k0, t), 0:COLS], layer)
                load("Lkv", of_layer(win2, layer, L_COL["Lkv"], width("Lkv")), layer)
                for c in range(2):
                    load(f"Lout{c}", of_layer(wout2, layer, c * COLS), layer)
                swiglu_loads("b", layer)
                for c in range(2):
                    load(f"Lple{c}", of_layer(wple, layer, c * COLS), layer)
                for c in range(2):
                    load(f"Lgate{c}", of_layer(wpleg, layer, c * COLS), layer)
            for t in range(TT):
                sp.wait_ge(s_result, t + 1)
                sp.dma_start(out[0, t * P:(t + 1) * P, :], xs[:, t, :]).then_inc(s_out, 16)
            sp.wait_ge(s_out, 16 * TT)

        @block.gpsimd
        def _(pool):
            chain = Chain(pool, pool_chain, POOL_LINKS)
            for i in range(2):
                w = a[["lru_wa", "lru_wx"][i]][0]
                pool.dma_start(w_gates[:, i, :, :], w.rearrange("n d e -> d n e")).then_inc(s_small, 16)
                w = a[["phi_k_w2", "phi_v_w2"][i]][0]
                pool.dma_start(w_phi2[:, i, :, :], w.rearrange("(k p) d -> p k d", p=P)).then_inc(s_small, 16)
            for i in range(12):
                w = a["q_norm_w"][0] if i < HEADS else a["k_norm_w"][0, 1 + (i - HEADS) // KV]
                pool.dma_start(qkw[:, i, :], w.partition_broadcast(P)).then_inc(s_small, 16)
            pool.dma_start(knw[:, :], a["k_norm_w"][0, 0].partition_broadcast(P)).then_inc(s_small, 16)
            pool.memset(kb[:, :, :, :], 0.0).then_inc(s_zero, 1)
            wait(pool, s_h, RESIDUAL.at("d", 2))
            pool.dma_start(pin[:, :, :, :], a["p_2"].rearrange("l o (t p) n -> p (l o) t n", p=P)).then_inc(s_late, 16)
            for l in range(LAYERS):
                pool.dma_start(gn[:, l, :], a["ple_norm_2"][l].partition_broadcast(P)).then_inc(s_late, 16)
            pool.dma_start(gn[:, LAYERS, :], a["final_norm_2"].partition_broadcast(P)).then_inc(s_late, 16)
            pool.memset(u_t[:, :, 0:TAPS2 - 1], 0.0).then_inc(s_zero, 1)
            pool.memset(mean[:, :], 1.0 / CONV).then_inc(s_zero, 1)
            pool.wait_ge(s_late, 16 * (LAYERS + 2))
            pool.wait_ge(s_zero, 3)
            with pool.Fori(0, layers) as layer:
                chain.enter(layer)
                pool.wait_ge(s_cur, layer + 1)
                pool.tensor_copy(pcur[:, :, :], pin[:, bass.ds(layer, 1), :, :].rearrange("p o t n -> p (o t) n")
                                 ).then_inc(s_pcur, 1)
                n = KC - 1
                turns_read(pool, "Lu", 2, layer)
                def tap(j):
                    return tcur[:, j * KC + n:j * KC + n + 1].to_broadcast([P, S])
                chain.link(pool.tensor_tensor(y[:, n, :], u_t[:, n, 0:S], tap(0), ALU.mult))
                bias = vcur[:, V2["conv_b"] + n:V2["conv_b"] + n + 1].to_broadcast([P, S])
                chain.link(pool.tensor_tensor(y[:, n, :], y[:, n, :], bias, ALU.add))
                for j in range(1, TAPS2):
                    chain.link(pool.tensor_tensor(ysq[:, n, :], u_t[:, n, j:j + S], tap(j), ALU.mult))
                    ins = pool.tensor_tensor(y[:, n, :], y[:, n, :], ysq[:, n, :], ALU.add)
                    if j < TAPS2 - 1:
                        chain.link(ins)
                ins.then_inc(s_ypool, 1)
                chain.leave(layers)

        @block.scalar
        def _(act):
            def split(name, layer=None, step=None, per_step=0, k=0, units=None):
                for i in units if units is not None else range(N_UNITS[name]):
                    n = UNITS.at(name, i + k, layer, step, per_step)
                    wait(act, landed[n.slot(STAGE)], n.lap(STAGE) + 1, 16)
                    if n.const >= SPLIT:
                        wait(act, unit_used, n + (1 - SPLIT))
                    t, w = tiles_of(name), width(name)
                    act.activation(w_hi[:, n.slot(SPLIT), 0:t, 0:w], stage[:, n.slot(STAGE), 0:t, 0:w],
                                   ACT.Copy).then_inc(hi_done, 1)

            def chunk_done(name, layer=None, step=None, k=0):
                wait(act, unit_used, UNITS.at(name, k * N_UNITS[name] + N_UNITS[name], layer, step, 2 * N_UNITS[name]))
                return CHUNKS.at(name, k, layer, step, 2).slot(2)

            chain = Chain(act, act_chain, ACT_LINKS)

            def squares(src, width=D, at=0):
                for t in range(TT):
                    ins = act.activation(xs[:, t, 0:width], src[:, t, :], ACT.Square, scale=1.0 / width ** 0.5,
                                         accum_out=stat[:, at + t:at + t + 1])
                chain.link(ins)
                act.activation(stat[:, at:at + TT], stat[:, at:at + TT], ACT.Sqrt, bias=eps).then_inc(s_rms, 1)

            def root(dst, name, scale=1.0, bias=None, layer=None):
                n = ROOTS.at(name, 1, layer)
                wait(act, s_sums, n)
                act.activation(dst, dst, ACT.Sqrt, bias=0.0 if bias is None else bias, scale=scale).then_inc(s_roots, 1)

            def turned_hi(dst, name, k, gain=None, layer=None, step=None, per_step=0, at=None):
                n = TURNS.at(name, k, layer, step, per_step)
                wait(act, turn_done, n + 1)
                bank = turn[n.slot(2)][:, :].rearrange("p (k s) -> p k s", k=2)
                at = 2 * k if at is None else at
                if gain is None:
                    act.activation(dst[:, bass.ds(at, 2), :], bank, ACT.Copy).then_inc(turn_hi, 1)
                else:
                    for i in range(2):
                        ins = act.activation(dst[:, at + i, :], bank[:, i, :], ACT.Copy, scale=gain[:, at + i:at + i + 1])
                    ins.then_inc(turn_hi, 1)

            def turned_copy(dst, name, k, layer=None):
                n = TURNS.at(name, k, layer)
                wait(act, turn_done, n + 1)
                act.activation(dst, turn[n.slot(2)][:, :].rearrange("p (k s) -> p k s", k=2),
                               ACT.Copy).then_inc(turn_free[n.slot(2)], 1)

            def exps(name, j, sink, layer=None):
                w, b = P * (j // PAIRS + 1), j % 2
                wait(act, s_negm, HEAD_PAIRS.at(name, j + 1, layer))
                if sink:
                    act.activation(esink[:, b, :], esink[:, b, :], ACT.Exp)
                for i in range(2):
                    ins = act.activation(sm[:, b, i, 0:w], sm[:, b, i, 0:w], ACT.Exp,
                                         bias=negm[:, b, i:i + 1], accum_out=den[:, b, i:i + 1])
                ins.then_inc(s_exp, 1)

            def exps_t(name, j, layer=None):
                t = j // PAIRS
                n = TURNS.at(name, j, layer)
                wait(act, turn_done, n + 1)
                act.activation(p_t[:, :, 0:t + 1, :],
                               turn[n.slot(2)][:, 0:2 * (t + 1) * P].rearrange("p (i s q) -> p i s q", i=2, q=P),
                               ACT.Copy).then_inc(turn_free[n.slot(2)], 1)

            def attention(name, sink, layer=None):
                exps(name, 0, sink, layer)
                for j in range(2 * PAIRS):
                    if j + 1 < 2 * PAIRS:
                        exps(name, j + 1, sink, layer)
                    exps_t(name, j, layer)

            act.dma_start(ct[:, :], consts).then_inc(s_table, 16)

            def vector_rows(dst, row, v, done):
                act.dma_start(dst[row:row + v.shape[-1] // P, :], v.rearrange("(r p) -> r p", p=P)).then_inc(done, 16)

            for name, v in [("norm1", a["norm1_w"][0]), ("norm2", a["norm2_w"][0]), ("conv_b", a["conv_b"][0]),
                            ("lam", a["lru_lambda"][0])]:
                vector_rows(raw1, V1[name], v, s_const)
            act.dma_start(raw1[V1["conv_w"]:V1["conv_w"] + TAPS1 * KD, :],
                          a["conv_w"][0].rearrange("j (r p) -> (j r) p", p=P)).then_inc(s_const, 16)
            act.dma_start(raw1[V1["ba"]:V1["ba"] + KD, :], a["lru_ba"][0]).then_inc(s_const, 16)
            act.dma_start(raw1[V1["bx"]:V1["bx"] + KD, :], a["lru_bx"][0]).then_inc(s_const, 16)
            for name in ["k", "v"]:
                act.dma_start(raw1[V1["pos_" + name]:V1["pos_" + name] + KPHI, :],
                              a[f"phi_{name}_pos"][0].rearrange("(j l) d -> j (l d)", l=2)).then_inc(s_const, 16)
            act.wait_ge(s_x, 16 * TT)
            act.wait_ge(s_table, 16)
            squares(h)
            for l in range(LAYERS):
                for name, v in [("ffn1", "ffn1_norm_2"), ("mix", "mix_norm_2"), ("ffn2", "ffn2_norm_2"),
                                ("attn", "attn_out_norm_2"), ("conv", "conv_out_norm_2"), ("conv_b", "conv_b_2"),
                                ("ln_g", "conv_ln_g_2"), ("ln_b", "conv_ln_b_2")]:
                    vector_rows(raw2, l * NV2 + V2[name], a[v][l], s_vecs2)
                act.dma_start(rawt[:, l, :], a["conv_w_2"][l].rearrange("j (r p) -> (j r) p", p=P)).then_inc(s_vecs2, 16)
            act.dma_start(sinks[:, :, :], a["sinks_2"].partition_broadcast(P)).then_inc(s_vecs2, 16)
            for t in range(TT):
                act.dma_start(pos_i[:, t:t + 1], a["positions_2"][0, t * P:(t + 1) * P].unsqueeze(1)).then_inc(s_vecs2, 16)
            split("xr0")
            act.wait_ge(s_vec, 1)
            for k in range(4):
                turned_hi(x_hi, "norm1", k, vec1[:, V1["norm1"]:V1["norm1"] + KD])
            act.wait_ge(s_lam, 1)
            act.activation(softp[:, 3, :], softp[:, 2, :], ACT.Exp).then_inc(s_elam, 1)
            split("xr1")
            act.wait_ge(s_vec, 4)
            for c in range(2):
                split(["q", "ks"][c])
                b = chunk_done(f"xr{c}")
                act.activation(gy[:, :, c * COLS:(c + 1) * COLS], acc[b][:, :, :], ACT.Copy).then_inc(acc_free[b], 1)
            for k in range(4):
                turned_copy(x_rt[:, 2 * k:2 * k + 2, TAPS1 - 1:], "xr", k)
            split("kw")
            b = chunk_done("q")
            act.activation(qk[:, :, 0:HEADS, :], acc[b][:, :, :].rearrange("p t (n d) -> p t n d", d=HD),
                           ACT.Copy).then_inc(acc_free[b], 1)
            split("yr0")
            b = chunk_done("ks")
            for i in range(2):
                act.activation(cd[:, :, :, i, :], acc[b][:, :, 0:2 * KV * HD].rearrange("p t (n d) -> p t n d", d=HD),
                               ACT.Copy)
            act.activation(qk[:, :, HEADS:HEADS + KV, :],
                           acc[b][:, :, 256:384].rearrange("p t (n d) -> p t n d", d=HD), ACT.Copy)
            act.activation(vv[:, :, 0, :], acc[b][:, :, 384:512], ACT.Copy).then_inc(acc_free[b], 1)
            split("yr1")
            b = chunk_done("kw")
            act.activation(qk[:, :, HEADS + KV:, :], acc[b][:, :, 0:P].rearrange("p t (n d) -> p t n d", d=HD), ACT.Copy)
            act.activation(vv[:, :, 1, :], acc[b][:, :, P:2 * P], ACT.Copy)
            act.activation(gsig[:, :, :, :], acc[b][:, :, 2 * P:W_KW].rearrange("p t (b n) -> p t b n", b=3),
                           ACT.Sigmoid).then_inc(acc_free[b], 1)
            root(qk_ss[:, :], "qk", bias=eps)
            split("phi_k", units=range(4))
            for k in range(4):
                for plan, done, free, bank, dst, bias in [
                        (SCORES, score_done, score_free, score, lru_r, "ba"), (OUTS, out_done, out_free, outp, lru_i, "bx")]:
                    wait(act, done, plan.at("gates", k + 1))
                    for m in range(2):
                        f = 2 * k + m
                        ins = act.activation(dst[:, f, :], bank[:, m * S:(m + 1) * S], ACT.Sigmoid,
                                             bias=vec1[:, V1[bias] + f:V1[bias] + f + 1])
                    ins.then_inc(free, 1)
            wait(act, score_free, SCORES.at("gates", 4))
            act.wait_ge(s_soft, 1)
            for f in range(KD):
                act.activation(th[:, f, :], lru_r[:, f, :], ACT.Tanh, scale=softp[:, 0, f:f + 1])
            for f in range(KD):
                ins = act.activation(lru_r[:, f, :], lru_r[:, f, :], ACT.Exp, scale=softp[:, 1, f:f + 1])
            ins.then_inc(s_ab, 1)
            root(den2, "lru", scale=2.0)
            for c in range(2):
                b = chunk_done(f"yr{c}")
                act.activation(gy[:, :, c * COLS:(c + 1) * COLS], acc[b][:, :, :],
                               ACT.Gelu_apprx_tanh).then_inc(acc_free[b], 1)
            for k in range(2):
                turned_copy(q_t[:, 2 * k:2 * k + 2, :], "q", k)
            for k in range(2):
                turned_copy(k_t[:, 2 * k:2 * k + 2, :], "k", k)
            for k in range(2):
                n = TURNS.at("z", k)
                wait(act, turn_done, n + 1)
                bank = turn[n.slot(2)][:, :].rearrange("p (k s) -> p k s", k=2)
                act.activation(z[0:HD, 2 * k:2 * k + 2, :], bank[0:HD, :, :], ACT.Copy)
                act.activation(z[HD:P, 2 * k:2 * k + 2, 0:S - 1], bank[HD:P, :, 1:S],
                               ACT.Copy).then_inc(turn_free[n.slot(2)], 1)
            for i in range(2):
                act.wait_ge(s_zj, i + 1)
                act.activation(zj_hi[:, i, :, :], zj[:, :, :, :].rearrange("p j g n -> p j (g n)"),
                               ACT.Copy).then_inc(s_zjhi, 1)
            split("phi_k", units=range(4, 8))
            split("phi_v")
            split("gm0")
            wait(act, unit_used, UNITS.at("phi_v", 8))
            act.activation(ghid[:, :], score[0:ROWS_C, :], ACT.Gelu_apprx_tanh).then_inc(score_free, 1)
            n = TURNS.at("hid")
            wait(act, turn_done, n + 1)
            act.activation(ghid_t[:, :, :],
                           turn[n.slot(2)][:, 0:4 * ROWS_C].rearrange("p (k s) -> p k s", k=4),
                           ACT.Copy).then_inc(turn_free[n.slot(2)], 1)
            root(kcr[:, ROT:ROT + 1], "kc", bias=eps[0:ROWS_C, :])
            act.wait_ge(s_pcm, 1)
            act.activation(pc[:, :, :, :], pc[:, :, :, :], ACT.Exp).then_inc(s_pce, 1)
            n = TURNS.at("pc")
            wait(act, turn_done, n + 1)
            act.activation(pc_t[:, :], turn[n.slot(2)][0:HEADS * NCMP, 0:S], ACT.Copy).then_inc(turn_free[n.slot(2)], 1)
            for k in range(4):
                act.wait_ge(s_olru, k + 1)
                act.activation(lru_hi[:, 2 * k:2 * k + 2, :], xc[:, 2 * k:2 * k + 2, :], ACT.Copy).then_inc(s_lruhi, 1)

            def gate_chunk(c):
                b = chunk_done(f"gm{c}")
                act.activation(gate[:, :, c * COLS:(c + 1) * COLS], acc[b][:, :, :], ACT.Sigmoid).then_inc(acc_free[b], 1)

            split("gm1")
            gate_chunk(0)
            split("gm2")
            gate_chunk(1)
            attention("slc", False)
            split("gm3")
            gate_chunk(2)
            attention("win", False)
            split("nsa0")
            split("lru0", units=range(2))
            gate_chunk(3)
            for k in range(2):
                turned_hi(nsa_hi, "nsa", k)
            split("lru0", units=range(2, 4))
            for name in ["nsa1", "lru1", "o0"]:
                split(name)
            for k in range(4):
                turned_hi(x_hi, "merged", k)
            split("o1")
            split("f0")
            wait(act, s_h, RESIDUAL.at("o", 2))
            squares(h)
            for k in range(4):
                turned_hi(x_hi, "norm2", k, vec1[:, V1["norm2"]:V1["norm2"] + KD])

            def relu_chunk(i, step=None):
                b = chunk_done("f0", None, step, i)
                act.activation(relu[:, i % 2, :, :], acc[b][:, :, :], ACT.Relu).then_inc(s_rl, 1)

            def ff_hi(i, step=None):
                for m in range(2):
                    k = 2 * i + m
                    turned_hi(f_hi, "ff", k, None, None, step, 4, 2 * k if step is None else step * 8 + 2 * k)

            split("f1")
            relu_chunk(0)
            with act.Fori(0, NF // 2 - 1) as j:
                for i in (1, 2):
                    split("f0", None, j, 2 * U, (i + 1) * U)
                    relu_chunk(i, j)
                    ff_hi(i - 1, j)
            split("d0", units=range(U))
            relu_chunk(NF - 1)
            ff_hi(NF - 2)
            ff_hi(NF - 1)
            split("d0", units=range(U, N_UNITS["d0"]))
            split("d1")
            act.wait_ge(s_ang, 1)
            for m in range(2):
                act.activation(rope2[:, :, m * HALF:(m + 1) * HALF], ang[:, 1, :, :], ACT.Sin)
            act.activation(rope2[:, :, 2 * HALF:3 * HALF], ang[:, 0, :, :], ACT.Sin, scale=-1.0)
            act.activation(rope2[:, :, 3 * HALF:4 * HALF], ang[:, 0, :, :], ACT.Sin).then_inc(s_rope2, 1)

            def swiglu(f, gain, before, layer):
                split(f"L{f}_up0", layer)
                wait(act, s_h, before)
                squares(h)
                if f == "a":
                    act.wait_ge(s_cur, layer + 1)
                for k in range(4):
                    turned_hi(x_hi, f"L{f}_norm", k, vcur[:, V2[gain]:V2[gain] + KD], layer)

                def silu_chunk(i, step=None):
                    b = chunk_done(f"L{f}_up0", layer, step, i)
                    act.activation(silu[:, i % 2, :, :], acc[b][:, :, 0:HALFW], ACT.Silu).then_inc(s_rl, 1)

                def hid_hi(i, step=None):
                    turned_hi(g_hi, f"L{f}_hid", i, None, layer, step, 2, 2 * i if step is None else step * 4 + 2 * i)

                split(f"L{f}_up1", layer)
                silu_chunk(0)
                with act.Fori(0, (UPS - 1) // 2 - 1) as j:
                    for i in (1, 2):
                        split(f"L{f}_up0", layer, j, 2 * U, (i + 1) * U)
                        silu_chunk(i, j)
                        hid_hi(i - 1, j)
                split(f"L{f}_up{UPS - 1}", layer)
                silu_chunk(UPS - 2)
                hid_hi(UPS - 3)
                split(f"L{f}_dn0", layer, units=range(U))
                silu_chunk(UPS - 1)
                hid_hi(UPS - 2)
                hid_hi(UPS - 1)
                split(f"L{f}_dn0", layer, units=range(U, N_UNITS[f"L{f}_dn0"]))
                split(f"L{f}_dn1", layer)

            with act.Fori(0, layers) as layer:
                chain.enter(layer)
                swiglu("a", "ffn1", RESIDUAL.at("La_dn", 0, layer), layer)
                split("Lca", layer)
                wait(act, s_h, RESIDUAL.at("La_dn", 2, layer))
                squares(h)
                for k in range(4):
                    turned_hi(x_hi, "Lmix", k, vcur[:, V2["mix"]:V2["mix"] + KD], layer)
                split("Lcg", layer)
                split("Lq", layer)
                b = chunk_done("Lcg", layer)
                act.activation(sig[:, :, :], acc[b][:, :, :], ACT.Sigmoid).then_inc(acc_free[b], 1)
                split("Lkv", layer)
                b = chunk_done("Lq", layer)
                act.activation(qk[:, :, 0:HEADS, :], acc[b][:, :, :].rearrange("p t (n d) -> p t n d", d=HD),
                               ACT.Copy, scale=HD ** -0.5).then_inc(acc_free[b], 1)
                act.wait_ge(s_zero, 3)
                for k in range(2):
                    turned_copy(u_t[:, 2 * k:2 * k + 2, TAPS2 - 1:], "Lu", k, layer)
                split("Lout0", layer)
                b = chunk_done("Lkv", layer)
                act.activation(qk[:, :, HEADS:HEADS + KV, :],
                               acc[b][:, :, 0:P].rearrange("p t (n d) -> p t n d", d=HD), ACT.Copy)
                act.activation(vv[:, :, 0, :], acc[b][:, :, P:2 * P], ACT.Copy).then_inc(acc_free[b], 1)
                for k in range(2):
                    turned_copy(q_t[:, 2 * k:2 * k + 2, :], "Lq", k, layer)
                turned_copy(k_t[:, 0:2, :], "Lk", 0, layer)
                attention("Latt", True, layer)
                wait(act, s_mixo, Count(2, [(layer, 1)]))
                squares(mixo, CONV, TT)
                for k in range(2):
                    turned_hi(x_hi, "Lmixed", k, vcur[:, V2["attn"]:V2["attn"] + 4], layer)
                def sums_root(i):
                    n = SCORES.at("Lsum", i, layer)
                    wait(act, score_done, n + 1)
                    act.activation(sig[:, 0, 0:S], score[:, 0:S], ACT.Sqrt, bias=eps).then_inc(score_free, 1)

                wait(act, score_free, SCORES.at("Lsum", 1, layer))
                act.activation(ysq[:, :, :], y[:, :, :], ACT.Square).then_inc(s_ysq, 1)
                sums_root(1)
                wait(act, s_yn, Count(1, [(layer, 2)]))
                for n in range(KC):
                    ins = act.activation(y[:, n, :], y[:, n, :], ACT.Silu, scale=vcur[:, V2["ln_g"] + n:V2["ln_g"] + n + 1],
                                         bias=vcur[:, V2["ln_b"] + n:V2["ln_b"] + n + 1])
                ins.then_inc(s_silu, 1)
                act.wait_ge(s_silu, layer + 1)
                act.activation(ysq[:, :, :], y[:, :, :], ACT.Square).then_inc(s_ysq, 1)
                sums_root(2)
                wait(act, s_yn, Count(2, [(layer, 2)]))
                for n in range(KC):
                    ins = act.activation(x_hi[:, 4 + n, :], y[:, n, :], ACT.Copy,
                                         scale=vcur[:, V2["conv"] + n:V2["conv"] + n + 1])
                ins.then_inc(s_convhi, 1)
                split("Lout1", layer)
                swiglu("b", "ffn2", RESIDUAL.at("Lout", 2, layer), layer)
                split("Lple0", layer)
                turned_hi(pl_hi, "Lp", 0, None, layer)
                split("Lple1", layer)
                split("Lgate0", layer, units=range(2))
                for c in range(2):
                    b = chunk_done(f"Lple{c}", layer)
                    for t in range(TT):
                        squared = sig[:, t, :] if c == 0 else ysq[:, 2 * t:2 * t + 2, :].rearrange("p k s -> p (k s)")
                        act.activation(squared, acc[b][:, t, :], ACT.Square, scale=1.0 / D ** 0.5,
                                       accum_out=stat[:, 4 + 2 * t + c:5 + 2 * t + c]).then_inc(s_ple, 1)
                root(stat[:, 8:8 + TT], "Lple", bias=eps, layer=layer)
                for k in range(4):
                    turned_hi(x_hi, "Lraw", k, None, layer)
                split("Lgate0", layer, units=range(2, 4))
                split("Lgate1", layer)
                for c in range(2):
                    b = chunk_done(f"Lgate{c}", layer)
                    if c == 1:
                        wait(act, s_h, RESIDUAL.at("Lgate", 1, layer))
                    act.activation(sig[:, :, :], acc[b][:, :, :], ACT.Sigmoid).then_inc(acc_free[b], 1)
                chain.leave(layers)
            act.wait_ge(s_h, 4 + RESIDUAL.per_layer * layers)
            squares(h)

        @block.vector
        def _(dve):
            chain = Chain(dve, dve_chain, DVE_LINKS)
            link = chain.link

            def split(name, layer=None, step=None, per_step=0, k=0, units=None):
                for i in units if units is not None else range(N_UNITS[name]):
                    n = UNITS.at(name, i + k, layer, step, per_step)
                    wait(dve, hi_done, n + 1)
                    t, w = tiles_of(name), width(name)
                    dve.tensor_tensor(w_lo[:, n.slot(SPLIT), 0:t, 0:w], stage[:, n.slot(STAGE), 0:t, 0:w],
                                      w_hi[:, n.slot(SPLIT), 0:t, 0:w].bitcast(F32), ALU.subtract).then_inc(lo_done, 1)

            def chunk_done(name, layer=None):
                wait(dve, unit_used, UNITS.at(name, N_UNITS[name], layer))
                return CHUNKS.at(name, 0, layer).slot(2)

            def normalise(name, layer=None):
                wait(dve, s_rms, NORMS.at(name, 1, layer))
                link(dve.reciprocal(stat[:, 0:TT], stat[:, 0:TT]))
                for t in range(TT):
                    ins = dve.tensor_scalar(xs[:, t, :], h[:, t, :], stat[:, t:t + 1], None, ALU.mult)
                ins.then_inc(s_xs, 1)

            def rooted(ins, name, layer=None):
                ins.then_inc(s_sums, 1)
                wait(dve, s_roots, ROOTS.at(name, 1, layer))

            def turned_lo(hi, lo, name, k, gain=None, layer=None, step=None, per_step=0, at=None):
                n = TURNS.at(name, k, layer, step, per_step)
                wait(dve, turn_hi, HI_TURNS.at(name, k + 1, layer, step, per_step))
                bank = turn[n.slot(2)][:, :].rearrange("p (k s) -> p k s", k=2)
                at = 2 * k if at is None else at
                if gain is None:
                    dve.tensor_tensor(lo[:, bass.ds(at, 2), :], bank, hi[:, bass.ds(at, 2), :].bitcast(F32),
                                      ALU.subtract).then_inc(turn_free[n.slot(2)], 1)
                else:
                    for i in range(2):
                        ins = dve.scalar_tensor_tensor(lo[:, at + i, :], bank[:, i, :], gain[:, at + i:at + i + 1],
                                                       hi[:, at + i, :].bitcast(F32), ALU.mult, ALU.subtract)
                    ins.then_inc(turn_free[n.slot(2)], 1)

            def add_residual(name, c, scale, layer=None):
                b = chunk_done(name, layer)
                hc = h[:, :, c * COLS:(c + 1) * COLS]
                dve.scalar_tensor_tensor(hc, acc[b][:, :, :], scale, hc, ALU.mult, ALU.add).then_inc(acc_free[b], 1)
                evacuated(dve, name, layer)
                dve.sem_inc(s_h, 1)

            def rotate(x, table, tmp, x1_x2):
                lo, hi = x1_x2
                dve.tensor_tensor(tmp[0], hi, table(2), ALU.mult)
                link(dve.tensor_tensor(tmp[1], lo, table(3), ALU.mult))
                dve.tensor_tensor(lo, lo, table(0), ALU.mult)
                link(dve.tensor_tensor(hi, hi, table(1), ALU.mult))
                dve.tensor_tensor(lo, lo, tmp[0], ALU.add)
                return dve.tensor_tensor(hi, hi, tmp[1], ALU.add)

            def rotate_heads(heads, table):
                x = qk[:, :, 0:heads, :]
                def part(i):
                    return table[:, :, i * HALF:(i + 1) * HALF].unsqueeze(2).to_broadcast([P, TT, heads, HALF])
                return rotate(x, part, [ropet[:, :, 0:heads, 0:HALF], ropet[:, :, 0:heads, HALF:ROT]],
                              (x[:, :, :, 0:HALF], x[:, :, :, HALF:ROT]))

            def mask_scores(name, j, mask, sink, layer=None):
                t, p, b, w = j // PAIRS, j % PAIRS, j % 2, P * (j // PAIRS + 1)
                n = SCORES.at(name, j, layer)
                wait(dve, score_done, n + 1)
                m = ct[:, mask + S - w:mask + S].unsqueeze(1).to_broadcast([P, 2, w])
                dve.tensor_tensor(sm[:, b, :, 0:w], score[:, 0:2 * w].rearrange("p (i s) -> p i s", i=2), m,
                                  ALU.add).then_inc(score_free, 1)
                wait(dve, score_free, n + 1)
                link(dve.tensor_reduce(mx[:, b, :], sm[:, b, :, 0:w], AX_X, ALU.max))
                if sink:
                    sink = heads_of(scur[:, :], p).rearrange("q a d -> q (a d)")
                    link(dve.tensor_tensor(mx[:, b, :], mx[:, b, :], sink, ALU.max))
                    dve.tensor_tensor(esink[:, b, :], sink, mx[:, b, :], ALU.subtract)
                dve.tensor_scalar(negm[:, b, :], mx[:, b, :], -1.0, None, ALU.mult).then_inc(s_negm, 1)

            def weigh_output(name, j, branch, sink, layer=None):
                t, p, b = j // PAIRS, j % PAIRS, j % 2
                wait(dve, s_exp, HEAD_PAIRS.at(name, j + 1, layer))
                if sink:
                    link(dve.tensor_tensor(den[:, b, :], den[:, b, :], esink[:, b, :], ALU.add))
                link(dve.reciprocal(coef[:, :], den[:, b, :]))
                if branch is not None:
                    link(dve.tensor_tensor(coef[:, :], coef[:, :],
                                           heads_of(gsig[:, t, branch, :], p).rearrange("q a d -> q (a d)"), ALU.mult))
                n = OUTS.at(name, j, layer)
                wait(dve, out_done, n + 1)
                o = heads_of(mixo[:, t, :], p)
                res = outp[:, 0:2 * HD].rearrange("p (n d) -> p n d", d=HD)
                cb = coef[:, :].unsqueeze(2).to_broadcast([P, 2, HD])
                dve.tensor_tensor(o if branch is None else tmpo[:, :, :], res, cb, ALU.mult).then_inc(out_free, 1)
                wait(dve, out_free, n + 1)
                if branch is not None:
                    link(dve.tensor_tensor(o, o, tmpo[:, :, :], ALU.add))

            def attention(name, mask, branch, sink, layer=None, between=lambda j: None):
                mask_scores(name, 0, mask, sink, layer)
                for j in range(2 * PAIRS):
                    if j + 1 < 2 * PAIRS:
                        mask_scores(name, j + 1, mask, sink, layer)
                    between(j)
                    weigh_output(name, j, branch, sink, layer)

            def vector_in(k, plan, done, free, bank, dst, cols):
                wait(dve, done, plan.at("vec", k + 1))
                dve.tensor_copy(dst, bank[:, 0:cols]).then_inc(free, 1)
                wait(dve, free, plan.at("vec", k + 1))
                dve.sem_inc(s_vec, 1)

            vector_in(0, SCORES, score_done, score_free, score, vec1[:, :], NV1)
            normalise("norm1")
            split("xr0")
            for k in range(4):
                turned_lo(x_hi, x_lo, "norm1", k, vec1[:, V1["norm1"]:V1["norm1"] + KD])
            lam = vec1[:, V1["lam"]:V1["lam"] + KD]
            dve.scalar_tensor_tensor(softp[:, 2, :], lam, -1.0, lam, ALU.mult, ALU.min).then_inc(s_lam, 1)
            vector_in(0, OUTS, out_done, out_free, outp, vec2[:, :, :].rearrange("p l v -> p (l v)"), LAYERS * NV2)
            vector_in(1, SCORES, score_done, score_free, score, taps2[:, 0, :], TAPS2 * KC)
            vector_in(1, OUTS, out_done, out_free, outp, taps2[:, 1, :], TAPS2 * KC)
            dve.memset(x_rt[:, :, 0:TAPS1 - 1], 0.0)
            split("xr1")
            dve.wait_ge(s_elam, 1)
            e, z1, z2, s = (softp[:, i, :] for i in (3, 4, 5, 6))
            link(dve.tensor_scalar(z2, e, 2.0, None, ALU.add))
            link(dve.reciprocal(z2, z2))
            link(dve.tensor_tensor(z1, e, z2, ALU.mult))
            link(dve.tensor_tensor(z2, z1, z1, ALU.mult))
            link(dve.tensor_scalar(s, z2, 1.0 / 19, None, ALU.mult))
            for odd in range(17, 1, -2):
                link(dve.scalar_tensor_tensor(s, s, 1.0 / odd, z2, ALU.add, ALU.mult))
            link(dve.scalar_tensor_tensor(s, s, 1.0, z1, ALU.add, ALU.mult))
            link(dve.tensor_scalar(z1, lam, -8.0, 0.0, ALU.mult, ALU.max))
            link(dve.scalar_tensor_tensor(softp[:, 0, :], s, 16.0, z1, ALU.mult, ALU.add))
            dve.tensor_scalar(softp[:, 1, :], softp[:, 0, :], -1.0, None, ALU.mult).then_inc(s_soft, 1)
            for name in ["q", "ks"]:
                split(name)
            for k in range(4):
                turn_read(dve, "xr", k)
            for j in range(TAPS1):
                for f in range(KD):
                    wj = vec1[:, V1["conv_w"] + j * KD + f:V1["conv_w"] + j * KD + f + 1]
                    if j == 0:
                        ins = dve.tensor_scalar(xc[:, f, :], x_rt[:, f, 0:S], wj,
                                                vec1[:, V1["conv_b"] + f:V1["conv_b"] + f + 1], ALU.mult, ALU.add)
                    else:
                        ins = dve.scalar_tensor_tensor(xc[:, f, :], x_rt[:, f, j:j + S], wj, xc[:, f, :],
                                                       ALU.mult, ALU.add)
                if j < TAPS1 - 1:
                    link(ins)
                if j == 1:
                    split("kw")
            ins.then_inc(s_xc, 1)
            split("yr0")
            for name in ["q", "ks", "kw"]:
                evacuated(dve, name)
            dve.wait_ge(s_small, 16 * 17)
            turns_read(dve, "norm1", 4)
            qk_flat = qk[:, :, :, :].rearrange("p t n d -> p t (n d)")
            heads = qk[:, :, :, :].rearrange("p t n d -> p (t n) d")
            ss = qk_ss[:, :]
            link(dve.scalar_tensor_tensor(sq, qk_flat, 1.0 / HD, qk_flat, ALU.mult, ALU.mult))
            rooted(dve.tensor_reduce(ss.rearrange("p (t n) -> p t n", t=TT), sq.rearrange("p t (n d) -> p t n d", d=HD),
                                     AX_X, ALU.add), "qk")
            link(dve.reciprocal(ss, ss))
            ssq = ss.rearrange("p (t n) -> p t n", t=TT)[:, :, 0:HEADS]
            link(dve.tensor_scalar(ssq, ssq, HD ** -0.5, None, ALU.mult))
            link(dve.tensor_tensor(heads, heads, ss.unsqueeze(2).to_broadcast([P, TT * 12, HD]), ALU.mult))
            for t in range(TT):
                ins = dve.tensor_tensor(qk[:, t, :, :], qk[:, t, :, :], qkw[:, :, :], ALU.mult)
            link(ins)
            rotate_heads(12, ct[:, C_ROPE:C_ROPE + TT * 2 * ROT].rearrange("p (t r) -> p t r", t=TT)).then_inc(s_qk, 1)
            dve.wait_ge(s_qk, 1)
            for i in range(2):
                ins = dve.tensor_copy(kd[:, :, :, i, :], qk[:, :, HEADS:, :])
            ins.then_inc(s_kd, 1)
            split("yr1")
            split("phi_k", units=range(4))
            dve.wait_ge(s_ab, 1)
            wait(dve, out_free, OUTS.at("gates", 4))
            link(dve.tensor_scalar(den2, th, 1.0, None, ALU.add))
            link(dve.reciprocal(den2, den2))
            ins = dve.tensor_tensor(den2, den2, th, ALU.mult)
            rooted(ins, "lru")
            link(dve.tensor_tensor(lru_i[:, :, :], lru_i[:, :, :], xc[:, :, :], ALU.mult))
            link(dve.tensor_tensor(lru_i[:, :, :], lru_i[:, :, :], den2, ALU.mult))
            for f in range(KD):
                ins = dve.tensor_tensor_scan(xc[:, f, :], lru_r[:, f, :], lru_i[:, f, :], 0.0, ALU.mult, ALU.add)
            link(ins)
            for i in range(2):
                turn_read(dve, "z", i)
                if i == 1:
                    dve.wait_ge(s_zjlo, 1)
                zi = z[:, 2 * i:2 * i + 2, :]
                src = bass.AP(zi.tensor, zi.offset, [zi.ap[0], [2, KPHI], [S, KV], [CMP_STRIDE, NCMP]])
                pos = vec1[:, V1["pos_" + "kv"[i]]:V1["pos_" + "kv"[i]] + KPHI]
                dve.tensor_tensor(zj[:, :, :, :], src, pos.unsqueeze(2).unsqueeze(3).to_broadcast([P, KPHI, KV, NCMP]),
                                  ALU.add).then_inc(s_zj, 1)
                dve.wait_ge(s_zjhi, i + 1)
                dve.tensor_tensor(zj_lo[:, i, :, :], zj[:, :, :, :].rearrange("p j g n -> p j (g n)"),
                                  zj_hi[:, i, :, :].bitcast(F32), ALU.subtract).then_inc(s_zjlo, 1)
            split("phi_k", units=range(4, 8))
            split("phi_v")
            split("gm0")
            wait(dve, out_done, OUTS.at("kvc", 1))
            dve.tensor_copy(kvc[:, :, :], outp[0:ROWS_C, 0:2 * HD].rearrange("p (i d) -> p i d", i=2)).then_inc(out_free, 1)
            wait(dve, out_free, OUTS.at("kvc", 1))
            kc, rt = kvc[:, 0, :], kcr[:, ROT:ROT + 1]
            link(dve.scalar_tensor_tensor(kcs[:, :], kc, 1.0 / HD, kc, ALU.mult, ALU.mult))
            rooted(dve.tensor_reduce(rt, kcs[:, :], AX_X, ALU.add), "kc")
            link(dve.reciprocal(rt, rt))
            link(dve.scalar_tensor_tensor(kc, kc, rt, knw[0:ROWS_C, :], ALU.mult, ALU.mult))
            link(rotate(kc, lambda i: ct[0:ROWS_C, C_ROPEC + i * HALF:C_ROPEC + (i + 1) * HALF],
                        [kcr[:, 0:HALF], kcr[:, HALF:ROT]], (kc[:, 0:HALF], kc[:, HALF:ROT])))
            for i in range(2):
                ins = dve.tensor_copy(kcd[:, i, :], kc)
            ins.then_inc(s_kcd, 1)
            dve.wait_ge(s_zero, 1)
            n = TURNS.at("kc")
            wait(dve, turn_done, n + 1)
            for i in range(2):
                ins = dve.tensor_copy(kb[i * HD:(i + 1) * HD, :, i, :],
                                      turn[n.slot(2)][i * HD:(i + 1) * HD, 0:ROWS_C].rearrange("p (g n) -> p g n", g=KV))
            ins.then_inc(turn_free[n.slot(2)], 1)
            wait(dve, out_done, OUTS.at("vb", 1))
            dve.tensor_tensor(vb[:, :, :], outp[0:HEADS * NCMP, 0:HD].unsqueeze(1).to_broadcast([HEADS * NCMP, HEADS, HD]),
                              ct[0:HEADS * NCMP, C_SELM:C_SELM + HEADS].unsqueeze(2).to_broadcast([HEADS * NCMP, HEADS, HD]),
                              ALU.mult).then_inc(out_free, 1)
            wait(dve, score_done, SCORES.at("cmp", 1))
            mask = ct[:, C_CMASK:C_CMASK + TT * NCMP].rearrange("p (t n) -> p t n", t=TT)
            for t in range(TT):
                ins = dve.tensor_tensor(pc[:, t, :, :], score[:, t * HEADS * NCMP:(t + 1) * HEADS * NCMP].rearrange("p (h n) -> p h n", n=NCMP),
                                        mask[:, t, :].unsqueeze(1).to_broadcast([P, HEADS, NCMP]), ALU.add)
            ins.then_inc(score_free, 1)
            wait(dve, score_free, SCORES.at("cmp", 1))
            pcf = pc[:, :, :, :].rearrange("p t h n -> p (t h) n")
            pmx, pco = (pcs[:, i, :, :].rearrange("p t h -> p (t h)") for i in range(2))
            link(dve.tensor_reduce(pmx, pcf, AX_X, ALU.max))
            dve.tensor_tensor(pcf, pcf, pmx.unsqueeze(2).to_broadcast([P, TT * HEADS, NCMP]), ALU.subtract).then_inc(s_pcm, 1)
            dve.wait_ge(s_pce, 1)
            link(dve.tensor_reduce(pmx, pcf, AX_X, ALU.add))
            link(dve.reciprocal(pco, pmx))
            for t in range(TT):
                ins = dve.scalar_tensor_tensor(pcs[:, 1, t, :], pcs[:, 1, t, :], ct[:, C_ROWOK + t:C_ROWOK + t + 1],
                                               gsig[:, t, 0, :], ALU.mult, ALU.mult)
            link(ins)
            for t in range(TT):
                n = OUTS.at("cmp", t)
                wait(dve, out_done, n + 1)
                dve.tensor_tensor(mixo[:, t, :].rearrange("p (h d) -> p h d", d=HD),
                                  outp[:, :].rearrange("p (h d) -> p h d", d=HD),
                                  pcs[:, 1, t, :].unsqueeze(2).to_broadcast([P, HEADS, HD]), ALU.mult).then_inc(out_free, 1)
            for k in range(4):
                n = TURNS.at("yr", k)
                wait(dve, turn_done, n + 1)
                xk = xc[:, 2 * k:2 * k + 2, :]
                dve.tensor_tensor(xk, turn[n.slot(2)][:, :].rearrange("p (k s) -> p k s", k=2), xk,
                                  ALU.mult).then_inc(turn_free[n.slot(2)], 1)
                turn_read(dve, "yr", k)
                dve.sem_inc(s_olru, 1)
                dve.wait_ge(s_lruhi, k + 1)
                dve.tensor_tensor(lru_lo[:, 2 * k:2 * k + 2, :], xk, lru_hi[:, 2 * k:2 * k + 2, :].bitcast(F32),
                                  ALU.subtract).then_inc(s_lrulo, 1)
            split("gm1")
            split("gm2")
            attention("slc", C_M1, 1, False)
            split("gm3")
            attention("win", C_M1, 2, False)
            dve.sem_inc(s_mixo, 1)
            split("nsa0")
            split("lru0", units=range(2))
            for k in range(2):
                turned_lo(nsa_hi, nsa_lo, "nsa", k)
            split("lru0", units=range(2, 4))
            for c in range(2):
                if c == 0:
                    split("nsa1")
                for i, name in enumerate(["nsa", "lru"]):
                    if i == 1:
                        split(["lru1", "o0"][c])
                    b = chunk_done(f"{name}{c}")
                    evacuated(dve, f"gm{2 * i + c}")
                    gc = gate[:, :, (2 * i + c) * COLS:(2 * i + c + 1) * COLS]
                    mc = merged[:, :, c * COLS:(c + 1) * COLS]
                    dve.tensor_tensor(mc if i == 0 else gc, acc[b][:, :, :], gc, ALU.mult).then_inc(acc_free[b], 1)
                    evacuated(dve, f"{name}{c}")
                    if i == 1:
                        dve.tensor_tensor(mc, mc, gc, ALU.add).then_inc(s_merged, 1)
            for k in range(4):
                turned_lo(x_hi, x_lo, "merged", k)
            split("o1")
            add_residual("o0", 0, 1.0)
            split("f0")
            add_residual("o1", 1, 1.0)
            normalise("norm2")
            for k in range(4):
                turned_lo(x_hi, x_lo, "norm2", k, vec1[:, V1["norm2"]:V1["norm2"] + KD])

            def square_chunk(i, step=None):
                wait(dve, s_rl, HIDDEN.at("ff", i + 1, None, step, 2))
                n = CHUNKS.at("f0", i, None, step, 2)
                b = n.slot(2)
                dve.tensor_tensor(hid1[:, i % 2, :, :], acc[b][:, :, :], relu[:, i % 2, :, :],
                                  ALU.mult).then_inc(acc_free[b], 1)

            def ff_lo(i, step=None):
                for m in range(2):
                    k = 2 * i + m
                    turned_lo(f_hi, f_lo, "ff", k, None, None, step, 4, 2 * k if step is None else step * 8 + 2 * k)

            split("f1")
            square_chunk(0)
            with dve.Fori(0, NF // 2 - 1) as j:
                for i in (1, 2):
                    split("f0", None, j, 2 * U, (i + 1) * U)
                    square_chunk(i, j)
                    ff_lo(i - 1, j)
            split("d0", units=range(U))
            square_chunk(NF - 1)
            ff_lo(NF - 2)
            ff_lo(NF - 1)
            split("d0", units=range(U, N_UNITS["d0"]))
            TURN = [float(np.float32(6.28125)), float(np.float32(2 * np.pi - 6.28125)),
                    float(2 * np.pi - 6.28125 - np.float32(2 * np.pi - 6.28125))]
            a0, a1, a2 = (ang[:, i, :, :] for i in range(3))
            link(dve.tensor_copy(pos_f[:, :], pos_i[:, :]))
            link(dve.tensor_tensor(a0, pos_f[:, :].unsqueeze(2).to_broadcast([P, TT, HALF]),
                                   ct[:, C_INV:C_INV + HALF].unsqueeze(1).to_broadcast([P, TT, HALF]), ALU.mult))
            link(dve.tensor_scalar(a1, a0, 0.5 / np.pi, None, ALU.mult))
            link(dve.tensor_scalar(a1, a1, 1.5 * 2 ** 23, None, ALU.add))
            link(dve.tensor_scalar(a1, a1, 1.5 * 2 ** 23, None, ALU.subtract))
            for part in TURN:
                link(dve.scalar_tensor_tensor(a0, a1, -part, a0, ALU.mult, ALU.add))
            link(dve.tensor_scalar(a0, a0, float(np.float32(3.1415925)), -float(np.float32(3.1415925)), ALU.min, ALU.max))
            link(dve.scalar_tensor_tensor(a2, a0, -1.0, a0, ALU.mult, ALU.max))
            dve.tensor_scalar(a1, a2, -1.0, float(np.float32(np.pi / 2)), ALU.mult, ALU.add).then_inc(s_ang, 1)
            split("d1", units=range(U))
            add_residual("d0", 0, 1.0)
            split("d1", units=range(U, N_UNITS["d1"]))

            def swiglu(f, gain, layer):
                split(f"L{f}_up0", layer)
                if f == "a":
                    add_last(layer)
                else:
                    add_residual("Lout1", 1, 1.0, layer)
                normalise(f"L{f}_norm", layer)
                for k in range(4):
                    turned_lo(x_hi, x_lo, f"L{f}_norm", k, vcur[:, V2[gain]:V2[gain] + KD], layer)

                def hid_chunk(i, step=None):
                    wait(dve, s_rl, HIDDEN.at(f"L{f}_hid", i + 1, layer, step, 2))
                    b = CHUNKS.at(f"L{f}_up0", i, layer, step, 2).slot(2)
                    dve.tensor_tensor(hid2[:, i % 2, :, :], acc[b][:, :, HALFW:COLS], silu[:, i % 2, :, :],
                                      ALU.mult).then_inc(acc_free[b], 1)

                def hid_lo(i, step=None):
                    turned_lo(g_hi, g_lo, f"L{f}_hid", i, None, layer, step, 2, 2 * i if step is None else step * 4 + 2 * i)

                split(f"L{f}_up1", layer)
                hid_chunk(0)
                with dve.Fori(0, (UPS - 1) // 2 - 1) as j:
                    for i in (1, 2):
                        split(f"L{f}_up0", layer, j, 2 * U, (i + 1) * U)
                        hid_chunk(i, j)
                        hid_lo(i - 1, j)
                split(f"L{f}_up{UPS - 1}", layer)
                hid_chunk(UPS - 2)
                hid_lo(UPS - 3)
                split(f"L{f}_dn0", layer, units=range(U))
                hid_chunk(UPS - 1)
                hid_lo(UPS - 2)
                hid_lo(UPS - 1)
                split(f"L{f}_dn0", layer, units=range(U, N_UNITS[f"L{f}_dn0"]))
                split(f"L{f}_dn1", layer, units=range(U))
                add_residual(f"L{f}_dn0", 0, 0.5, layer)
                split(f"L{f}_dn1", layer, units=range(U, N_UNITS[f"L{f}_dn1"]))

            def add_last(layer):
                dve.tensor_copy(vcur[:, :], vec2[:, bass.ds(layer, 1), :].rearrange("p o v -> p (o v)"))
                dve.tensor_copy(scur[:, :], sinks[:, bass.ds(layer, 1), :].rearrange("p o v -> p (o v)"))
                dve.tensor_copy(tcur[:, :], taps2[:, bass.ds(layer, 1), :].rearrange("p o v -> p (o v)")).then_inc(s_cur, 1)
                dve.wait_ge(s_cur, layer + 1)

            add_residual("d1", 1, 1.0)
            with dve.Fori(0, layers) as layer:
                chain.enter(layer)
                swiglu("a", "ffn1", layer)
                split("Lca", layer)
                add_residual("La_dn1", 1, 0.5, layer)
                normalise("Lmix", layer)
                for k in range(4):
                    turned_lo(x_hi, x_lo, "Lmix", k, vcur[:, V2["mix"]:V2["mix"] + KD], layer)
                split("Lcg", layer)
                split("Lq", layer)
                b = chunk_done("Lca", layer)
                evacuated(dve, "Lcg", layer)
                dve.tensor_tensor(u[:, :, :], acc[b][:, :, :], sig[:, :, :], ALU.mult).then_inc(acc_free[b], 1)
                split("Lkv", layer)
                split("Lout0", layer)
                evacuated(dve, "Lq", layer)
                evacuated(dve, "Lkv", layer)
                dve.wait_ge(s_rope2, 1)
                rotate_heads(HEADS + KV, rope2).then_inc(s_qk, 1)
                wait(dve, s_qk, Count(2, [(layer, 1)]))
                for i in range(2):
                    ins = dve.tensor_copy(kd[:, :, 0:KV, i, :], qk[:, :, HEADS:HEADS + KV, :])
                ins.then_inc(s_kd, 1)
                turns_read(dve, "Lu", 2, layer)

                def taps(lo, hi):
                    for j in range(lo, hi):
                        for n in range(KC - 1):
                            w = tcur[:, j * KC + n:j * KC + n + 1]
                            if j == 0:
                                ins = dve.tensor_scalar(y[:, n, :], u_t[:, n, 0:S], w,
                                                        vcur[:, V2["conv_b"] + n:V2["conv_b"] + n + 1], ALU.mult, ALU.add)
                            else:
                                ins = dve.scalar_tensor_tensor(y[:, n, :], u_t[:, n, j:j + S], w, y[:, n, :],
                                                               ALU.mult, ALU.add)
                        if j < TAPS2 - 1:
                            link(ins)
                    return ins

                attention("Latt", C_M2, None, True, layer, lambda j: taps(4 * j, 4 * j + 4) if j < 7 else None)
                dve.sem_inc(s_mixo, 1)
                taps(28, TAPS2).then_inc(s_y, 1)
                wait(dve, s_rms, NORMS.at("Lmixed", 1, layer))
                link(dve.reciprocal(stat[:, TT:2 * TT], stat[:, TT:2 * TT]))
                for t in range(TT):
                    ins = dve.tensor_scalar(xs[:, t, 0:CONV], mixo[:, t, :], stat[:, TT + t:TT + t + 1], None, ALU.mult)
                ins.then_inc(s_xs, 1)
                for k in range(2):
                    turned_lo(x_hi, x_lo, "Lmixed", k, vcur[:, V2["attn"]:V2["attn"] + 4], layer)
                rs = sig[:, 0, 0:S]
                over = [P, KC, S]
                wait(dve, score_done, SCORES.at("Lsum", 1, layer))
                dve.scalar_tensor_tensor(y[:, :, :], score[:, 0:S].unsqueeze(1).to_broadcast(over), -1.0, y[:, :, :],
                                         ALU.mult, ALU.add).then_inc(score_free, 1)
                wait(dve, score_free, SCORES.at("Lsum", 1, layer))
                for i in range(2):
                    wait(dve, score_free, SCORES.at("Lsum", 2 + i, layer))
                    if i:
                        wait(dve, s_silu, Count(1, [(layer, 1)]))
                    link(dve.reciprocal(rs, rs))
                    dve.tensor_tensor(y[:, :, :], y[:, :, :], rs.unsqueeze(1).to_broadcast(over), ALU.mult).then_inc(s_yn, 1)
                dve.wait_ge(s_convhi, layer + 1)
                for n in range(KC):
                    ins = dve.scalar_tensor_tensor(x_lo[:, 4 + n, :], y[:, n, :], vcur[:, V2["conv"] + n:V2["conv"] + n + 1],
                                                   x_hi[:, 4 + n, :].bitcast(F32), ALU.mult, ALU.subtract)
                ins.then_inc(s_convlo, 1)
                split("Lout1", layer)
                add_residual("Lout0", 0, 1.0, layer)
                swiglu("b", "ffn2", layer)
                split("Lple0", layer)
                turned_lo(pl_hi, pl_lo, "Lp", 0, None, layer)
                split("Lple1", layer)
                split("Lgate0", layer, units=range(2))
                add_residual("Lb_dn1", 1, 0.5, layer)
                wait(dve, s_ple, Count(4, [(layer, 4)]))
                rooted(dve.tensor_tensor(stat[:, 8:10], stat[:, 4:8:2], stat[:, 5:8:2], ALU.add), "Lple", layer)
                link(dve.reciprocal(stat[:, 8:10], stat[:, 8:10]))
                for c in range(2):
                    b = chunk_done(f"Lple{c}", layer)
                    for t in range(TT):
                        ins = dve.scalar_tensor_tensor(
                            e_ple[:, t, c * COLS:(c + 1) * COLS], acc[b][:, t, :], stat[:, 8 + t:9 + t],
                            gn[:, bass.ds(layer, 1), c * COLS:(c + 1) * COLS].rearrange("p o n -> p (o n)"),
                            ALU.mult, ALU.mult)
                    ins.then_inc(acc_free[b], 1)
                for k in range(4):
                    turned_lo(x_hi, x_lo, "Lraw", k, None, layer)
                split("Lgate0", layer, units=range(2, 4))
                split("Lgate1", layer)
                for c in range(2):
                    evacuated(dve, f"Lgate{c}", layer)
                    evacuated(dve, f"Lple{c}", layer)
                    link(dve.tensor_tensor(sig[:, :, :], sig[:, :, :], e_ple[:, :, c * COLS:(c + 1) * COLS], ALU.mult))
                    hc = h[:, :, c * COLS:(c + 1) * COLS]
                    dve.tensor_tensor(hc, hc, sig[:, :, :], ALU.add).then_inc(s_h, 1)
                    wait(dve, s_h, RESIDUAL.at("Lgate", c + 1, layer))
                chain.leave(layers)
            dve.wait_ge(s_rms, 2 + NORMS.per_layer * layers + 1)
            link(dve.reciprocal(stat[:, 0:TT], stat[:, 0:TT]))
            for t in range(TT):
                dve.scalar_tensor_tensor(xs[:, t, :], h[:, t, :], stat[:, t:t + 1], gn[:, LAYERS, :],
                                         ALU.mult, ALU.mult).then_inc(s_result, 1)

        @block.tensor
        def _(pe):
            def chunk(name, hi, lo, layer=None, step=None, k=0, ready=lambda kt: None, bank=None):
                c = CHUNKS.at(name, k, layer, step, 2) if bank is None else None
                w, tiles = width(name), tiles_of(name)
                if bank is None and c.const >= 2:
                    wait(pe, acc_free[c.slot(2)], c.lap(2))
                last = N_UNITS[name] * tiles - 1
                for i in range(N_UNITS[name]):
                    n = UNITS.at(name, i + k * N_UNITS[name], layer, step, 2 * N_UNITS[name])
                    wait(pe, lo_done, n + 1)
                    for q in range(tiles):
                        kt = i * tiles + q
                        ready(kt)
                        wh, wl = w_hi[:, n.slot(SPLIT), q, 0:w], w_lo[:, n.slot(SPLIT), q, 0:w]
                        for t in range(TT if bank is None else 1):
                            if bank is None:
                                dst = acc[c.slot(2)][:, t, 0:w]
                                xh, xl = hi[:, kt, t * P:(t + 1) * P], lo[:, kt, t * P:(t + 1) * P]
                            else:
                                dst, xh, xl = bank, hi[:, kt, :], lo[:, kt, :]
                            pe.matmul(dst, xh, wh, start=kt == 0, stop=False)
                            pe.matmul(dst, xh, wl, start=False, stop=False)
                            mm = pe.matmul(dst, xl, wh, start=False, stop=kt == last)
                    mm.then_inc(unit_used, 1)

            def turned(name, k, pieces, layer=None, step=None, per_step=0):
                n = TURNS.at(name, k, layer, step, per_step)
                if n.const >= 2:
                    wait(pe, turn_free[n.slot(2)], n.lap(2))
                at = 0
                for src in pieces:
                    rows_in, cols_in = src.shape
                    mm = pe.transpose(turn[n.slot(2)][0:cols_in, at:at + rows_in], src, ident[0:rows_in, 0:rows_in])
                    at += rows_in
                mm.then_inc(turn_done, 1)

            def pieces(src, k):
                return [src[:, t, f * P:(f + 1) * P] for f in (2 * k, 2 * k + 1) for t in range(TT)]

            def turn_rows(name, src, count, layer=None):
                for k in range(count):
                    turned(name, k, pieces(src, k), layer)

            def free(plan, sem_free, name, k, layer=None):
                wait(pe, sem_free, plan.at(name, k, layer))

            def scores(name, j, kbase, layer=None):
                t, p = j // PAIRS, j % PAIRS
                w = P * (t + 1)
                free(SCORES, score_free, name, j, layer)
                half = slice(p % 2 * HD, (p % 2 + 1) * HD)
                for i in range(2):
                    mm = pe.matmul(score[:, i * w:(i + 1) * w], q_t[half, p // 2 * 2 + i, t * P:(t + 1) * P],
                                   k_t[half, kbase + p // 2, 0:w], start=True, stop=True)
                mm.then_inc(score_done, 1)

            def values(name, j, branch, layer=None):
                t, p, b = j // PAIRS, j % PAIRS, j % 2
                wait(pe, s_exp, HEAD_PAIRS.at(name, j + 1, layer))
                turned(name, j, [sm[:, b, i, s * P:(s + 1) * P] for i in range(2) for s in range(t + 1)], layer)
                free(OUTS, out_free, name, j, layer)
                turn_read(pe, name, j, layer)
                g = p // 2
                for i in range(2):
                    for s in range(t + 1):
                        mm = pe.matmul(outp[:, i * HD:(i + 1) * HD], p_t[:, i, s, :],
                                       vv[:, s, branch, g * HD:(g + 1) * HD], start=s == 0, stop=s == t)
                mm.then_inc(out_done, 1)

            def attention(name, kbase, branch, layer=None):
                scores(name, 0, kbase, layer)
                for j in range(2 * PAIRS):
                    if j + 1 < 2 * PAIRS:
                        scores(name, j + 1, kbase, layer)
                    values(name, j, branch, layer)

            pe.wait_ge(s_table, 16)
            pe.wait_ge(s_const, 16 * 9)
            pe.transpose(score[:, 0:NV1], raw1[:, :], ident[0:NV1, 0:NV1]).then_inc(score_done, 1)
            wait(pe, s_xs, NORMS.at("norm1", 1))
            turn_rows("norm1", xs, 4)
            pe.wait_ge(s_vecs2, 16 * (9 * LAYERS + 1 + TT))
            pe.transpose(outp[:, 0:LAYERS * NV2], raw2[:, :], ident[0:LAYERS * NV2, 0:LAYERS * NV2]).then_inc(out_done, 1)
            rows_t = TAPS2 * KC
            pe.wait_ge(score_free, 1)
            pe.transpose(score[:, 0:rows_t], rawt[:, 0, :], ident[0:rows_t, 0:rows_t]).then_inc(score_done, 1)
            pe.wait_ge(out_free, 1)
            pe.transpose(outp[:, 0:rows_t], rawt[:, 1, :], ident[0:rows_t, 0:rows_t]).then_inc(out_done, 1)
            turns_read(pe, "norm1", 4)
            for name in ["xr0", "xr1", "q"]:
                chunk(name, x_hi, x_lo)
            for c in range(2):
                evacuated(pe, f"xr{c}")
            turn_rows("xr", gy, 4)
            for name in ["ks", "kw", "yr0", "yr1"]:
                chunk(name, x_hi, x_lo)
            pe.wait_ge(s_xc, 1)
            pe.wait_ge(s_small, 16 * 17)
            for k in range(4):
                for i, (plan, done, sem_free, bank) in enumerate([(SCORES, score_done, score_free, score),
                                                                  (OUTS, out_done, out_free, outp)]):
                    free(plan, sem_free, "gates", k)
                    for m in range(2):
                        f = 2 * k + m
                        mm = pe.matmul(bank[:, m * S:(m + 1) * S], w_gates[:, i, f, :], xc[:, f, :], start=True, stop=True)
                    mm.then_inc(done, 1)
            pe.wait_ge(s_qk, 1)
            turn_rows("q", qk[:, :, 0:HEADS, :].rearrange("p t n d -> p t (n d)"), 2)
            pe.wait_ge(s_kd, 1)
            turn_rows("k", kd[:, :, :, :, :].rearrange("p t b i d -> p t (b i d)"), 2)
            evacuated(pe, "ks")
            turn_rows("z", cd[:, :, :, :, :].rearrange("p t b i d -> p t (b i d)"), 2)
            free(SCORES, score_free, "hid", 0)
            for i, name in enumerate(phi1):
                pe.wait_ge(s_zjlo, i + 1)
                chunk(name, zj_hi[:, i, :, :], zj_lo[:, i, :, :], bank=score[0:ROWS_C, i * PHI:(i + 1) * PHI])
            wait(pe, score_free, SCORES.at("hid", 1))
            pe.sem_inc(score_done, 1)
            turned("hid", 0, [ghid[:, i * P:(i + 1) * P] for i in range(4)])
            turn_read(pe, "hid", 0)
            free(OUTS, out_free, "kvc", 0)
            for i in range(2):
                for m in range(2):
                    mm = pe.matmul(outp[0:ROWS_C, i * HD:(i + 1) * HD], ghid_t[:, 2 * i + m, :], w_phi2[:, i, m, :],
                                   start=m == 0, stop=m == 1)
            mm.then_inc(out_done, 1)
            pe.wait_ge(s_kcd, 1)
            turned("kc", 0, [kcd[:, :, :].rearrange("p i d -> p (i d)")])
            free(OUTS, out_free, "vb", 0)
            pe.matmul(outp[0:HEADS * NCMP, 0:HD], ct[0:ROWS_C, C_SEL:C_SEL + HEADS * NCMP], kvc[:, 1, :],
                      start=True, stop=True).then_inc(out_done, 1)
            turn_read(pe, "kc", 0)
            turns_read(pe, "q", 2)
            for t in range(TT):
                for p in range(PAIRS):
                    at = t * HEADS * NCMP + p * 2 * NCMP
                    mm = pe.matmul(score[:, at:at + 2 * NCMP], q_t[:, p, t * P:(t + 1) * P],
                                   kb[:, p // KV, :, :].rearrange("p i n -> p (i n)"), start=True, stop=True)
            mm.then_inc(score_done, 1)
            pe.wait_ge(s_pce, 1)
            turned("pc", 0, [pc[:, t, :, :].rearrange("p h n -> p (h n)") for t in range(TT)])
            turn_read(pe, "pc", 0)
            for t in range(TT):
                free(OUTS, out_free, "cmp", t)
                pe.matmul(outp[:, :], pc_t[:, t * P:(t + 1) * P], vb[:, :, :].rearrange("p h d -> p (h d)"),
                          start=True, stop=True).then_inc(out_done, 1)
            for c in range(2):
                evacuated(pe, f"yr{c}")
            turn_rows("yr", gy, 4)
            turns_read(pe, "k", 2)
            chunk("gm0", x_hi, x_lo)
            chunk("gm1", x_hi, x_lo)
            attention("slc", 0, 0)
            chunk("gm2", x_hi, x_lo)
            chunk("gm3", x_hi, x_lo)
            attention("win", KV, 1)
            pe.wait_ge(s_mixo, 1)
            turn_rows("nsa", mixo, 2)
            turns_read(pe, "nsa", 2)
            pe.wait_ge(s_lrulo, 4)
            for c in range(2):
                chunk(f"nsa{c}", nsa_hi, nsa_lo)
                chunk(f"lru{c}", lru_hi, lru_lo)
            pe.wait_ge(s_merged, 2)
            turn_rows("merged", merged, 4)
            turns_read(pe, "merged", 4)
            for c in range(2):
                chunk(f"o{c}", x_hi, x_lo)
            wait(pe, s_xs, NORMS.at("norm2", 1))
            turn_rows("norm2", xs, 4)
            turns_read(pe, "norm2", 4)

            def ff_turns(i, step=None):
                n = CHUNKS.at("f0", i, None, step, 2)
                wait(pe, acc_free[n.slot(2)], n.lap(2) + 1)
                for m in range(2):
                    turned("ff", 2 * i + m, pieces(hid1[:, i % 2, :, :], m), None, step, 4)

            chunk("f0", x_hi, x_lo)
            with pe.Fori(0, NF // 2 - 1) as j:
                for i in (1, 2):
                    chunk("f0", x_hi, x_lo, None, j, i)
                    ff_turns(i - 1, j)
            chunk(f"f{NF - 1}", x_hi, x_lo)
            ff_turns(NF - 2)
            ff_turns(NF - 1)
            turns_read(pe, "ff", 2 * NF)
            for c in range(2):
                chunk(f"d{c}", f_hi, f_lo)

            def normed(name, count, src, layer):
                if name in NORMS.start:
                    wait(pe, s_xs, NORMS.at(name, 1, layer))
                turn_rows(name, src, count, layer)
                turns_read(pe, name, count, layer)

            def swiglu(f, layer):
                normed(f"L{f}_norm", 4, xs, layer)

                def hid_turns(i, step=None):
                    n = CHUNKS.at(f"L{f}_up0", i, layer, step, 2)
                    wait(pe, acc_free[n.slot(2)], n.lap(2) + 1)
                    turned(f"L{f}_hid", i, pieces(hid2[:, i % 2, :, :], 0), layer, step, 2)

                chunk(f"L{f}_up0", x_hi, x_lo, layer)
                with pe.Fori(0, (UPS - 1) // 2 - 1) as j:
                    for i in (1, 2):
                        chunk(f"L{f}_up0", x_hi, x_lo, layer, j, i)
                        hid_turns(i - 1, j)
                chunk(f"L{f}_up{UPS - 2}", x_hi, x_lo, layer)
                hid_turns(UPS - 3)
                chunk(f"L{f}_up{UPS - 1}", x_hi, x_lo, layer)
                hid_turns(UPS - 2)
                hid_turns(UPS - 1)
                turns_read(pe, f"L{f}_hid", UPS, layer)
                for c in range(2):
                    chunk(f"L{f}_dn{c}", g_hi, g_lo, layer)

            with pe.Fori(0, layers) as layer:
                swiglu("a", layer)
                normed("Lmix", 4, xs, layer)
                chunk("Lca", x_hi, x_lo, layer)
                chunk("Lcg", x_hi, x_lo, layer)
                chunk("Lq", x_hi, x_lo, layer)
                evacuated(pe, "Lca", layer)
                turn_rows("Lu", u, 2, layer)
                chunk("Lkv", x_hi, x_lo, layer)
                wait(pe, s_qk, Count(2, [(layer, 1)]))
                turn_rows("Lq", qk[:, :, 0:HEADS, :].rearrange("p t n d -> p t (n d)"), 2, layer)
                wait(pe, s_kd, Count(2, [(layer, 1)]))
                turned("Lk", 0, pieces(kd[:, :, 0:KV, :, :].rearrange("p t b i d -> p t (b i d)"), 0), layer)
                turns_read(pe, "Lq", 2, layer)
                turn_read(pe, "Lk", 0, layer)
                attention("Latt", 0, 0, layer)
                normed("Lmixed", 2, xs, layer)
                pe.wait_ge(s_zero, 3)
                wait(pe, s_y, Count(1, [(layer, 1)]))
                wait(pe, s_ypool, Count(1, [(layer, 1)]))
                for i in range(3):
                    free(SCORES, score_free, "Lsum", i, layer)
                    if i:
                        wait(pe, s_ysq, Count(i, [(layer, 2)]))
                    for n in range(KC):
                        mm = pe.matmul(score[:, 0:S], mean[:, :], (ysq if i else y)[:, n, :], start=n == 0, stop=n == KC - 1)
                    mm.then_inc(score_done, 1)
                wait(pe, s_convlo, Count(1, [(layer, 1)]))
                for c in range(2):
                    chunk(f"Lout{c}", x_hi, x_lo, layer)
                swiglu("b", layer)
                wait(pe, s_pcur, Count(1, [(layer, 1)]))
                turned("Lp", 0, pieces(pcur, 0), layer)
                turn_read(pe, "Lp", 0, layer)
                for c in range(2):
                    chunk(f"Lple{c}", pl_hi, pl_lo, layer)
                wait(pe, s_h, RESIDUAL.at("Lb_dn", 2, layer))
                normed("Lraw", 4, h, layer)
                for c in range(2):
                    chunk(f"Lgate{c}", x_hi, x_lo, layer)


def kernel(**inputs):
    from concourse import bacc
    from concourse.bass_utils import run_bass_kernel_spmd

    nc = bacc.Bacc("TRN2", target_bir_lowering=False, num_devices=1)
    arrays, aps = {}, {}
    for name, value in inputs.items():
        if name.endswith("w_gate_up_2"):
            value = np.asarray(value).reshape(LAYERS, D, 2, UPS, HALFW).transpose(0, 1, 3, 2, 4).reshape(value.shape)
        arrays[f"in_{name}"] = np.ascontiguousarray(value)
    arrays["in_tables"] = constants()
    for name, value in arrays.items():
        aps[name[3:]] = nc.dram_tensor(name, value.shape, mybir.dt.from_np(value.dtype), kind="ExternalInput").ap()
    out = nc.dram_tensor("out", (1, S, D), F32, kind="ExternalOutput").ap()
    build(nc, aps, aps.pop("tables"), out)
    return run_bass_kernel_spmd(nc, [arrays], core_ids=[0]).results[0]["out"]
```

```python
from contextlib import ExitStack

import numpy as np

import concourse.bass as bass
from concourse import mybir

F32 = mybir.dt.float32
F32R = mybir.dt.float32r
I32 = mybir.dt.int32
ALU = mybir.AluOpType
ACT = mybir.ActivationFunctionType
AX_X = mybir.AxisListType.X

P = 128
S = 256
TT = S // P
D = 1024
KD = D // P
COLS = 512
UNIT_K = 2
EPS = 1e-6
NEG = -1e30
HEADS, HD, KV = 8, 64, 2
PAIRS = HEADS // 2
ROT = HD // 4
HALF = ROT // 2
THETA = 500000.0
CMP_BLOCK, CMP_STRIDE = 32, 16
NCMP = (S - CMP_BLOCK) // CMP_STRIDE + 1
ROWS_C = KV * NCMP
KPHI = CMP_BLOCK * HD // P
PHI = 256
TAPS1 = 4
FF1 = 4096
KF1 = FF1 // P
OFF_KV, OFF_KW, OFF_XR, OFF_YR, OFF_GM = 512, 1024, 1304, 2328, 3352
W_KW = OFF_XR - OFF_KW
LAYERS = 2
FF2 = 2816
KF2 = FF2 // P
TAPS2 = 31
CONV = 512
KC = CONV // P
WINDOW = 128
PLE = 256
KPLE = PLE // P
HALFW = COLS // 2
UPS = FF2 // HALFW

STAGE, SPLIT = 8, 4

V1 = dict(norm1=0, norm2=8, conv_w=16, conv_b=48, ba=56, bx=64, lam=72, pos_k=80, pos_v=96)
NV1 = 112
V2 = dict(ffn1=0, mix=8, ffn2=16, attn=24, conv=28, conv_b=32, ln_g=36, ln_b=40)
NV2 = 44

STATS = dict(rstd=0, attn=TT, ple=2 * TT, e=4 * TT, half=5 * TT, q=7 * TT)
C_STATS = 8 * TT

C_ID, C_M1, C_M2, C_ROPE, C_ROPEC, C_CMASK, C_ROWOK, C_INV, C_SEL, C_SELM, C_EPS, C_END = np.cumsum(
    [0, P, S, S, TT * 2 * ROT, 2 * ROT, TT * NCMP, TT, HALF, HEADS * NCMP, HEADS, 1]).tolist()


class Count:

    def __init__(self, const, terms=()):
        self.const, self.terms = const, [t for t in terms if t[0] is not None and t[1]]

    def __add__(self, n):
        return Count(self.const + n, self.terms)

    def slot(self, n):
        assert all(c % n == 0 for _, c in self.terms)
        return self.const % n

    def lap(self, n):
        assert all(c % n == 0 for _, c in self.terms)
        return Count(self.const // n, [(r, c // n) for r, c in self.terms])

    def value(self, times=1):
        v = self.const * times
        for r, c in self.terms:
            v = r * (c * times) + v
        return v


def wait(eng, sem, count, times=1):
    v = count.value(times)
    if not isinstance(v, int) or v > 0:
        eng.wait_ge(sem, v)


class Plan:

    def __init__(self, before, layer):
        self.start, n = {}, 0
        for name, k in before:
            self.start[name] = (n, False)
            n += k
        self.per_layer = 0
        for name, k in layer:
            self.start[name] = (n + self.per_layer, True)
            self.per_layer += k

    def at(self, name, k=0, layer=None, step=None, per_step=0):
        n, looped = self.start[name]
        assert looped == (layer is not None), name
        return Count(n + k, [(layer, self.per_layer), (step, per_step)])


def units_of(k_tiles, per=UNIT_K):
    return k_tiles // per


U = units_of(KD)
NF = FF1 // COLS
_U1 = ([(n, U) for n in ("ks", "q", "kw", "xr0")] + [("phi_k", units_of(KPHI)), ("xr1", U), ("phi_v", units_of(KPHI))]
       + [(n, U) for n in ("yr0", "yr1", "gm0", "gm1", "gm2", "gm3")]
       + [("nsa0", units_of(4)), ("lru0", U), ("nsa1", units_of(4)), ("lru1", U), ("o0", U), ("o1", U)]
       + [(f"f{i}", U) for i in range(NF)] + [("d0", units_of(KF1)), ("d1", units_of(KF1))])
_U2 = ([(f"a_up{i}", U) for i in range(UPS)] + [("a_dn0", units_of(KF2)), ("a_dn1", units_of(KF2))]
       + [(n, U) for n in ("ca", "cg", "q", "kv", "out0", "out1")]
       + [(f"b_up{i}", U) for i in range(UPS)] + [("b_dn0", units_of(KF2)), ("b_dn1", units_of(KF2))]
       + [("ple0", units_of(KPLE, 1)), ("ple1", units_of(KPLE, 1)), ("gate0", U), ("gate1", U)])
_U2 = [("L" + n, k) for n, k in _U2]
N_UNITS = dict(_U1 + _U2)
UNITS = Plan(_U1, _U2)
CHUNKS = Plan([(n, 1) for n, _ in _U1 if not n.startswith("phi")], [(n, 1) for n, _ in _U2])
TURNS = Plan([("norm1", 4), ("z", 2), ("q", 2), ("k", 2), ("hid", 1), ("xr", 4), ("kc", 1), ("pc", 1),
              ("slc", 8), ("yr", 4), ("win", 8), ("nsa", 2), ("merged", 4), ("norm2", 4), ("ff", 2 * NF)],
             [("La_norm", 4), ("La_hid", UPS), ("Lmix", 4), ("Lu", 2), ("Lq", 2), ("Lk", 1), ("Latt", 8),
              ("Lmixed", 2), ("Lb_norm", 4), ("Lb_hid", UPS), ("Lp", 1), ("Lraw", 4)])
HI_TURNS = Plan([("norm1", 4), ("nsa", 2), ("merged", 4), ("norm2", 4), ("ff", 2 * NF)],
                [("La_norm", 4), ("La_hid", UPS), ("Lmix", 4), ("Lmixed", 2), ("Lb_norm", 4), ("Lb_hid", UPS),
                 ("Lp", 1), ("Lraw", 4)])
RSTD = Plan([("norm1", 1), ("norm2", 1)], [("La_norm", 1), ("Lmix", 1), ("Lb_norm", 1)])
ROOTS = Plan([("norm1", 1), ("qk", 1), ("kc", 1), ("lru", 1), ("norm2", 1)],
             [("La_norm", 1), ("Lmix", 1), ("Lb_norm", 1), ("Lple", 1)])
HIDDEN = Plan([("ff", NF)], [("La_hid", UPS), ("Lb_hid", UPS)])
RESIDUAL = Plan([("o", 2), ("d", 2)], [("La_dn", 2), ("Lout", 2), ("Lb_dn", 2), ("Lgate", 2)])
SCORES = Plan([("vec", 2), ("hid", 1), ("cmp", 1), ("gates", 4), ("slc", 8), ("win", 8)],
              [("Latt", 8), ("Lsum", 3)])
OUTS = Plan([("vec", 2), ("kvc", 1), ("vb", 1), ("cmp", TT), ("gates", 4), ("slc", 8), ("win", 8)],
            [("Latt", 8)])
HEAD_PAIRS = Plan([("slc", 8), ("win", 8)], [("Latt", 8)])

JOBS = [(name, j) for name in ("slc", "win") for j in range(2 * PAIRS)]
BESIDE = ([(f"gm{c}", i) for c in range(4) for i in range(U)] + [("nsa0", i) for i in range(units_of(4))]
          + [("lru0", i) for i in range(U - units_of(4))])

DVE_LINKS = 70
ACT_LINKS = 1
POOL_LINKS = 2 * TAPS2 - 1


class Chain:

    def __init__(self, eng, sem, per_layer):
        self.eng, self.sem, self.per_layer = eng, sem, per_layer
        self.n, self.layer, self.first = 0, None, 0

    def enter(self, layer):
        self.layer, self.first = layer, self.n

    def leave(self, layers):
        assert self.n - self.first == self.per_layer, (self.n - self.first, self.per_layer)
        self.n, self.layer = self.first + layers * self.per_layer, None

    def link(self, ins):
        self.n += 1
        ins.then_inc(self.sem, 1)
        wait(self.eng, self.sem, Count(self.n, [(self.layer, self.per_layer)]))


def heads_of(x, p):
    return x.rearrange("q (g a i d) -> q g i a d", g=KV, a=2, i=2)[:, p // 2, p % 2, :, :]


def constants():
    c = np.zeros((P, C_END), np.float32)
    i, j = np.arange(P)[:, None], np.arange(P)[None, :]
    c[:, C_ID:C_ID + P] = i == j
    causal = np.where(j <= i, 0.0, NEG)
    c[:, C_M1 + P:C_M1 + S] = causal
    c[:, C_M2:C_M2 + P] = np.where(i + P - j < WINDOW, 0.0, NEG)
    c[:, C_M2 + P:C_M2 + S] = causal
    inv = (THETA ** (-np.arange(HALF, dtype=np.float64) / HALF)).astype(np.float32)

    def rope(pos):
        ang = (pos.astype(np.float32)[:, None] * inv[None, :]).astype(np.float64)
        return np.concatenate([np.cos(ang), np.cos(ang), -np.sin(ang), np.sin(ang)], 1)

    ends = np.arange(NCMP) * CMP_STRIDE + CMP_BLOCK - 1
    for t in range(TT):
        tok = t * P + np.arange(P)
        c[:, C_ROPE + t * 2 * ROT:C_ROPE + (t + 1) * 2 * ROT] = rope(tok)
        c[:, C_CMASK + t * NCMP:C_CMASK + (t + 1) * NCMP] = np.where(ends[None, :] <= tok[:, None], 0.0, NEG)
        c[:, C_ROWOK + t] = tok >= CMP_BLOCK - 1
    c[:ROWS_C, C_ROPEC:C_ROPEC + 2 * ROT] = np.tile(rope(ends), (KV, 1))
    c[:, C_INV:C_INV + HALF] = inv
    for head in range(HEADS):
        for n in range(NCMP):
            c[(head // (HEADS // KV)) * NCMP + n, C_SEL + head * NCMP + n] = 1.0
            c[head * NCMP + n, C_SELM + head] = 1.0
    c[:, C_EPS] = EPS
    return c


def build(nc, a, consts, out, layers=LAYERS):
    ctx = ExitStack()
    with ctx:
        def sb(name, shape, dt=F32, stack=ctx):
            return stack.enter_context(nc.sbuf_tensor(name, shape, dt))

        def sem(name):
            return ctx.enter_context(nc.semaphore(name))

        def overlay(stack, *groups):
            made, free, least = [], nc.sbuf_bytes_remaining, nc.sbuf_bytes_remaining
            for group in groups:
                with ExitStack() as own:
                    made += [sb(*spec, stack=own) for spec in group]
                    least = min(least, nc.sbuf_bytes_remaining)
            sb(f"room_{groups[0][0][0]}", [P, -(-(free - least) // 4)], stack=stack)
            return made

        stage = sb("stage", [P, STAGE, UNIT_K, COLS])
        w_hi = sb("w_hi", [P, SPLIT, UNIT_K, COLS], F32R)
        w_lo = sb("w_lo", [P, SPLIT, UNIT_K, COLS], F32R)
        x_hi = sb("x_hi", [P, KD, S], F32R)
        x_lo = sb("x_lo", [P, KD, S], F32R)
        h = sb("h", [P, TT, D])
        xs = sb("xs", [P, TT, D])
        ct = sb("ct", [P, C_END])
        stat = sb("stat", [P, C_STATS])
        vec1 = sb("vec1", [P, NV1])
        vec2 = sb("vec2", [P, LAYERS, NV2])
        taps2 = sb("taps2", [P, LAYERS, TAPS2 * KC])
        sinks = sb("sinks", [P, LAYERS, HEADS])
        vcur = sb("vcur", [P, NV2])
        tcur = sb("tcur", [P, TAPS2 * KC])
        scur = sb("scur", [P, HEADS])
        pos_i = sb("pos_i", [P, TT], I32)
        pos_f = sb("pos_f", [P, TT])
        ang = sb("ang", [P, 3, TT, HALF])
        rope2 = sb("rope2", [P, TT, 2 * ROT])
        mx = sb("mx", [P, 2, 2])
        negm = sb("negm", [P, 2, 2])
        den = sb("den", [P, 2, 2])
        esink = sb("esink", [P, 2, 2])
        coef = sb("coef", [P, 2])
        ident, eps = ct[:, C_ID:C_ID + P], ct[:, C_EPS:C_EPS + 1]

        masks = sb("masks", [P, 2, S], F32R)
        ident_r = sb("ident_r", [P, P], F32R)
        x_rt, raw1, raw2, rawt, gate, x2_hi, x2_lo = overlay(
            ctx, [("x_rt", [P, KD, TAPS1 - 1 + S])],
            [("raw1", [NV1, P]), ("raw2", [LAYERS * NV2, P]), ("rawt", [TAPS2 * KC, LAYERS, P])],
            [("gate", [P, TT, 2 * D])], [("x2_hi", [P, KD, S], F32R), ("x2_lo", [P, KD, S], F32R)])

        attn, mixer, mlp, lay = ExitStack(), ExitStack(), ExitStack(), ExitStack()
        qk = sb("qk", [P, TT, 12, HD], stack=attn)
        vv = sb("vv", [P, TT, 2, P], stack=attn)
        kd = sb("kd", [P, TT, 4, 2, HD], stack=attn)
        q_t = sb("q_t", [P, PAIRS, S], stack=attn)
        k_t = sb("k_t", [P, 4, S], stack=attn)
        sm = sb("sm", [P, 2, 2, S], stack=attn)
        p_t = sb("p_t", [P, 2, TT, P], stack=attn)
        ropet = sb("ropet", [P, TT, 12, ROT], stack=attn)
        tmpo = sb("tmpo", [P, 2, HD], stack=attn)
        mixo, z = overlay(attn, [("mixo", [P, TT, 512])], [("z", [P, 4, S])])
        gy = sb("gy", [P, TT, D], stack=mixer)
        lru_r, lru_i, lru_hi, lru_lo, zj_hi, zj_lo = overlay(
            mixer, [("lru_r", [P, KD, S]), ("lru_i", [P, KD, S])],
            [("lru_hi", [P, KD, S], F32R), ("lru_lo", [P, KD, S], F32R)],
            [("zj_hi", [P, 2, KPHI, ROWS_C], F32R), ("zj_lo", [P, 2, KPHI, ROWS_C], F32R)])
        w_gates, nsa_hi, nsa_lo = overlay(
            mixer, [("w_gates", [P, 2, KD, P])], [("nsa_hi", [P, 4, S], F32R), ("nsa_lo", [P, 4, S], F32R)])
        cd, xc = overlay(mixer, [("cd", [P, TT, 4, 2, HD])], [("xc", [P, KD, S])])
        zj, pc, pc_t = overlay(mixer, [("zj", [P, KPHI, KV, NCMP])],
                               [("pc", [P, TT, HEADS, NCMP]), ("pc_t", [HEADS * NCMP, S])])
        gsig = sb("gsig", [P, TT, 3, HEADS], stack=mixer)
        softp = sb("softp", [P, 9, KD], stack=mixer)
        qk_ss = sb("qk_ss", [P, TT * 12], stack=mixer)
        w_phi2 = sb("w_phi2", [P, 2, 2, HD], stack=mixer)
        ghid = sb("ghid", [ROWS_C, 2 * PHI], stack=mixer)
        ghid_t = sb("ghid_t", [P, 4, ROWS_C], stack=mixer)
        kvc = sb("kvc", [ROWS_C, 2, HD], stack=mixer)
        kcs = sb("kcs", [ROWS_C, HD], stack=mixer)
        kcd = sb("kcd", [ROWS_C, 2, HD], stack=mixer)
        kcr = sb("kcr", [ROWS_C, ROT + 1], stack=mixer)
        knw = sb("knw", [P, HD], stack=mixer)
        qkw = sb("qkw", [P, 12, HD], stack=mixer)
        kb = sb("kb", [P, KV, 2, NCMP], stack=mixer)
        vb = sb("vb", [HEADS * NCMP, HEADS, HD], stack=mixer)
        pcs = sb("pcs", [P, 2, TT, HEADS], stack=mixer)
        mixer.close()
        u = sb("u", [P, TT, CONV], stack=attn)
        y = sb("y", [P, KC, S], stack=attn)
        ysq = sb("ysq", [P, KC, S], stack=attn)
        attn.close()
        f_hi = sb("f_hi", [P, KF1, S], F32R, stack=mlp)
        f_lo = sb("f_lo", [P, KF1, S], F32R, stack=mlp)
        hid1 = sb("hid1", [P, 2, TT, COLS], stack=mlp)
        relu = sb("relu", [P, 2, TT, COLS], stack=mlp)
        mlp.close()
        g_hi = sb("g_hi", [P, KF2, S], F32R, stack=lay)
        g_lo = sb("g_lo", [P, KF2, S], F32R, stack=lay)
        hid2 = sb("hid2", [P, 2, TT, HALFW], stack=lay)
        silu = sb("silu", [P, 2, TT, HALFW], stack=lay)
        sig = sb("sig", [P, TT, COLS], stack=lay)
        u_t = sb("u_t", [P, KC, TAPS2 - 1 + S], stack=lay)
        pcur = sb("pcur", [P, TT, PLE], stack=lay)
        pl_hi = sb("pl_hi", [P, KPLE, S], F32R, stack=lay)
        pl_lo = sb("pl_lo", [P, KPLE, S], F32R, stack=lay)
        e_ple = sb("e_ple", [P, TT, D], stack=lay)
        gn = sb("gn", [P, LAYERS + 1, D], stack=lay)
        mean = masks[:, 0, 0:P].bitcast(F32)
        lay.close()
        merged, sq, th = xs, xs[:, :, 0:12 * HD], x_rt[:, :, 0:S]
        den2 = xs[:, :, :].rearrange("p t (f s) -> p (t f) s", s=S)

        acc = [ctx.enter_context(nc.psum_tensor(f"acc{i}", [P, TT, COLS], F32)) for i in range(2)]
        turn = [ctx.enter_context(nc.psum_tensor(f"turn{i}", [P, 512], F32)) for i in range(2)]
        score = ctx.enter_context(nc.psum_tensor("score", [P, 512], F32))
        outp = ctx.enter_context(nc.psum_tensor("outp", [P, 512], F32))

        s_x = sem("s_x")
        s_table = sem("s_table")
        s_const = sem("s_const")
        s_vecs2 = sem("s_vecs2")
        s_small = sem("s_small")
        s_late = sem("s_late")
        s_zero = sem("s_zero")
        s_pcur = sem("s_pcur")
        landed = [sem(f"landed{i}") for i in range(STAGE)]
        hi_done = sem("hi_done")
        lo_done = sem("lo_done")
        unit_used = sem("unit_used")
        acc_free = [sem(f"acc_free{i}") for i in range(2)]
        turn_done = sem("turn_done")
        turn_hi = sem("turn_hi")
        turn_free = [sem(f"turn_free{i}") for i in range(2)]
        score_done, score_free = sem("score_done"), sem("score_free")
        out_done, out_free = sem("out_done"), sem("out_free")
        dve_chain, act_chain, pool_chain = sem("dve_chain"), sem("act_chain"), sem("pool_chain")
        s_squares = sem("s_squares")
        s_rstd = sem("s_rstd")
        s_rms = sem("s_rms")
        s_qscale = sem("s_qscale")
        s_xs = sem("s_xs")
        s_sums, s_roots = sem("s_sums"), sem("s_roots")
        s_h = sem("s_h")
        s_vec = sem("s_vec")
        s_lam = sem("s_lam")
        s_elam = sem("s_elam")
        s_soft = sem("s_soft")
        s_xc = sem("s_xc")
        s_ab = sem("s_ab")
        s_gated = sem("s_gated")
        s_scan = sem("s_scan")
        s_olru = sem("s_olru")
        s_lruhi = sem("s_lruhi")
        s_lrulo = sem("s_lrulo")
        s_qk = sem("s_qk")
        s_kd = sem("s_kd")
        s_zj = sem("s_zj")
        s_zjhi = sem("s_zjhi")
        s_zjlo = sem("s_zjlo")
        s_kcd = sem("s_kcd")
        s_pcm = sem("s_pcm")
        s_pce = sem("s_pce")
        s_masks = sem("s_masks")
        s_negm = sem("s_negm")
        s_mixo = sem("s_mixo")
        s_merged = sem("s_merged")
        s_rl = sem("s_rl")
        s_hid = sem("s_hid")
        s_ang = sem("s_ang")
        s_rope2 = sem("s_rope2")
        s_cur = sem("s_cur")
        s_y = sem("s_y")
        s_ypool = sem("s_ypool")
        s_ysq = sem("s_ysq")
        s_yn = sem("s_yn")
        s_silu = sem("s_silu")
        s_convhi = sem("s_convhi")
        s_convlo = sem("s_convlo")
        s_ple = sem("s_ple")
        s_result = sem("s_result")
        s_out = sem("s_out")

        def rows(w):
            return w.rearrange("(k p) n -> p k n", p=P)

        def layer_rows(w):
            return w.rearrange("l (k p) n -> l p k n", p=P)

        win1 = rows(a["w_in"][0])
        FIRST_COL = {"xr0": OFF_XR, "xr1": OFF_XR + COLS, "q": 0, "ks": OFF_KV, "kw": OFF_KW, "yr0": OFF_YR,
                     "yr1": OFF_YR + COLS, **{f"gm{i}": OFF_GM + i * COLS for i in range(4)}}
        view1 = {"nsa": rows(a["w_nsa_up"][0]), "lru": rows(a["w_lru_up"][0]), "o": rows(a["w_o"][0]),
                 "d": rows(a["w_ff2"][0])}
        phi1 = {"phi_k": rows(a["phi_k_w1"][0]), "phi_v": rows(a["phi_v_w1"][0])}
        ff1 = rows(a["w_ff1"][0])
        win2, wout2 = layer_rows(a["w_in_2"]), layer_rows(a["w_out_2"])
        win2_flat = a["w_in_2"].rearrange("l (k p) n -> p (l k) n", p=P)
        up2 = {"a": layer_rows(a["ffn1_w_gate_up_2"]), "b": layer_rows(a["ffn2_w_gate_up_2"])}
        dn2 = {"a": layer_rows(a["ffn1_w_down_2"]), "b": layer_rows(a["ffn2_w_down_2"])}
        wple, wpleg = layer_rows(a["w_ple_2"]), layer_rows(a["w_ple_gate_2"])
        L_COL = {"Lkv": HEADS * HD, "Lca": HEADS * HD + 2 * KV * HD,
                 "Lcg": HEADS * HD + 2 * KV * HD + CONV}

        def width(name):
            return W_KW if name == "kw" else 2 * KV * HD if name == "Lkv" else PHI if name in phi1 else COLS

        def tiles_of(name):
            return 1 if name.startswith("Lple") else UNIT_K

        def evacuated(eng, name, layer=None):
            n = CHUNKS.at(name, 0, layer)
            wait(eng, acc_free[n.slot(2)], n.lap(2) + 1)

        def turn_read(eng, name, k, layer=None):
            n = TURNS.at(name, k, layer)
            wait(eng, turn_free[n.slot(2)], n.lap(2) + 1)

        def turns_read(eng, name, count, layer=None):
            for k in range(max(0, count - 2), count):
                turn_read(eng, name, k, layer)

        block = ctx.enter_context(nc.Block())

        @block.sync
        def _(sp):
            def load(name, source, layer=None, step=None, per_step=0, k=0):
                for i in range(N_UNITS[name]):
                    n = UNITS.at(name, i + k, layer, step, per_step)
                    t = tiles_of(name)
                    src = source(i * t, t)
                    if n.const >= STAGE:
                        wait(sp, lo_done, n + (1 - STAGE))
                    sp.dma_start(stage[:, n.slot(STAGE), 0:t, 0:width(name)],
                                 src).then_inc(landed[n.slot(STAGE)], 16)

            def plain(view, c0, w=COLS):
                return lambda k0, t: view[:, k0:k0 + t, c0:c0 + w]

            def of_layer(view, layer, c0, w=COLS):
                return lambda k0, t: view[bass.ds(layer, 1), :, k0:k0 + t, c0:c0 + w].rearrange(
                    "o p k n -> (o p) k n")

            for t in range(TT):
                sp.dma_start(h[:, t, :], a["x"][0, t * P:(t + 1) * P, :]).then_inc(s_x, 16)
            for name in ["ks", "q", "kw", "xr0", "phi_k", "xr1", "phi_v", "yr0", "yr1", "gm0", "gm1", "gm2", "gm3"]:
                load(name, plain(phi1[name], 0, PHI) if name in phi1 else plain(win1, FIRST_COL[name], width(name)))
            for name in ["nsa0", "lru0", "nsa1", "lru1", "o0", "o1"]:
                load(name, plain(view1[name[:-1]], int(name[-1]) * COLS))
            with sp.Fori(0, NF // 2) as j:
                for i in range(2):
                    load("f0", lambda k0, t: ff1[:, k0:k0 + t, bass.ds(j * (2 * COLS) + i * COLS, COLS)],
                         step=j, per_step=2 * U, k=i * U)
            for name in ["d0", "d1"]:
                load(name, plain(view1["d"], int(name[-1]) * COLS))

            def swiglu_loads(f, layer):
                load(f"L{f}_up0", of_layer(up2[f], layer, 0), layer)
                with sp.Fori(0, (UPS - 1) // 2) as j:
                    for i in range(2):
                        load(f"L{f}_up1", lambda k0, t: up2[f][bass.ds(layer, 1), :, k0:k0 + t,
                             bass.ds(j * (2 * COLS) + (1 + i) * COLS, COLS)].rearrange("o p k n -> (o p) k n"),
                             layer, step=j, per_step=2 * U, k=i * U)
                for c in range(2):
                    load(f"L{f}_dn{c}", of_layer(dn2[f], layer, c * COLS), layer)

            with sp.Fori(0, layers) as layer:
                swiglu_loads("a", layer)
                for name in ["Lca", "Lcg"]:
                    load(name, of_layer(win2, layer, L_COL[name]), layer)
                load("Lq", lambda k0, t: win2_flat[:, bass.ds(layer * KD + k0, t), 0:COLS], layer)
                load("Lkv", of_layer(win2, layer, L_COL["Lkv"], width("Lkv")), layer)
                for c in range(2):
                    load(f"Lout{c}", of_layer(wout2, layer, c * COLS), layer)
                swiglu_loads("b", layer)
                for c in range(2):
                    load(f"Lple{c}", of_layer(wple, layer, c * COLS), layer)
                for c in range(2):
                    load(f"Lgate{c}", of_layer(wpleg, layer, c * COLS), layer)
            for t in range(TT):
                sp.wait_ge(s_result, t + 1)
                sp.dma_start(out[0, t * P:(t + 1) * P, :], xs[:, t, :]).then_inc(s_out, 16)
            sp.wait_ge(s_out, 16 * TT)

        @block.gpsimd
        def _(pool):
            chain = Chain(pool, pool_chain, POOL_LINKS)
            for i in range(2):
                w = a[["lru_wa", "lru_wx"][i]][0]
                pool.dma_start(w_gates[:, i, :, :], w.rearrange("n d e -> d n e")).then_inc(s_small, 16)
                w = a[["phi_k_w2", "phi_v_w2"][i]][0]
                pool.dma_start(w_phi2[:, i, :, :], w.rearrange("(k p) d -> p k d", p=P)).then_inc(s_small, 16)
            for i in range(12):
                w = a["q_norm_w"][0] if i < HEADS else a["k_norm_w"][0, 1 + (i - HEADS) // KV]
                pool.dma_start(qkw[:, i, :], w.partition_broadcast(P)).then_inc(s_small, 16)
            pool.dma_start(knw[:, :], a["k_norm_w"][0, 0].partition_broadcast(P)).then_inc(s_small, 16)
            pool.memset(kb[:, :, :, :], 0.0).then_inc(s_zero, 1)
            wait(pool, s_h, RESIDUAL.at("d", 2))
            for l in range(LAYERS):
                pool.dma_start(gn[:, l, :], a["ple_norm_2"][l].partition_broadcast(P)).then_inc(s_late, 16)
            pool.dma_start(gn[:, LAYERS, :], a["final_norm_2"].partition_broadcast(P)).then_inc(s_late, 16)
            pool.memset(u_t[:, :, 0:TAPS2 - 1], 0.0).then_inc(s_zero, 1)
            pool.memset(mean, 1.0 / CONV).then_inc(s_zero, 1)
            pool.wait_ge(s_late, 16 * (LAYERS + 1))
            p_rows = a["p_2"].rearrange("l o (t p) n -> p (l o t) n", p=P)
            pool.wait_ge(s_zero, 3)
            with pool.Fori(0, layers) as layer:
                chain.enter(layer)
                pool.wait_ge(s_cur, layer + 1)
                pool.dma_start(pcur[:, :, :], p_rows[:, bass.ds(layer * TT, TT), :]).then_inc(s_pcur, 16)
                n = KC - 1
                turns_read(pool, "Lu", 2, layer)
                def tap(j):
                    return tcur[:, j * KC + n:j * KC + n + 1].to_broadcast([P, S])
                chain.link(pool.tensor_tensor(y[:, n, :], u_t[:, n, 0:S], tap(0), ALU.mult))
                bias = vcur[:, V2["conv_b"] + n:V2["conv_b"] + n + 1].to_broadcast([P, S])
                chain.link(pool.tensor_tensor(y[:, n, :], y[:, n, :], bias, ALU.add))
                for j in range(1, TAPS2):
                    chain.link(pool.tensor_tensor(ysq[:, n, :], u_t[:, n, j:j + S], tap(j), ALU.mult))
                    ins = pool.tensor_tensor(y[:, n, :], y[:, n, :], ysq[:, n, :], ALU.add)
                    if j < TAPS2 - 1:
                        chain.link(ins)
                ins.then_inc(s_ypool, 1)
                chain.leave(layers)

        @block.scalar
        def _(act):
            def split(name, layer=None, step=None, per_step=0, k=0, units=None):
                for i in units if units is not None else range(N_UNITS[name]):
                    n = UNITS.at(name, i + k, layer, step, per_step)
                    wait(act, landed[n.slot(STAGE)], n.lap(STAGE) + 1, 16)
                    if n.const >= SPLIT:
                        wait(act, unit_used, n + (1 - SPLIT))
                    t, w = tiles_of(name), width(name)
                    act.activation(w_hi[:, n.slot(SPLIT), 0:t, 0:w], stage[:, n.slot(STAGE), 0:t, 0:w],
                                   ACT.Copy).then_inc(hi_done, 1)

            def chunk_done(name, layer=None, step=None, k=0):
                wait(act, unit_used, UNITS.at(name, k * N_UNITS[name] + N_UNITS[name], layer, step, 2 * N_UNITS[name]))
                return CHUNKS.at(name, k, layer, step, 2).slot(2)

            chain = Chain(act, act_chain, ACT_LINKS)

            def squares(src, width=D, at=0):
                for t in range(TT):
                    ins = act.activation(xs[:, t, 0:width], src[:, t, :], ACT.Square, scale=1.0 / width ** 0.5,
                                         accum_out=stat[:, at + t:at + t + 1])
                chain.link(ins)
                act.activation(stat[:, at:at + TT], stat[:, at:at + TT], ACT.Sqrt, bias=eps).then_inc(s_rms, 1)

            def half_squares(c):
                cols, at = slice(c * COLS, (c + 1) * COLS), STATS["half"] + c * TT
                for t in range(TT):
                    ins = act.activation(xs[:, t, cols], h[:, t, cols], ACT.Square, scale=1.0 / D ** 0.5,
                                         accum_out=stat[:, at + t:at + t + 1])
                if c == 1:
                    ins.then_inc(s_squares, 1)

            def rows_scaled(dst, src, func, at="rstd"):
                for t in range(TT):
                    at_t = STATS[at] + t
                    ins = act.activation(dst(t), src(t), func, scale=stat[:, at_t:at_t + 1])
                return ins

            def rms_boundary(last, norm, dst, gain, first, residual, layer=None):
                n_last, a = N_UNITS[last], 3 if N_UNITS[last] > U else 2
                split(last, layer, units=range(min(n_last, a + 3)))
                for k in (0, 1):
                    turned_hi(dst, norm, k, gain, layer)
                wait(act, s_h, RESIDUAL.at(residual, 1, layer))
                half_squares(0)
                split(last, layer, units=range(min(n_last, a + 3), n_last))
                split(first, layer, units=range(3))
                for k in (2, 3):
                    turned_hi(dst, norm, k, gain, layer)
                split(first, layer, units=range(3, U))
                wait(act, s_h, RESIDUAL.at(residual, 2, layer))
                half_squares(1)
                root(stat[:, 0:TT], norm, bias=eps, layer=layer)

            def root(dst, name, scale=1.0, bias=None, layer=None):
                n = ROOTS.at(name, 1, layer)
                wait(act, s_sums, n)
                act.activation(dst, dst, ACT.Sqrt, bias=0.0 if bias is None else bias, scale=scale).then_inc(s_roots, 1)

            def turned_hi(dst, name, k, gain=None, layer=None, step=None, per_step=0, at=None):
                n = TURNS.at(name, k, layer, step, per_step)
                wait(act, turn_done, n + 1)
                bank = turn[n.slot(2)][:, :].rearrange("p (k s) -> p k s", k=2)
                at = 2 * k if at is None else at
                if gain is None:
                    act.activation(dst[:, bass.ds(at, 2), :], bank, ACT.Copy).then_inc(turn_hi, 1)
                else:
                    for i in range(2):
                        ins = act.activation(dst[:, at + i, :], bank[:, i, :], ACT.Copy, scale=gain[:, at + i:at + i + 1])
                    ins.then_inc(turn_hi, 1)

            def turned_copy(dst, name, k, layer=None):
                n = TURNS.at(name, k, layer)
                wait(act, turn_done, n + 1)
                act.activation(dst, turn[n.slot(2)][:, :].rearrange("p (k s) -> p k s", k=2),
                               ACT.Copy).then_inc(turn_free[n.slot(2)], 1)

            def exps(name, j, sink, layer=None):
                w, b = P * (j // PAIRS + 1), j % 2
                wait(act, s_negm, HEAD_PAIRS.at(name, j + 1, layer))
                if sink:
                    act.activation(esink[:, b, :], esink[:, b, :], ACT.Exp)
                for i in range(2):
                    ins = act.activation(sm[:, b, i, 0:w], score[:, i * w:(i + 1) * w], ACT.Exp,
                                         bias=negm[:, b, i:i + 1], accum_out=den[:, b, i:i + 1])
                ins.then_inc(score_free, 1)

            def exps_t(name, j, layer=None):
                t = j // PAIRS
                n = TURNS.at(name, j, layer)
                wait(act, turn_done, n + 1)
                act.activation(p_t[:, :, 0:t + 1, :],
                               turn[n.slot(2)][:, 0:2 * (t + 1) * P].rearrange("p (i s q) -> p i s q", i=2, q=P),
                               ACT.Copy).then_inc(turn_free[n.slot(2)], 1)

            def attention(name, sink, layer=None):
                exps(name, 0, sink, layer)
                for j in range(2 * PAIRS):
                    if j + 1 < 2 * PAIRS:
                        exps(name, j + 1, sink, layer)
                    exps_t(name, j, layer)

            act.dma_start(ct[:, :], consts).then_inc(s_table, 16)

            def vector_rows(dst, row, v, done):
                act.dma_start(dst[row:row + v.shape[-1] // P, :], v.rearrange("(r p) -> r p", p=P)).then_inc(done, 16)

            for name, v in [("norm1", a["norm1_w"][0]), ("norm2", a["norm2_w"][0]), ("conv_b", a["conv_b"][0]),
                            ("lam", a["lru_lambda"][0])]:
                vector_rows(raw1, V1[name], v, s_const)
            act.dma_start(raw1[V1["conv_w"]:V1["conv_w"] + TAPS1 * KD, :],
                          a["conv_w"][0].rearrange("j (r p) -> (j r) p", p=P)).then_inc(s_const, 16)
            act.dma_start(raw1[V1["ba"]:V1["ba"] + KD, :], a["lru_ba"][0]).then_inc(s_const, 16)
            act.dma_start(raw1[V1["bx"]:V1["bx"] + KD, :], a["lru_bx"][0]).then_inc(s_const, 16)
            for name in ["k", "v"]:
                act.dma_start(raw1[V1["pos_" + name]:V1["pos_" + name] + KPHI, :],
                              a[f"phi_{name}_pos"][0].rearrange("(j l) d -> j (l d)", l=2)).then_inc(s_const, 16)
            act.wait_ge(s_x, 16 * TT)
            for c in range(2):
                half_squares(c)
            act.wait_ge(s_table, 16)
            root(stat[:, 0:TT], "norm1", bias=eps)
            split("ks")
            act.wait_ge(s_vec, 1)
            for k in range(4):
                turned_hi(x_hi, "norm1", k, vec1[:, V1["norm1"]:V1["norm1"] + KD])
            for l in range(LAYERS):
                for name, v in [("ffn1", "ffn1_norm_2"), ("mix", "mix_norm_2"), ("ffn2", "ffn2_norm_2"),
                                ("attn", "attn_out_norm_2"), ("conv", "conv_out_norm_2"), ("conv_b", "conv_b_2"),
                                ("ln_g", "conv_ln_g_2"), ("ln_b", "conv_ln_b_2")]:
                    vector_rows(raw2, l * NV2 + V2[name], a[v][l], s_vecs2)
                act.dma_start(rawt[:, l, :], a["conv_w_2"][l].rearrange("j (r p) -> (j r) p", p=P)).then_inc(s_vecs2, 16)
            act.dma_start(sinks[:, :, :], a["sinks_2"].partition_broadcast(P)).then_inc(s_vecs2, 16)
            for t in range(TT):
                act.dma_start(pos_i[:, t:t + 1], a["positions_2"][0, t * P:(t + 1) * P].unsqueeze(1)).then_inc(s_vecs2, 16)
            act.wait_ge(s_lam, 1)
            act.activation(softp[:, 3, :], softp[:, 2, :], ACT.Exp).then_inc(s_elam, 1)
            for i, at in enumerate([C_M1, C_M2]):
                act.activation(masks[:, i, :], ct[:, at:at + S], ACT.Copy)
            act.activation(ident_r[:, :], ident, ACT.Copy).then_inc(s_masks, 1)

            def heads(b, lo, hi):
                return lambda t: acc[b][:, t, lo:hi].rearrange("p (n d) -> p n d", d=HD)

            split("q")
            b = chunk_done("ks")
            act.wait_ge(s_rstd, 1)
            for i in range(2):
                rows_scaled(lambda t: cd[:, t, :, i, :], heads(b, 0, 2 * P), ACT.Copy)
            rows_scaled(lambda t: qk[:, t, HEADS:HEADS + KV, :], heads(b, 2 * P, 3 * P), ACT.Copy)
            rows_scaled(lambda t: vv[:, t, 0, :], lambda t: acc[b][:, t, 3 * P:], ACT.Copy).then_inc(acc_free[b], 1)
            split("kw")
            b = chunk_done("q")
            rows_scaled(lambda t: qk[:, t, 0:HEADS, :], heads(b, 0, COLS), ACT.Copy).then_inc(acc_free[b], 1)
            for k in range(2):
                n = TURNS.at("z", k)
                wait(act, turn_done, n + 1)
                bank = turn[n.slot(2)][:, :].rearrange("p (k s) -> p k s", k=2)
                act.activation(z[0:HD, 2 * k:2 * k + 2, :], bank[0:HD, :, :], ACT.Copy)
                act.activation(z[HD:P, 2 * k:2 * k + 2, 0:S - 1], bank[HD:P, :, 1:S],
                               ACT.Copy).then_inc(turn_free[n.slot(2)], 1)
            split("xr0")
            b = chunk_done("kw")
            rows_scaled(lambda t: qk[:, t, HEADS + KV:, :], heads(b, 0, P), ACT.Copy)
            rows_scaled(lambda t: vv[:, t, 1, :], lambda t: acc[b][:, t, P:2 * P], ACT.Copy)
            rows_scaled(lambda t: gsig[:, t, :, :], lambda t: acc[b][:, t, 2 * P:W_KW].rearrange("p (b n) -> p b n", b=3),
                        ACT.Sigmoid).then_inc(acc_free[b], 1)
            for i in range(2):
                act.wait_ge(s_zj, i + 1)
                act.activation(zj_hi[:, i, :, :], zj[:, :, :, :].rearrange("p j g n -> p j (g n)"),
                               ACT.Copy).then_inc(s_zjhi, 1)
            root(qk_ss[:, :], "qk", bias=eps)
            split("phi_k")

            def xr_rows(c):
                b = chunk_done(f"xr{c}")
                rows_scaled(lambda t: gy[:, t, c * COLS:(c + 1) * COLS], lambda t: acc[b][:, t, :],
                            ACT.Copy).then_inc(acc_free[b], 1)

            xr_rows(0)
            split("xr1")
            split("phi_v")
            xr_rows(1)
            split("yr0")
            for k in range(2):
                turned_copy(q_t[:, 2 * k:2 * k + 2, :], "q", k)
            for k in range(2):
                turned_copy(k_t[:, 2 * k:2 * k + 2, :], "k", k)
            wait(act, unit_used, UNITS.at("phi_v", units_of(KPHI)))
            act.activation(ghid[:, :], score[0:ROWS_C, :], ACT.Gelu_apprx_tanh).then_inc(score_free, 1)
            n = TURNS.at("hid")
            wait(act, turn_done, n + 1)
            act.activation(ghid_t[:, :, :],
                           turn[n.slot(2)][:, 0:4 * ROWS_C].rearrange("p (k s) -> p k s", k=4),
                           ACT.Copy).then_inc(turn_free[n.slot(2)], 1)
            act.wait_ge(s_vec, 4)
            for k in range(4):
                turned_copy(x_rt[:, 2 * k:2 * k + 2, TAPS1 - 1:], "xr", k)
            root(kcr[:, ROT:ROT + 1], "kc", bias=eps[0:ROWS_C, :])

            def yr_rows(c):
                b = chunk_done(f"yr{c}")
                rows_scaled(lambda t: gy[:, t, c * COLS:(c + 1) * COLS], lambda t: acc[b][:, t, :],
                            ACT.Gelu_apprx_tanh).then_inc(acc_free[b], 1)

            split("yr1")
            yr_rows(0)
            act.wait_ge(s_pcm, 1)
            act.activation(pc[:, :, :, :], pc[:, :, :, :], ACT.Exp).then_inc(s_pce, 1)
            split("gm0")
            yr_rows(1)
            n = TURNS.at("pc")
            wait(act, turn_done, n + 1)
            act.activation(pc_t[:, :], turn[n.slot(2)][0:HEADS * NCMP, 0:S], ACT.Copy).then_inc(turn_free[n.slot(2)], 1)
            for k in range(4):
                for plan, done, free, bank, dst, bias in [
                        (SCORES, score_done, score_free, score, lru_r, "ba"), (OUTS, out_done, out_free, outp, lru_i, "bx")]:
                    wait(act, done, plan.at("gates", k + 1))
                    for m in range(2):
                        f = 2 * k + m
                        ins = act.activation(dst[:, f, :], bank[:, m * S:(m + 1) * S], ACT.Sigmoid,
                                             bias=vec1[:, V1[bias] + f:V1[bias] + f + 1])
                    ins.then_inc(free, 1)
            wait(act, score_free, SCORES.at("gates", 4))
            act.wait_ge(s_soft, 1)
            for f in range(KD):
                act.activation(th[:, f, :], lru_r[:, f, :], ACT.Tanh, scale=softp[:, 0, f:f + 1])
            for f in range(KD):
                ins = act.activation(lru_r[:, f, :], lru_r[:, f, :], ACT.Exp, scale=softp[:, 1, f:f + 1])
            ins.then_inc(s_ab, 1)
            root(den2, "lru")

            def gate_chunk(c):
                b = chunk_done(f"gm{c}")
                rows_scaled(lambda t: gate[:, t, c * COLS:(c + 1) * COLS], lambda t: acc[b][:, t, :],
                            ACT.Sigmoid).then_inc(acc_free[b], 1)

            exps("slc", 0, False)
            for i, (name, j) in enumerate(JOBS):
                if i + 1 < len(JOBS):
                    exps(*JOBS[i + 1], False)
                exps_t(name, j)
                split(BESIDE[i + SPLIT][0], units=[BESIDE[i + SPLIT][1]])
                if i % U == U - 1:
                    gate_chunk(i // U)
                if (name, j) == ("slc", 2 * PAIRS - 1):
                    for k in range(4):
                        act.wait_ge(s_olru, k + 1)
                        act.activation(lru_hi[:, 2 * k:2 * k + 2, :], xc[:, 2 * k:2 * k + 2, :],
                                       ACT.Copy).then_inc(s_lruhi, 1)
            for k in range(2):
                turned_hi(nsa_hi, "nsa", k)
            split("lru0", units=range(2, 4))
            for name in ["nsa1", "lru1", "o0"]:
                split(name)
            for k in range(4):
                turned_hi(x_hi, "merged", k)
            rms_boundary("o1", "norm2", x2_hi, vec1[:, V1["norm2"]:V1["norm2"] + KD], "f0", "o")

            def relu_chunk(i, step=None):
                b = chunk_done("f0", None, step, i)
                rows_scaled(lambda t: relu[:, i % 2, t, :], lambda t: acc[b][:, t, :], ACT.Relu).then_inc(s_rl, 1)

            def ff_hi(i, step=None):
                for m in range(2):
                    k = 2 * i + m
                    turned_hi(f_hi, "ff", k, None, None, step, 4, 2 * k if step is None else step * 8 + 2 * k)

            split("f1")
            act.wait_ge(s_rstd, 2)
            relu_chunk(0)
            with act.Fori(0, NF // 2 - 1) as j:
                for i in (1, 2):
                    split("f0", None, j, 2 * U, (i + 1) * U)
                    relu_chunk(i, j)
                    ff_hi(i - 1, j)
            split("d0", units=range(U))
            relu_chunk(NF - 1)
            ff_hi(NF - 2)
            ff_hi(NF - 1)
            split("d0", units=range(U, N_UNITS["d0"]))
            split("d1")
            act.wait_ge(s_ang, 1)
            for m in range(2):
                act.activation(rope2[:, :, m * HALF:(m + 1) * HALF], ang[:, 1, :, :], ACT.Sin)
            act.activation(rope2[:, :, 2 * HALF:3 * HALF], ang[:, 0, :, :], ACT.Sin, scale=-1.0)
            act.activation(rope2[:, :, 3 * HALF:4 * HALF], ang[:, 0, :, :], ACT.Sin).then_inc(s_rope2, 1)

            def swiglu(f, after, layer):

                def silu_chunk(i, step=None):
                    b = chunk_done(f"L{f}_up0", layer, step, i)
                    rows_scaled(lambda t: silu[:, i % 2, t, :], lambda t: acc[b][:, t, 0:HALFW],
                                ACT.Silu).then_inc(s_rl, 1)

                def hid_hi(i, step=None):
                    turned_hi(g_hi, f"L{f}_hid", i, None, layer, step, 2, 2 * i if step is None else step * 4 + 2 * i)

                split(f"L{f}_up1", layer)
                wait(act, s_rstd, RSTD.at(f"L{f}_norm", 1, layer))
                silu_chunk(0)
                with act.Fori(0, (UPS - 1) // 2 - 1) as j:
                    for i in (1, 2):
                        split(f"L{f}_up0", layer, j, 2 * U, (i + 1) * U)
                        silu_chunk(i, j)
                        hid_hi(i - 1, j)
                split(f"L{f}_up{UPS - 1}", layer)
                silu_chunk(UPS - 2)
                hid_hi(UPS - 3)
                split(f"L{f}_dn0", layer, units=range(U))
                silu_chunk(UPS - 1)
                hid_hi(UPS - 2)
                hid_hi(UPS - 1)
                split(f"L{f}_dn0", layer, units=range(U, N_UNITS[f"L{f}_dn0"]))
                after()

            def mix_boundary():
                rms_boundary("La_dn1", "Lmix", x_hi, vcur[:, V2["mix"]:V2["mix"] + KD], "Lca", "La_dn", layer)

            def raw_boundary():
                split("Lb_dn1", layer, units=range(3))
                turned_hi(pl_hi, "Lp", 0, None, layer)
                split("Lb_dn1", layer, units=range(3, 6))
                for k in (0, 1):
                    turned_hi(x_hi, "Lraw", k, None, layer)
                split("Lb_dn1", layer, units=range(6, N_UNITS["Lb_dn1"]))
                split("Lple0", layer)
                split("Lple1", layer)
                for k in (2, 3):
                    turned_hi(x_hi, "Lraw", k, None, layer)

            with act.Fori(0, layers) as layer:
                chain.enter(layer)
                split("La_up0", layer)
                act.wait_ge(s_cur, layer + 1)
                for k in range(4):
                    turned_hi(x2_hi, "La_norm", k, vcur[:, V2["ffn1"]:V2["ffn1"] + KD], layer)
                wait(act, s_h, RESIDUAL.at("La_dn", 0, layer))
                for c in range(2):
                    half_squares(c)
                root(stat[:, 0:TT], "La_norm", bias=eps, layer=layer)
                swiglu("a", mix_boundary, layer)
                split("Lcg", layer)
                split("Lq", layer)
                b = chunk_done("Lcg", layer)
                wait(act, s_rstd, RSTD.at("Lmix", 1, layer))
                rows_scaled(lambda t: sig[:, t, :], lambda t: acc[b][:, t, :], ACT.Sigmoid).then_inc(acc_free[b], 1)
                split("Lkv", layer)
                b = chunk_done("Lq", layer)
                act.wait_ge(s_qscale, layer + 1)
                rows_scaled(lambda t: qk[:, t, 0:HEADS, :], heads(b, 0, COLS), ACT.Copy, "q").then_inc(acc_free[b], 1)
                act.wait_ge(s_zero, 3)
                for k in range(2):
                    turned_copy(u_t[:, 2 * k:2 * k + 2, TAPS2 - 1:], "Lu", k, layer)
                split("Lout0", layer)
                b = chunk_done("Lkv", layer)
                rows_scaled(lambda t: qk[:, t, HEADS:HEADS + KV, :], heads(b, 0, P), ACT.Copy)
                rows_scaled(lambda t: vv[:, t, 0, :], lambda t: acc[b][:, t, P:2 * P], ACT.Copy).then_inc(acc_free[b], 1)
                for k in range(2):
                    turned_copy(q_t[:, 2 * k:2 * k + 2, :], "Lq", k, layer)
                turned_copy(k_t[:, 0:2, :], "Lk", 0, layer)
                attention("Latt", True, layer)
                wait(act, s_mixo, Count(2, [(layer, 1)]))
                squares(mixo, CONV, STATS["attn"])
                for k in range(2):
                    turned_hi(x_hi, "Lmixed", k, vcur[:, V2["attn"]:V2["attn"] + 4], layer)
                def sums_root(i):
                    n = SCORES.at("Lsum", i, layer)
                    wait(act, score_done, n + 1)
                    act.activation(sig[:, 0, 0:S], score[:, 0:S], ACT.Sqrt, bias=eps).then_inc(score_free, 1)

                wait(act, score_free, SCORES.at("Lsum", 1, layer))
                act.activation(ysq[:, :, :], y[:, :, :], ACT.Square).then_inc(s_ysq, 1)
                sums_root(1)
                wait(act, s_yn, Count(1, [(layer, 2)]))
                for n in range(KC):
                    ins = act.activation(y[:, n, :], y[:, n, :], ACT.Silu, scale=vcur[:, V2["ln_g"] + n:V2["ln_g"] + n + 1],
                                         bias=vcur[:, V2["ln_b"] + n:V2["ln_b"] + n + 1])
                ins.then_inc(s_silu, 1)
                act.wait_ge(s_silu, layer + 1)
                act.activation(ysq[:, :, :], y[:, :, :], ACT.Square).then_inc(s_ysq, 1)
                sums_root(2)
                wait(act, s_yn, Count(2, [(layer, 2)]))
                for n in range(KC):
                    ins = act.activation(x_hi[:, 4 + n, :], y[:, n, :], ACT.Copy,
                                         scale=vcur[:, V2["conv"] + n:V2["conv"] + n + 1])
                ins.then_inc(s_convhi, 1)
                rms_boundary("Lout1", "Lb_norm", x2_hi, vcur[:, V2["ffn2"]:V2["ffn2"] + KD], "Lb_up0", "Lout", layer)
                swiglu("b", raw_boundary, layer)
                split("Lgate0", layer, units=range(2))
                for c in range(2):
                    b = chunk_done(f"Lple{c}", layer)
                    for t in range(TT):
                        squared = sig[:, t, :] if c == 0 else ysq[:, 2 * t:2 * t + 2, :].rearrange("p k s -> p (k s)")
                        act.activation(squared, acc[b][:, t, :], ACT.Square, scale=1.0 / D ** 0.5,
                                       accum_out=stat[:, STATS["ple"] + c * TT + t:STATS["ple"] + c * TT + t + 1]).then_inc(s_ple, 1)
                root(stat[:, STATS["e"]:STATS["e"] + TT], "Lple", bias=eps, layer=layer)
                split("Lgate0", layer, units=range(2, 4))
                split("Lgate1", layer)
                for c in range(2):
                    b = chunk_done(f"Lgate{c}", layer)
                    if c == 1:
                        wait(act, s_h, RESIDUAL.at("Lgate", 1, layer))
                    act.activation(sig[:, :, :], acc[b][:, :, :], ACT.Sigmoid).then_inc(acc_free[b], 1)
                chain.leave(layers)
            act.wait_ge(s_h, 4 + RESIDUAL.per_layer * layers)
            squares(h)

        @block.vector
        def _(dve):
            chain = Chain(dve, dve_chain, DVE_LINKS)
            link = chain.link

            def split(name, layer=None, step=None, per_step=0, k=0, units=None):
                for i in units if units is not None else range(N_UNITS[name]):
                    n = UNITS.at(name, i + k, layer, step, per_step)
                    wait(dve, hi_done, n + 1)
                    t, w = tiles_of(name), width(name)
                    dve.tensor_tensor(w_lo[:, n.slot(SPLIT), 0:t, 0:w], stage[:, n.slot(STAGE), 0:t, 0:w],
                                      w_hi[:, n.slot(SPLIT), 0:t, 0:w].bitcast(F32), ALU.subtract).then_inc(lo_done, 1)

            def chunk_done(name, layer=None):
                wait(dve, unit_used, UNITS.at(name, N_UNITS[name], layer))
                return CHUNKS.at(name, 0, layer).slot(2)

            def rooted(ins, name, layer=None):
                ins.then_inc(s_sums, 1)
                wait(dve, s_roots, ROOTS.at(name, 1, layer))

            def row_factors(name, layer=None):
                wait(dve, s_squares, RSTD.at(name, 1, layer))
                at = STATS["half"]
                rooted(dve.tensor_tensor(stat[:, 0:TT], stat[:, at:at + TT], stat[:, at + TT:at + 2 * TT], ALU.add),
                       name, layer)
                dve.reciprocal(stat[:, 0:TT], stat[:, 0:TT]).then_inc(s_rstd, 1)
                wait(dve, s_rstd, RSTD.at(name, 1, layer))

            def rms_boundary(parts, norm, hi, lo, gain, first, layer=None):
                n_last, a = N_UNITS[parts[1]], 3 if N_UNITS[parts[1]] > U else 2
                scale = 0.5 if "dn" in parts[1] else 1.0
                split(parts[1], layer, units=range(3))
                add_residual(parts[0], 0, scale, layer)
                split(parts[1], layer, units=range(3, min(n_last, a + 3)))
                for k in (0, 1):
                    turned_lo(hi, lo, norm, k, gain, layer)
                split(parts[1], layer, units=range(min(n_last, a + 3), n_last))
                split(first, layer, units=range(2))
                add_residual(parts[1], 1, scale, layer)
                split(first, layer, units=range(2, 3))
                for k in (2, 3):
                    turned_lo(hi, lo, norm, k, gain, layer)
                split(first, layer, units=range(3, U))
                row_factors(norm, layer)

            def turned_lo(hi, lo, name, k, gain=None, layer=None, step=None, per_step=0, at=None):
                n = TURNS.at(name, k, layer, step, per_step)
                wait(dve, turn_hi, HI_TURNS.at(name, k + 1, layer, step, per_step))
                bank = turn[n.slot(2)][:, :].rearrange("p (k s) -> p k s", k=2)
                at = 2 * k if at is None else at
                if gain is None:
                    dve.tensor_tensor(lo[:, bass.ds(at, 2), :], bank, hi[:, bass.ds(at, 2), :].bitcast(F32),
                                      ALU.subtract).then_inc(turn_free[n.slot(2)], 1)
                else:
                    for i in range(2):
                        ins = dve.scalar_tensor_tensor(lo[:, at + i, :], bank[:, i, :], gain[:, at + i:at + i + 1],
                                                       hi[:, at + i, :].bitcast(F32), ALU.mult, ALU.subtract)
                    ins.then_inc(turn_free[n.slot(2)], 1)

            def add_residual(name, c, scale, layer=None):
                b = chunk_done(name, layer)
                hc = h[:, :, c * COLS:(c + 1) * COLS]
                dve.scalar_tensor_tensor(hc, acc[b][:, :, :], scale, hc, ALU.mult, ALU.add).then_inc(acc_free[b], 1)
                evacuated(dve, name, layer)
                dve.sem_inc(s_h, 1)

            def rotate(x, table, tmp, x1_x2):
                lo, hi = x1_x2
                dve.tensor_tensor(tmp[0], hi, table(2), ALU.mult)
                link(dve.tensor_tensor(tmp[1], lo, table(3), ALU.mult))
                dve.tensor_tensor(lo, lo, table(0), ALU.mult)
                link(dve.tensor_tensor(hi, hi, table(1), ALU.mult))
                dve.tensor_tensor(lo, lo, tmp[0], ALU.add)
                return dve.tensor_tensor(hi, hi, tmp[1], ALU.add)

            def rotate_heads(heads, table):
                x = qk[:, :, 0:heads, :]
                def part(i):
                    return table[:, :, i * HALF:(i + 1) * HALF].unsqueeze(2).to_broadcast([P, TT, heads, HALF])
                return rotate(x, part, [ropet[:, :, 0:heads, 0:HALF], ropet[:, :, 0:heads, HALF:ROT]],
                              (x[:, :, :, 0:HALF], x[:, :, :, HALF:ROT]))

            def maxima(name, j, sink, layer=None):
                t, p, b, w = j // PAIRS, j % PAIRS, j % 2, P * (j // PAIRS + 1)
                wait(dve, score_done, SCORES.at(name, j + 1, layer))
                link(dve.tensor_reduce(mx[:, b, :], score[:, 0:2 * w].rearrange("p (i s) -> p i s", i=2), AX_X, ALU.max))
                if sink:
                    of_pair = heads_of(scur[:, :], p).rearrange("q a d -> q (a d)")
                    link(dve.tensor_tensor(mx[:, b, :], mx[:, b, :], of_pair, ALU.max))
                    dve.tensor_tensor(esink[:, b, :], of_pair, mx[:, b, :], ALU.subtract)
                dve.tensor_scalar(negm[:, b, :], mx[:, b, :], -1.0, None, ALU.mult).then_inc(s_negm, 1)

            def weigh_output(name, j, branch, sink, layer=None):
                t, p, b = j // PAIRS, j % PAIRS, j % 2
                wait(dve, score_free, SCORES.at(name, j + 1, layer))
                if sink:
                    link(dve.tensor_tensor(den[:, b, :], den[:, b, :], esink[:, b, :], ALU.add))
                link(dve.reciprocal(coef[:, :], den[:, b, :]))
                if branch is not None:
                    link(dve.tensor_tensor(coef[:, :], coef[:, :],
                                           heads_of(gsig[:, t, branch, :], p).rearrange("q a d -> q (a d)"), ALU.mult))
                n = OUTS.at(name, j, layer)
                wait(dve, out_done, n + 1)
                o = heads_of(mixo[:, t, :], p)
                res = outp[:, 0:2 * HD].rearrange("p (n d) -> p n d", d=HD)
                cb = coef[:, :].unsqueeze(2).to_broadcast([P, 2, HD])
                dve.tensor_tensor(o if branch is None else tmpo[:, :, :], res, cb, ALU.mult).then_inc(out_free, 1)
                wait(dve, out_free, n + 1)
                if branch is not None:
                    link(dve.tensor_tensor(o, o, tmpo[:, :, :], ALU.add))

            def vector_in(k, plan, done, free, bank, dst, cols):
                wait(dve, done, plan.at("vec", k + 1))
                dve.tensor_copy(dst, bank[:, 0:cols]).then_inc(free, 1)
                wait(dve, free, plan.at("vec", k + 1))
                dve.sem_inc(s_vec, 1)

            vector_in(0, SCORES, score_done, score_free, score, vec1[:, :], NV1)
            row_factors("norm1")
            split("ks")
            for k in range(4):
                turned_lo(x_hi, x_lo, "norm1", k, vec1[:, V1["norm1"]:V1["norm1"] + KD])
            lam = vec1[:, V1["lam"]:V1["lam"] + KD]
            dve.scalar_tensor_tensor(softp[:, 2, :], lam, -1.0, lam, ALU.mult, ALU.min).then_inc(s_lam, 1)
            split("q")
            dve.wait_ge(s_elam, 1)
            e, z1, z2, s = (softp[:, i, :] for i in (3, 4, 5, 6))
            link(dve.tensor_scalar(z2, e, 2.0, None, ALU.add))
            link(dve.reciprocal(z2, z2))
            link(dve.tensor_tensor(z1, e, z2, ALU.mult))
            link(dve.tensor_tensor(z2, z1, z1, ALU.mult))
            link(dve.tensor_scalar(s, z2, 1.0 / 19, None, ALU.mult))
            for odd in range(17, 1, -2):
                link(dve.scalar_tensor_tensor(s, s, 1.0 / odd, z2, ALU.add, ALU.mult))
            link(dve.scalar_tensor_tensor(s, s, 1.0, z1, ALU.add, ALU.mult))
            link(dve.tensor_scalar(z1, lam, -8.0, 0.0, ALU.mult, ALU.max))
            link(dve.scalar_tensor_tensor(softp[:, 0, :], s, 16.0, z1, ALU.mult, ALU.add))
            dve.tensor_scalar(softp[:, 1, :], softp[:, 0, :], -1.0, None, ALU.mult).then_inc(s_soft, 1)
            split("kw")
            vector_in(0, OUTS, out_done, out_free, outp, vec2[:, :, :].rearrange("p l v -> p (l v)"), LAYERS * NV2)
            vector_in(1, SCORES, score_done, score_free, score, taps2[:, 0, :], TAPS2 * KC)
            vector_in(1, OUTS, out_done, out_free, outp, taps2[:, 1, :], TAPS2 * KC)
            dve.memset(x_rt[:, :, 0:TAPS1 - 1], 0.0)
            for i in range(2):
                turn_read(dve, "z", i)
                if i == 1:
                    dve.wait_ge(s_zjlo, 1)
                zi = z[:, 2 * i:2 * i + 2, :]
                src = bass.AP(zi.tensor, zi.offset, [zi.ap[0], [2, KPHI], [S, KV], [CMP_STRIDE, NCMP]])
                pos = vec1[:, V1["pos_" + "kv"[i]]:V1["pos_" + "kv"[i]] + KPHI]
                dve.tensor_tensor(zj[:, :, :, :], src, pos.unsqueeze(2).unsqueeze(3).to_broadcast([P, KPHI, KV, NCMP]),
                                  ALU.add).then_inc(s_zj, 1)
                dve.wait_ge(s_zjhi, i + 1)
                dve.tensor_tensor(zj_lo[:, i, :, :], zj[:, :, :, :].rearrange("p j g n -> p j (g n)"),
                                  zj_hi[:, i, :, :].bitcast(F32), ALU.subtract).then_inc(s_zjlo, 1)
            split("xr0")
            for name in ["q", "ks", "kw"]:
                evacuated(dve, name)
            dve.wait_ge(s_small, 16 * 17)
            turns_read(dve, "norm1", 4)
            qk_flat = qk[:, :, :, :].rearrange("p t n d -> p t (n d)")
            heads = qk[:, :, :, :].rearrange("p t n d -> p (t n) d")
            ss = qk_ss[:, :]
            link(dve.scalar_tensor_tensor(sq, qk_flat, 1.0 / HD, qk_flat, ALU.mult, ALU.mult))
            rooted(dve.tensor_reduce(ss.rearrange("p (t n) -> p t n", t=TT), sq.rearrange("p t (n d) -> p t n d", d=HD),
                                     AX_X, ALU.add), "qk")
            link(dve.reciprocal(ss, ss))
            ssq = ss.rearrange("p (t n) -> p t n", t=TT)[:, :, 0:HEADS]
            link(dve.tensor_scalar(ssq, ssq, HD ** -0.5, None, ALU.mult))
            link(dve.tensor_tensor(heads, heads, ss.unsqueeze(2).to_broadcast([P, TT * 12, HD]), ALU.mult))
            for t in range(TT):
                ins = dve.tensor_tensor(qk[:, t, :, :], qk[:, t, :, :], qkw[:, :, :], ALU.mult)
            link(ins)
            rotate_heads(12, ct[:, C_ROPE:C_ROPE + TT * 2 * ROT].rearrange("p (t r) -> p t r", t=TT)).then_inc(s_qk, 1)
            dve.wait_ge(s_qk, 1)
            for i in range(2):
                ins = dve.tensor_copy(kd[:, :, :, i, :], qk[:, :, HEADS:, :])
            ins.then_inc(s_kd, 1)
            for name in ["phi_k", "xr1", "phi_v", "yr0"]:
                split(name)
            wait(dve, out_done, OUTS.at("kvc", 1))
            dve.tensor_copy(kvc[:, :, :], outp[0:ROWS_C, 0:2 * HD].rearrange("p (i d) -> p i d", i=2)).then_inc(out_free, 1)
            wait(dve, out_free, OUTS.at("kvc", 1))
            kc, rt = kvc[:, 0, :], kcr[:, ROT:ROT + 1]
            link(dve.scalar_tensor_tensor(kcs[:, :], kc, 1.0 / HD, kc, ALU.mult, ALU.mult))
            rooted(dve.tensor_reduce(rt, kcs[:, :], AX_X, ALU.add), "kc")
            link(dve.reciprocal(rt, rt))
            link(dve.scalar_tensor_tensor(kc, kc, rt, knw[0:ROWS_C, :], ALU.mult, ALU.mult))
            link(rotate(kc, lambda i: ct[0:ROWS_C, C_ROPEC + i * HALF:C_ROPEC + (i + 1) * HALF],
                        [kcr[:, 0:HALF], kcr[:, HALF:ROT]], (kc[:, 0:HALF], kc[:, HALF:ROT])))
            for i in range(2):
                ins = dve.tensor_copy(kcd[:, i, :], kc)
            ins.then_inc(s_kcd, 1)
            dve.wait_ge(s_zero, 1)
            n = TURNS.at("kc")
            wait(dve, turn_done, n + 1)
            for i in range(2):
                ins = dve.tensor_copy(kb[i * HD:(i + 1) * HD, :, i, :],
                                      turn[n.slot(2)][i * HD:(i + 1) * HD, 0:ROWS_C].rearrange("p (g n) -> p g n", g=KV))
            ins.then_inc(turn_free[n.slot(2)], 1)
            wait(dve, out_done, OUTS.at("vb", 1))
            dve.tensor_tensor(vb[:, :, :], outp[0:HEADS * NCMP, 0:HD].unsqueeze(1).to_broadcast([HEADS * NCMP, HEADS, HD]),
                              ct[0:HEADS * NCMP, C_SELM:C_SELM + HEADS].unsqueeze(2).to_broadcast([HEADS * NCMP, HEADS, HD]),
                              ALU.mult).then_inc(out_free, 1)
            for k in range(4):
                turn_read(dve, "xr", k)
            for j in range(TAPS1):
                for f in range(KD):
                    wj = vec1[:, V1["conv_w"] + j * KD + f:V1["conv_w"] + j * KD + f + 1]
                    if j == 0:
                        ins = dve.tensor_scalar(xc[:, f, :], x_rt[:, f, 0:S], wj,
                                                vec1[:, V1["conv_b"] + f:V1["conv_b"] + f + 1], ALU.mult, ALU.add)
                    else:
                        ins = dve.scalar_tensor_tensor(xc[:, f, :], x_rt[:, f, j:j + S], wj, xc[:, f, :],
                                                       ALU.mult, ALU.add)
                if j < TAPS1 - 1:
                    link(ins)
            ins.then_inc(s_xc, 1)
            split("yr1")
            wait(dve, score_done, SCORES.at("cmp", 1))
            mask = ct[:, C_CMASK:C_CMASK + TT * NCMP].rearrange("p (t n) -> p t n", t=TT)
            for t in range(TT):
                ins = dve.tensor_tensor(pc[:, t, :, :], score[:, t * HEADS * NCMP:(t + 1) * HEADS * NCMP].rearrange("p (h n) -> p h n", n=NCMP),
                                        mask[:, t, :].unsqueeze(1).to_broadcast([P, HEADS, NCMP]), ALU.add)
            ins.then_inc(score_free, 1)
            wait(dve, score_free, SCORES.at("cmp", 1))
            pcf = pc[:, :, :, :].rearrange("p t h n -> p (t h) n")
            pmx, pco = (pcs[:, i, :, :].rearrange("p t h -> p (t h)") for i in range(2))
            link(dve.tensor_reduce(pmx, pcf, AX_X, ALU.max))
            dve.tensor_tensor(pcf, pcf, pmx.unsqueeze(2).to_broadcast([P, TT * HEADS, NCMP]), ALU.subtract).then_inc(s_pcm, 1)
            dve.wait_ge(s_pce, 1)
            link(dve.tensor_reduce(pmx, pcf, AX_X, ALU.add))
            link(dve.reciprocal(pco, pmx))
            for t in range(TT):
                ins = dve.scalar_tensor_tensor(pcs[:, 1, t, :], pcs[:, 1, t, :], ct[:, C_ROWOK + t:C_ROWOK + t + 1],
                                               gsig[:, t, 0, :], ALU.mult, ALU.mult)
            link(ins)
            split("gm0")
            for t in range(TT):
                n = OUTS.at("cmp", t)
                wait(dve, out_done, n + 1)
                dve.tensor_tensor(mixo[:, t, :].rearrange("p (h d) -> p h d", d=HD),
                                  outp[:, :].rearrange("p (h d) -> p h d", d=HD),
                                  pcs[:, 1, t, :].unsqueeze(2).to_broadcast([P, HEADS, HD]), ALU.mult).then_inc(out_free, 1)
            dve.wait_ge(s_ab, 1)
            wait(dve, out_free, OUTS.at("gates", 4))
            link(dve.tensor_tensor(den2, lru_r[:, :, :], lru_r[:, :, :], ALU.mult))
            dve.scalar_tensor_tensor(den2, den2, 1.0, th, ALU.add, ALU.mult).then_inc(s_sums, 1)

            def recurrence(step):
                if step == 0:
                    dve.tensor_tensor(lru_i[:, :, :], lru_i[:, :, :], xc[:, :, :], ALU.mult).then_inc(s_gated, 1)
                elif step == 1:
                    wait(dve, s_roots, ROOTS.at("lru", 1))
                    dve.wait_ge(s_gated, 1)
                    dve.tensor_tensor(lru_i[:, :, :], lru_i[:, :, :], den2, ALU.mult).then_inc(s_gated, 1)
                elif step < 6:
                    dve.wait_ge(s_gated, 2)
                    for f in (2 * step - 4, 2 * step - 3):
                        dve.tensor_tensor_scan(xc[:, f, :], lru_r[:, f, :], lru_i[:, f, :], 0.0, ALU.mult,
                                               ALU.add).then_inc(s_scan, 1)

            maxima("slc", 0, False)
            for i, (name, j) in enumerate(JOBS):
                if i + 1 < len(JOBS):
                    maxima(*JOBS[i + 1], False)
                recurrence(i)
                weigh_output(name, j, 1 if name == "slc" else 2, False)
                split(BESIDE[i + SPLIT][0], units=[BESIDE[i + SPLIT][1]])
                if (name, j) == ("slc", 2 * PAIRS - 1):
                    dve.wait_ge(s_scan, KD)
                    for k in range(4):
                        n = TURNS.at("yr", k)
                        wait(dve, turn_done, n + 1)
                        xk = xc[:, 2 * k:2 * k + 2, :]
                        dve.tensor_tensor(xk, turn[n.slot(2)][:, :].rearrange("p (k s) -> p k s", k=2), xk,
                                          ALU.mult).then_inc(turn_free[n.slot(2)], 1)
                        turn_read(dve, "yr", k)
                        dve.sem_inc(s_olru, 1)
                        dve.wait_ge(s_lruhi, k + 1)
                        dve.tensor_tensor(lru_lo[:, 2 * k:2 * k + 2, :], xk, lru_hi[:, 2 * k:2 * k + 2, :].bitcast(F32),
                                          ALU.subtract).then_inc(s_lrulo, 1)
            dve.sem_inc(s_mixo, 1)
            for k in range(2):
                turned_lo(nsa_hi, nsa_lo, "nsa", k)
            split("lru0", units=range(2, 4))
            for c in range(2):
                if c == 0:
                    split("nsa1")
                for i, name in enumerate(["nsa", "lru"]):
                    if i == 1:
                        split(["lru1", "o0"][c])
                    b = chunk_done(f"{name}{c}")
                    evacuated(dve, f"gm{2 * i + c}")
                    gc = gate[:, :, (2 * i + c) * COLS:(2 * i + c + 1) * COLS]
                    mc = merged[:, :, c * COLS:(c + 1) * COLS]
                    dve.tensor_tensor(mc if i == 0 else gc, acc[b][:, :, :], gc, ALU.mult).then_inc(acc_free[b], 1)
                    evacuated(dve, f"{name}{c}")
                    if i == 1:
                        dve.tensor_tensor(mc, mc, gc, ALU.add).then_inc(s_merged, 1)
            for k in range(4):
                turned_lo(x_hi, x_lo, "merged", k)
            rms_boundary(["o0", "o1"], "norm2", x2_hi, x2_lo, vec1[:, V1["norm2"]:V1["norm2"] + KD], "f0")

            def square_chunk(i, step=None):
                wait(dve, s_rl, HIDDEN.at("ff", i + 1, None, step, 2))
                n = CHUNKS.at("f0", i, None, step, 2)
                b = n.slot(2)
                for t in range(TT):
                    ins = dve.scalar_tensor_tensor(hid1[:, i % 2, t, :], acc[b][:, t, :], stat[:, t:t + 1],
                                                   relu[:, i % 2, t, :], ALU.mult, ALU.mult)
                ins.then_inc(acc_free[b], 1)

            def ff_lo(i, step=None):
                for m in range(2):
                    k = 2 * i + m
                    turned_lo(f_hi, f_lo, "ff", k, None, None, step, 4, 2 * k if step is None else step * 8 + 2 * k)

            split("f1")
            square_chunk(0)
            with dve.Fori(0, NF // 2 - 1) as j:
                for i in (1, 2):
                    split("f0", None, j, 2 * U, (i + 1) * U)
                    square_chunk(i, j)
                    ff_lo(i - 1, j)
            split("d0", units=range(U))
            square_chunk(NF - 1)
            ff_lo(NF - 2)
            ff_lo(NF - 1)
            split("d0", units=range(U, N_UNITS["d0"]))
            TURN = [float(np.float32(6.28125)), float(np.float32(2 * np.pi - 6.28125)),
                    float(2 * np.pi - 6.28125 - np.float32(2 * np.pi - 6.28125))]
            a0, a1, a2 = (ang[:, i, :, :] for i in range(3))
            link(dve.tensor_copy(pos_f[:, :], pos_i[:, :]))
            link(dve.tensor_tensor(a0, pos_f[:, :].unsqueeze(2).to_broadcast([P, TT, HALF]),
                                   ct[:, C_INV:C_INV + HALF].unsqueeze(1).to_broadcast([P, TT, HALF]), ALU.mult))
            link(dve.tensor_scalar(a1, a0, 0.5 / np.pi, None, ALU.mult))
            link(dve.tensor_scalar(a1, a1, 1.5 * 2 ** 23, None, ALU.add))
            link(dve.tensor_scalar(a1, a1, 1.5 * 2 ** 23, None, ALU.subtract))
            for part in TURN:
                link(dve.scalar_tensor_tensor(a0, a1, -part, a0, ALU.mult, ALU.add))
            link(dve.tensor_scalar(a0, a0, float(np.float32(3.1415925)), -float(np.float32(3.1415925)), ALU.min, ALU.max))
            link(dve.scalar_tensor_tensor(a2, a0, -1.0, a0, ALU.mult, ALU.max))
            dve.tensor_scalar(a1, a2, -1.0, float(np.float32(np.pi / 2)), ALU.mult, ALU.add).then_inc(s_ang, 1)
            split("d1", units=range(U))
            add_residual("d0", 0, 1.0)
            split("d1", units=range(U, N_UNITS["d1"]))

            def swiglu(f, layer):

                def hid_chunk(i, step=None):
                    wait(dve, s_rl, HIDDEN.at(f"L{f}_hid", i + 1, layer, step, 2))
                    b = CHUNKS.at(f"L{f}_up0", i, layer, step, 2).slot(2)
                    for t in range(TT):
                        ins = dve.scalar_tensor_tensor(hid2[:, i % 2, t, :], acc[b][:, t, HALFW:COLS], stat[:, t:t + 1],
                                                       silu[:, i % 2, t, :], ALU.mult, ALU.mult)
                    ins.then_inc(acc_free[b], 1)

                def hid_lo(i, step=None):
                    turned_lo(g_hi, g_lo, f"L{f}_hid", i, None, layer, step, 2, 2 * i if step is None else step * 4 + 2 * i)

                split(f"L{f}_up1", layer)
                hid_chunk(0)
                with dve.Fori(0, (UPS - 1) // 2 - 1) as j:
                    for i in (1, 2):
                        split(f"L{f}_up0", layer, j, 2 * U, (i + 1) * U)
                        hid_chunk(i, j)
                        hid_lo(i - 1, j)
                split(f"L{f}_up{UPS - 1}", layer)
                hid_chunk(UPS - 2)
                hid_lo(UPS - 3)
                split(f"L{f}_dn0", layer, units=range(U))
                hid_chunk(UPS - 1)
                hid_lo(UPS - 2)
                hid_lo(UPS - 1)
                split(f"L{f}_dn0", layer, units=range(U, N_UNITS[f"L{f}_dn0"]))

            def vectors_of(layer):
                dve.tensor_copy(vcur[:, :], vec2[:, bass.ds(layer, 1), :].rearrange("p o v -> p (o v)"))
                dve.tensor_copy(scur[:, :], sinks[:, bass.ds(layer, 1), :].rearrange("p o v -> p (o v)"))
                dve.tensor_copy(tcur[:, :], taps2[:, bass.ds(layer, 1), :].rearrange("p o v -> p (o v)")).then_inc(s_cur, 1)
                dve.wait_ge(s_cur, layer + 1)

            add_residual("d1", 1, 1.0)
            with dve.Fori(0, layers) as layer:
                chain.enter(layer)
                vectors_of(layer)
                split("La_up0", layer)
                for k in range(4):
                    turned_lo(x2_hi, x2_lo, "La_norm", k, vcur[:, V2["ffn1"]:V2["ffn1"] + KD], layer)
                row_factors("La_norm", layer)
                swiglu("a", layer)
                rms_boundary(["La_dn0", "La_dn1"], "Lmix", x_hi, x_lo, vcur[:, V2["mix"]:V2["mix"] + KD], "Lca", layer)
                at = STATS["q"]
                dve.tensor_scalar(stat[:, at:at + TT], stat[:, 0:TT], HD ** -0.5, None, ALU.mult).then_inc(s_qscale, 1)
                split("Lcg", layer)
                split("Lq", layer)
                b = chunk_done("Lca", layer)
                evacuated(dve, "Lcg", layer)
                for t in range(TT):
                    ins = dve.scalar_tensor_tensor(u[:, t, :], acc[b][:, t, :], stat[:, t:t + 1], sig[:, t, :],
                                                   ALU.mult, ALU.mult)
                ins.then_inc(acc_free[b], 1)
                split("Lkv", layer)
                split("Lout0", layer)
                evacuated(dve, "Lq", layer)
                evacuated(dve, "Lkv", layer)
                dve.wait_ge(s_rope2, 1)
                rotate_heads(HEADS + KV, rope2).then_inc(s_qk, 1)
                wait(dve, s_qk, Count(2, [(layer, 1)]))
                for i in range(2):
                    ins = dve.tensor_copy(kd[:, :, 0:KV, i, :], qk[:, :, HEADS:HEADS + KV, :])
                ins.then_inc(s_kd, 1)
                turns_read(dve, "Lu", 2, layer)

                def taps(lo, hi):
                    for j in range(lo, hi):
                        for n in range(KC - 1):
                            w = tcur[:, j * KC + n:j * KC + n + 1]
                            if j == 0:
                                ins = dve.tensor_scalar(y[:, n, :], u_t[:, n, 0:S], w,
                                                        vcur[:, V2["conv_b"] + n:V2["conv_b"] + n + 1], ALU.mult, ALU.add)
                            else:
                                ins = dve.scalar_tensor_tensor(y[:, n, :], u_t[:, n, j:j + S], w, y[:, n, :],
                                                               ALU.mult, ALU.add)
                        if j < TAPS2 - 1:
                            link(ins)
                    return ins

                maxima("Latt", 0, True, layer)
                for j in range(2 * PAIRS):
                    if j + 1 < 2 * PAIRS:
                        maxima("Latt", j + 1, True, layer)
                        taps(4 * j, 4 * j + 4)
                    weigh_output("Latt", j, None, True, layer)
                dve.sem_inc(s_mixo, 1)
                taps(28, TAPS2).then_inc(s_y, 1)
                wait(dve, s_rms, Count(1, [(layer, 1)]))
                at = STATS["attn"]
                link(dve.reciprocal(stat[:, at:at + TT], stat[:, at:at + TT]))
                for t in range(TT):
                    ins = dve.tensor_scalar(xs[:, t, 0:CONV], mixo[:, t, :], stat[:, at + t:at + t + 1], None, ALU.mult)
                ins.then_inc(s_xs, 1)
                for k in range(2):
                    turned_lo(x_hi, x_lo, "Lmixed", k, vcur[:, V2["attn"]:V2["attn"] + 4], layer)
                rs = sig[:, 0, 0:S]
                over = [P, KC, S]
                wait(dve, score_done, SCORES.at("Lsum", 1, layer))
                dve.scalar_tensor_tensor(y[:, :, :], score[:, 0:S].unsqueeze(1).to_broadcast(over), -1.0, y[:, :, :],
                                         ALU.mult, ALU.add).then_inc(score_free, 1)
                wait(dve, score_free, SCORES.at("Lsum", 1, layer))
                for i in range(2):
                    wait(dve, score_free, SCORES.at("Lsum", 2 + i, layer))
                    if i:
                        wait(dve, s_silu, Count(1, [(layer, 1)]))
                    link(dve.reciprocal(rs, rs))
                    dve.tensor_tensor(y[:, :, :], y[:, :, :], rs.unsqueeze(1).to_broadcast(over), ALU.mult).then_inc(s_yn, 1)
                dve.wait_ge(s_convhi, layer + 1)
                for n in range(KC):
                    ins = dve.scalar_tensor_tensor(x_lo[:, 4 + n, :], y[:, n, :], vcur[:, V2["conv"] + n:V2["conv"] + n + 1],
                                                   x_hi[:, 4 + n, :].bitcast(F32), ALU.mult, ALU.subtract)
                ins.then_inc(s_convlo, 1)
                rms_boundary(["Lout0", "Lout1"], "Lb_norm", x2_hi, x2_lo, vcur[:, V2["ffn2"]:V2["ffn2"] + KD], "Lb_up0",
                             layer)
                swiglu("b", layer)
                split("Lb_dn1", layer, units=range(3))
                turned_lo(pl_hi, pl_lo, "Lp", 0, None, layer)
                add_residual("Lb_dn0", 0, 0.5, layer)
                split("Lb_dn1", layer, units=range(3, 6))
                for k in (0, 1):
                    turned_lo(x_hi, x_lo, "Lraw", k, None, layer)
                split("Lb_dn1", layer, units=range(6, N_UNITS["Lb_dn1"]))
                split("Lple0", layer)
                add_residual("Lb_dn1", 1, 0.5, layer)
                split("Lple1", layer)
                for k in (2, 3):
                    turned_lo(x_hi, x_lo, "Lraw", k, None, layer)
                split("Lgate0", layer, units=range(2))
                wait(dve, s_ple, Count(4, [(layer, 4)]))
                at, e = STATS["ple"], STATS["e"]
                rooted(dve.tensor_tensor(stat[:, e:e + TT], stat[:, at:at + TT], stat[:, at + TT:at + 2 * TT], ALU.add),
                       "Lple", layer)
                link(dve.reciprocal(stat[:, e:e + TT], stat[:, e:e + TT]))
                for c in range(2):
                    b = chunk_done(f"Lple{c}", layer)
                    for t in range(TT):
                        ins = dve.scalar_tensor_tensor(
                            e_ple[:, t, c * COLS:(c + 1) * COLS], acc[b][:, t, :], stat[:, e + t:e + t + 1],
                            gn[:, bass.ds(layer, 1), c * COLS:(c + 1) * COLS].rearrange("p o n -> p (o n)"),
                            ALU.mult, ALU.mult)
                    ins.then_inc(acc_free[b], 1)
                split("Lgate0", layer, units=range(2, 4))
                split("Lgate1", layer)
                for c in range(2):
                    evacuated(dve, f"Lgate{c}", layer)
                    evacuated(dve, f"Lple{c}", layer)
                    link(dve.tensor_tensor(sig[:, :, :], sig[:, :, :], e_ple[:, :, c * COLS:(c + 1) * COLS], ALU.mult))
                    hc = h[:, :, c * COLS:(c + 1) * COLS]
                    dve.tensor_tensor(hc, hc, sig[:, :, :], ALU.add).then_inc(s_h, 1)
                    wait(dve, s_h, RESIDUAL.at("Lgate", c + 1, layer))
                chain.leave(layers)
            dve.wait_ge(s_rms, layers + 1)
            link(dve.reciprocal(stat[:, 0:TT], stat[:, 0:TT]))
            for t in range(TT):
                dve.scalar_tensor_tensor(xs[:, t, :], h[:, t, :], stat[:, t:t + 1], gn[:, LAYERS, :],
                                         ALU.mult, ALU.mult).then_inc(s_result, 1)

        @block.tensor
        def _(pe):
            def chunk(name, hi, lo, layer=None, step=None, k=0, ready=lambda kt: None, bank=None,
                      units=None):
                c = CHUNKS.at(name, k, layer, step, 2) if bank is None else None
                w, tiles = width(name), tiles_of(name)
                if bank is None and c.const >= 2 and (units is None or 0 in units):
                    wait(pe, acc_free[c.slot(2)], c.lap(2))
                last = N_UNITS[name] * tiles - 1
                for i in range(N_UNITS[name]) if units is None else units:
                    n = UNITS.at(name, i + k * N_UNITS[name], layer, step, 2 * N_UNITS[name])
                    wait(pe, lo_done, n + 1)
                    for q in range(tiles):
                        kt = i * tiles + q
                        ready(kt)
                        wh, wl = w_hi[:, n.slot(SPLIT), q, 0:w], w_lo[:, n.slot(SPLIT), q, 0:w]
                        for t in range(TT if bank is None else 1):
                            if bank is None:
                                dst = acc[c.slot(2)][:, t, 0:w]
                                xh, xl = hi[:, kt, t * P:(t + 1) * P], lo[:, kt, t * P:(t + 1) * P]
                            else:
                                dst, xh, xl = bank, hi[:, kt, :], lo[:, kt, :]
                            pe.matmul(dst, xh, wh, start=kt == 0, stop=False)
                            pe.matmul(dst, xh, wl, start=False, stop=False)
                            mm = pe.matmul(dst, xl, wh, start=False, stop=kt == last)
                    mm.then_inc(unit_used, 1)

            def turned(name, k, pieces, layer=None, step=None, per_step=0):
                n = TURNS.at(name, k, layer, step, per_step)
                if n.const >= 2:
                    wait(pe, turn_free[n.slot(2)], n.lap(2))
                at = 0
                for src in pieces:
                    rows_in, cols_in = src.shape
                    mm = pe.transpose(turn[n.slot(2)][0:cols_in, at:at + rows_in], src, ident[0:rows_in, 0:rows_in])
                    at += rows_in
                mm.then_inc(turn_done, 1)

            def pieces(src, k):
                return [src[:, t, f * P:(f + 1) * P] for f in (2 * k, 2 * k + 1) for t in range(TT)]

            def turn_rows(name, src, count, layer=None):
                for k in range(count):
                    turned(name, k, pieces(src, k), layer)

            def free(plan, sem_free, name, k, layer=None):
                wait(pe, sem_free, plan.at(name, k, layer))

            def scores(name, j, kbase, mask, layer=None):
                t, p = j // PAIRS, j % PAIRS
                w = P * (t + 1)
                free(SCORES, score_free, name, j, layer)
                half = slice(p % 2 * HD, (p % 2 + 1) * HD)
                for i in range(2):
                    pe.matmul(score[:, i * w:(i + 1) * w], q_t[half, p // 2 * 2 + i, t * P:(t + 1) * P],
                              k_t[half, kbase + p // 2, 0:w], start=True, stop=False)
                    mm = pe.matmul(score[:, i * w:(i + 1) * w], ident_r[:, :], masks[:, mask, S - w:S], start=False, stop=True)
                mm.then_inc(score_done, 1)

            def values(name, j, branch, layer=None):
                t, p, b = j // PAIRS, j % PAIRS, j % 2
                wait(pe, score_free, SCORES.at(name, j + 1, layer))
                turned(name, j, [sm[:, b, i, s * P:(s + 1) * P] for i in range(2) for s in range(t + 1)], layer)
                free(OUTS, out_free, name, j, layer)
                turn_read(pe, name, j, layer)
                g = p // 2
                for i in range(2):
                    for s in range(t + 1):
                        mm = pe.matmul(outp[:, i * HD:(i + 1) * HD], p_t[:, i, s, :],
                                       vv[:, s, branch, g * HD:(g + 1) * HD], start=s == 0, stop=s == t)
                mm.then_inc(out_done, 1)

            pe.wait_ge(s_table, 16)
            pe.wait_ge(s_const, 16 * 9)
            pe.transpose(score[:, 0:NV1], raw1[:, :], ident[0:NV1, 0:NV1]).then_inc(score_done, 1)
            pe.wait_ge(s_x, 16 * TT)
            turn_rows("norm1", h, 4)
            chunk("ks", x_hi, x_lo, ready=lambda kt: turn_read(pe, "norm1", kt // 2) if kt % 2 == 0 else None)
            chunk("q", x_hi, x_lo)
            evacuated(pe, "ks")
            turn_rows("z", cd[:, :, :, :, :].rearrange("p t b i d -> p t (b i d)"), 2)
            pe.wait_ge(s_vecs2, 16 * (9 * LAYERS + 1 + TT))
            pe.transpose(outp[:, 0:LAYERS * NV2], raw2[:, :], ident[0:LAYERS * NV2, 0:LAYERS * NV2]).then_inc(out_done, 1)
            rows_t = TAPS2 * KC
            pe.wait_ge(score_free, 1)
            pe.transpose(score[:, 0:rows_t], rawt[:, 0, :], ident[0:rows_t, 0:rows_t]).then_inc(score_done, 1)
            pe.wait_ge(out_free, 1)
            pe.transpose(outp[:, 0:rows_t], rawt[:, 1, :], ident[0:rows_t, 0:rows_t]).then_inc(out_done, 1)
            chunk("kw", x_hi, x_lo)
            chunk("xr0", x_hi, x_lo)
            free(SCORES, score_free, "hid", 0)
            for i, name in enumerate(phi1):
                pe.wait_ge(s_zjlo, i + 1)
                chunk(name, zj_hi[:, i, :, :], zj_lo[:, i, :, :], bank=score[0:ROWS_C, i * PHI:(i + 1) * PHI])
                if i == 0:
                    chunk("xr1", x_hi, x_lo)
            pe.wait_ge(s_qk, 1)
            turn_rows("q", qk[:, :, 0:HEADS, :].rearrange("p t n d -> p t (n d)"), 2)
            pe.wait_ge(s_kd, 1)
            turn_rows("k", kd[:, :, :, :, :].rearrange("p t b i d -> p t (b i d)"), 2)
            wait(pe, score_free, SCORES.at("hid", 1))
            pe.sem_inc(score_done, 1)
            turned("hid", 0, [ghid[:, i * P:(i + 1) * P] for i in range(4)])
            turn_read(pe, "hid", 0)
            free(OUTS, out_free, "kvc", 0)
            for i in range(2):
                for m in range(2):
                    mm = pe.matmul(outp[0:ROWS_C, i * HD:(i + 1) * HD], ghid_t[:, 2 * i + m, :], w_phi2[:, i, m, :],
                                   start=m == 0, stop=m == 1)
            mm.then_inc(out_done, 1)
            for c in range(2):
                evacuated(pe, f"xr{c}")
            turn_rows("xr", gy, 4)
            chunk("yr0", x_hi, x_lo)
            pe.wait_ge(s_kcd, 1)
            turned("kc", 0, [kcd[:, :, :].rearrange("p i d -> p (i d)")])
            free(OUTS, out_free, "vb", 0)
            pe.matmul(outp[0:HEADS * NCMP, 0:HD], ct[0:ROWS_C, C_SEL:C_SEL + HEADS * NCMP], kvc[:, 1, :],
                      start=True, stop=True).then_inc(out_done, 1)
            turn_read(pe, "kc", 0)
            turns_read(pe, "q", 2)
            for t in range(TT):
                for p in range(PAIRS):
                    at = t * HEADS * NCMP + p * 2 * NCMP
                    mm = pe.matmul(score[:, at:at + 2 * NCMP], q_t[:, p, t * P:(t + 1) * P],
                                   kb[:, p // KV, :, :].rearrange("p i n -> p (i n)"), start=True, stop=True)
            mm.then_inc(score_done, 1)
            chunk("yr1", x_hi, x_lo)
            pe.wait_ge(s_pce, 1)
            turned("pc", 0, [pc[:, t, :, :].rearrange("p h n -> p (h n)") for t in range(TT)])
            turn_read(pe, "pc", 0)
            for t in range(TT):
                free(OUTS, out_free, "cmp", t)
                pe.matmul(outp[:, :], pc_t[:, t * P:(t + 1) * P], vb[:, :, :].rearrange("p h d -> p (h d)"),
                          start=True, stop=True).then_inc(out_done, 1)
            pe.wait_ge(s_xc, 1)
            pe.wait_ge(s_small, 16 * 17)
            for k in range(4):
                for i, (plan, done, sem_free, bank) in enumerate([(SCORES, score_done, score_free, score),
                                                                  (OUTS, out_done, out_free, outp)]):
                    free(plan, sem_free, "gates", k)
                    for m in range(2):
                        f = 2 * k + m
                        mm = pe.matmul(bank[:, m * S:(m + 1) * S], w_gates[:, i, f, :], xc[:, f, :], start=True, stop=True)
                    mm.then_inc(done, 1)
            pe.wait_ge(s_masks, 1)
            turns_read(pe, "k", 2)

            def branch_of(name):
                return 0 if name == "slc" else 1

            scores("slc", 0, 0, 0)
            for i, (name, j) in enumerate(JOBS):
                if i + 1 < len(JOBS):
                    following, k = JOBS[i + 1]
                    scores(following, k, KV * branch_of(following), 0)
                chunk(BESIDE[i][0], x_hi, x_lo, units=[BESIDE[i][1]])
                values(name, j, branch_of(name))
                if (name, j) == ("slc", 2 * PAIRS - 1):
                    for c in range(2):
                        evacuated(pe, f"yr{c}")
                    turn_rows("yr", gy, 4)
            pe.wait_ge(s_mixo, 1)
            turn_rows("nsa", mixo, 2)
            turns_read(pe, "nsa", 2)
            pe.wait_ge(s_lrulo, 4)
            for c in range(2):
                chunk(f"nsa{c}", nsa_hi, nsa_lo)
                chunk(f"lru{c}", lru_hi, lru_lo)
            pe.wait_ge(s_merged, 2)
            turn_rows("merged", merged, 4)
            turns_read(pe, "merged", 4)
            def first_half(name, residual, last, layer=None):
                def ready(kt):
                    if kt == UNIT_K * (3 if N_UNITS[last] > U else 2):
                        wait(pe, s_h, RESIDUAL.at(residual, 1, layer))
                        for k in (0, 1):
                            turned(name, k, pieces(h, k), layer)
                return ready

            def second_half(name, residual, layer=None):
                def ready(kt):
                    if kt == UNIT_K:
                        wait(pe, s_h, RESIDUAL.at(residual, 2, layer))
                        for k in (2, 3):
                            turned(name, k, pieces(h, k), layer)
                    if kt == 0:
                        turns_read(pe, name, 2, layer)
                    elif kt >= KD // 2 and kt % 2 == 0:
                        turn_read(pe, name, kt // 2, layer)
                return ready

            chunk("o0", x_hi, x_lo)
            chunk("o1", x_hi, x_lo, ready=first_half("norm2", "o", "o1"))

            def ff_turns(i, step=None):
                n = CHUNKS.at("f0", i, None, step, 2)
                wait(pe, acc_free[n.slot(2)], n.lap(2) + 1)
                for m in range(2):
                    turned("ff", 2 * i + m, pieces(hid1[:, i % 2, :, :], m), None, step, 4)

            chunk("f0", x2_hi, x2_lo, ready=second_half("norm2", "o"))
            with pe.Fori(0, NF // 2 - 1) as j:
                for i in (1, 2):
                    chunk("f0", x2_hi, x2_lo, None, j, i)
                    ff_turns(i - 1, j)
            chunk(f"f{NF - 1}", x2_hi, x2_lo)
            ff_turns(NF - 2)
            ff_turns(NF - 1)
            turns_read(pe, "ff", 2 * NF)
            for c in range(2):
                chunk(f"d{c}", f_hi, f_lo)

            def swiglu(f, layer, first=lambda kt: None, last=lambda kt: None):

                def hid_turns(i, step=None):
                    n = CHUNKS.at(f"L{f}_up0", i, layer, step, 2)
                    wait(pe, acc_free[n.slot(2)], n.lap(2) + 1)
                    turned(f"L{f}_hid", i, pieces(hid2[:, i % 2, :, :], 0), layer, step, 2)

                chunk(f"L{f}_up0", x2_hi, x2_lo, layer, ready=first)
                with pe.Fori(0, (UPS - 1) // 2 - 1) as j:
                    for i in (1, 2):
                        chunk(f"L{f}_up0", x2_hi, x2_lo, layer, j, i)
                        hid_turns(i - 1, j)
                chunk(f"L{f}_up{UPS - 2}", x2_hi, x2_lo, layer)
                hid_turns(UPS - 3)
                chunk(f"L{f}_up{UPS - 1}", x2_hi, x2_lo, layer)
                hid_turns(UPS - 2)
                hid_turns(UPS - 1)
                turns_read(pe, f"L{f}_hid", UPS, layer)
                chunk(f"L{f}_dn0", g_hi, g_lo, layer)
                chunk(f"L{f}_dn1", g_hi, g_lo, layer, ready=last)

            with pe.Fori(0, layers) as layer:
                wait(pe, s_h, RESIDUAL.at("La_dn", 0, layer))
                turn_rows("La_norm", h, 4, layer)
                turns_read(pe, "La_norm", 4, layer)
                swiglu("a", layer, last=first_half("Lmix", "La_dn", "La_dn1", layer))
                chunk("Lca", x_hi, x_lo, layer, ready=second_half("Lmix", "La_dn", layer))
                chunk("Lcg", x_hi, x_lo, layer)
                chunk("Lq", x_hi, x_lo, layer)
                evacuated(pe, "Lca", layer)
                turn_rows("Lu", u, 2, layer)
                chunk("Lkv", x_hi, x_lo, layer)
                wait(pe, s_qk, Count(2, [(layer, 1)]))
                turn_rows("Lq", qk[:, :, 0:HEADS, :].rearrange("p t n d -> p t (n d)"), 2, layer)
                wait(pe, s_kd, Count(2, [(layer, 1)]))
                turned("Lk", 0, pieces(kd[:, :, 0:KV, :, :].rearrange("p t b i d -> p t (b i d)"), 0), layer)
                turns_read(pe, "Lq", 2, layer)
                turn_read(pe, "Lk", 0, layer)
                scores("Latt", 0, 0, 1, layer)
                for j in range(2 * PAIRS):
                    if j + 1 < 2 * PAIRS:
                        scores("Latt", j + 1, 0, 1, layer)
                    values("Latt", j, 0, layer)
                wait(pe, s_xs, Count(1, [(layer, 1)]))
                turn_rows("Lmixed", xs, 2, layer)
                turns_read(pe, "Lmixed", 2, layer)
                pe.wait_ge(s_zero, 3)
                wait(pe, s_y, Count(1, [(layer, 1)]))
                wait(pe, s_ypool, Count(1, [(layer, 1)]))
                for i in range(3):
                    free(SCORES, score_free, "Lsum", i, layer)
                    if i:
                        wait(pe, s_ysq, Count(i, [(layer, 2)]))
                    for n in range(KC):
                        mm = pe.matmul(score[:, 0:S], mean, (ysq if i else y)[:, n, :], start=n == 0, stop=n == KC - 1)
                    mm.then_inc(score_done, 1)
                wait(pe, s_convlo, Count(1, [(layer, 1)]))
                chunk("Lout0", x_hi, x_lo, layer)
                chunk("Lout1", x_hi, x_lo, layer, ready=first_half("Lb_norm", "Lout", "Lout1", layer))

                def embedding_in(kt):
                    if kt == 0:
                        wait(pe, s_pcur, Count(1, [(layer, 1)]), 16)
                        turned("Lp", 0, pieces(pcur, 0), layer)
                    half(kt)

                half = first_half("Lraw", "Lb_dn", "Lb_dn1", layer)
                swiglu("b", layer, second_half("Lb_norm", "Lout", layer), embedding_in)
                turn_read(pe, "Lp", 0, layer)
                chunk("Lple0", pl_hi, pl_lo, layer)
                wait(pe, s_h, RESIDUAL.at("Lb_dn", 2, layer))
                for k in (2, 3):
                    turned("Lraw", k, pieces(h, k), layer)
                chunk("Lple1", pl_hi, pl_lo, layer)
                turns_read(pe, "Lraw", 4, layer)
                for c in range(2):
                    chunk(f"Lgate{c}", x_hi, x_lo, layer)


def kernel(**inputs):
    from concourse import bacc
    from concourse.bass_utils import run_bass_kernel_spmd

    nc = bacc.Bacc("TRN2", target_bir_lowering=False, num_devices=1)
    arrays, aps = {}, {}
    for name, value in inputs.items():
        if name.endswith("w_gate_up_2"):
            value = np.asarray(value).reshape(LAYERS, D, 2, UPS, HALFW).transpose(0, 1, 3, 2, 4).reshape(value.shape)
        arrays[f"in_{name}"] = np.ascontiguousarray(value)
    arrays["in_tables"] = constants()
    for name, value in arrays.items():
        aps[name[3:]] = nc.dram_tensor(name, value.shape, mybir.dt.from_np(value.dtype), kind="ExternalInput").ap()
    out = nc.dram_tensor("out", (1, S, D), F32, kind="ExternalOutput").ap()
    build(nc, aps, aps.pop("tables"), out)
    return run_bass_kernel_spmd(nc, [arrays], core_ids=[0]).results[0]["out"]
```

```python
from contextlib import ExitStack

import numpy as np

import concourse.bass as bass
from concourse import mybir

F32 = mybir.dt.float32
F32R = mybir.dt.float32r
I32 = mybir.dt.int32
ALU = mybir.AluOpType
ACT = mybir.ActivationFunctionType
AX_X = mybir.AxisListType.X

P = 128
S = 256
TT = S // P
D = 1024
KD = D // P
COLS = 512
UNIT_K = 2
EPS = 1e-6
NEG = -1e30
HEADS, HD, KV = 8, 64, 2
PAIRS = HEADS // 2
ROT = HD // 4
HALF = ROT // 2
THETA = 500000.0
CMP_BLOCK, CMP_STRIDE = 32, 16
NCMP = (S - CMP_BLOCK) // CMP_STRIDE + 1
ROWS_C = KV * NCMP
KPHI = CMP_BLOCK * HD // P
PHI = 256
TAPS1 = 4
FF1 = 4096
KF1 = FF1 // P
OFF_KV, OFF_KW, OFF_XR, OFF_YR, OFF_GM = 512, 1024, 1304, 2328, 3352
W_KW = OFF_XR - OFF_KW
LAYERS = 2
FF2 = 2816
KF2 = FF2 // P
TAPS2 = 31
CONV = 512
KC = CONV // P
WINDOW = 128
PLE = 256
KPLE = PLE // P
HALFW = COLS // 2
UPS = FF2 // HALFW

STAGE, SPLIT = 8, 4

V1 = dict(norm1=0, norm2=8, conv_w=16, conv_b=48, ba=56, bx=64, lam=72, pos_k=80, pos_v=96)
NV1 = 112
V2 = dict(ffn1=0, mix=8, ffn2=16, attn=24, conv=28, conv_b=32, ln_g=36, ln_b=40)
NV2 = 44

STATS = dict(rstd=0, attn=TT, ple=2 * TT, e=4 * TT, half=5 * TT, q=7 * TT, conv=8 * TT)
C_STATS = 9 * TT

C_ID, C_M1, C_M2, C_ROPE, C_ROPEC, C_CMASK, C_ROWOK, C_INV, C_SEL, C_SELM, C_EPS, C_END = np.cumsum(
    [0, P, S, S, TT * 2 * ROT, 2 * ROT, TT * NCMP, TT, HALF, HEADS * NCMP, HEADS, 1]).tolist()


class Count:

    def __init__(self, const, terms=()):
        self.const, self.terms = const, [t for t in terms if t[0] is not None and t[1]]

    def __add__(self, n):
        return Count(self.const + n, self.terms)

    def slot(self, n):
        assert all(c % n == 0 for _, c in self.terms)
        return self.const % n

    def lap(self, n):
        assert all(c % n == 0 for _, c in self.terms)
        return Count(self.const // n, [(r, c // n) for r, c in self.terms])

    def value(self, times=1):
        v = self.const * times
        for r, c in self.terms:
            v = r * (c * times) + v
        return v


def wait(eng, sem, count, times=1):
    v = count.value(times)
    if not isinstance(v, int) or v > 0:
        eng.wait_ge(sem, v)


class Plan:

    def __init__(self, before, layer):
        self.start, n = {}, 0
        for name, k in before:
            self.start[name] = (n, False)
            n += k
        self.per_layer = 0
        for name, k in layer:
            self.start[name] = (n + self.per_layer, True)
            self.per_layer += k

    def at(self, name, k=0, layer=None, step=None, per_step=0):
        n, looped = self.start[name]
        assert looped == (layer is not None), name
        return Count(n + k, [(layer, self.per_layer), (step, per_step)])


def units_of(k_tiles, per=UNIT_K):
    return k_tiles // per


U = units_of(KD)
NF = FF1 // COLS
_U1 = ([(n, U) for n in ("ks", "q", "kw", "xr0")] + [("phi_k", units_of(KPHI)), ("xr1", U), ("phi_v", units_of(KPHI))]
       + [(n, U) for n in ("yr0", "yr1", "gm0", "gm1", "gm2", "gm3")]
       + [("lru0", U), ("nsa0", units_of(4)), ("lru1", U), ("nsa1", units_of(4)), ("o0", U), ("o1", U)]
       + [(f"f{i}", U) for i in range(NF)] + [("d0", units_of(KF1)), ("d1", units_of(KF1))])
_U2 = ([(f"a_up{i}", U) for i in range(UPS)] + [("a_dn0", units_of(KF2)), ("a_dn1", units_of(KF2))]
       + [(n, U) for n in ("cg", "ca", "kv", "q")]
       + [(n, units_of(4)) for n in ("out_a0", "out_a1", "out_c0", "out_c1")]
       + [(f"b_up{i}", U) for i in range(UPS)] + [("b_dn0", units_of(KF2)), ("b_dn1", units_of(KF2))]
       + [("ple0", units_of(KPLE, 1)), ("ple1", units_of(KPLE, 1)), ("gate0", U), ("gate1", U)])
_U2 = [("L" + n, k) for n, k in _U2]
N_UNITS = dict(_U1 + _U2)
UNITS = Plan(_U1, _U2)
CHUNKS = Plan([(n, 1) for n, _ in _U1 if not n.startswith("phi")], [(n, 1) for n, _ in _U2])
YR_AT = 3
TURNS = Plan([("norm1", 4), ("z", 2), ("q", 2), ("k", 2), ("hid", 1), ("xr", 4), ("kc", 1), ("pc", 1),
              ("slc", 8), ("win", YR_AT), ("yr", 4), ("win_on", 8 - YR_AT), ("nsa", 2), ("merged", 4), ("norm2", 4), ("ff", 2 * NF)],
             [("La_norm", 4), ("La_hid", UPS), ("Lmix", 4), ("Lu", 2), ("Lk", 1), ("Lq", 2), ("Latt", 8),
              ("Lmixed", 2), ("Lb_norm", 4), ("Lb_hid", UPS), ("Lp", 1), ("Lraw", 4)])
HI_TURNS = Plan([("norm1", 4), ("nsa", 2), ("merged", 4), ("norm2", 4), ("ff", 2 * NF)],
                [("La_norm", 4), ("La_hid", UPS), ("Lmix", 4), ("Lmixed", 2), ("Lb_norm", 4), ("Lb_hid", UPS),
                 ("Lp", 1), ("Lraw", 4)])
RSTD = Plan([("norm1", 1), ("norm2", 1)], [("La_norm", 1), ("Lmix", 1), ("Lb_norm", 1)])
ROOTS = Plan([("norm1", 1), ("qk", 1), ("kc", 1), ("lru", 1), ("norm2", 1)],
             [("La_norm", 1), ("Lmix", 1), ("Lb_norm", 1), ("Lple", 1)])
HIDDEN = Plan([("ff", NF)], [("La_hid", UPS), ("Lb_hid", UPS)])
RESIDUAL = Plan([("o", 2), ("d", 2)], [("La_dn", 2), ("Lout_a", 2), ("Lout_c", 2), ("Lb_dn", 2), ("Lgate", 2)])
SCORES = Plan([("vec", 2), ("hid", 1), ("cmp", 1), ("gates", 4), ("slc", 8), ("win", 8)],
              [("Latt", 8), ("Lsum", 3)])
OUTS = Plan([("vec", 2), ("kvc", 1), ("vb", 1), ("gates", 4), ("cmp", TT), ("slc", 8), ("win", 8)],
            [("Latt", 8)])
HEAD_PAIRS = Plan([("slc", 8), ("win", 8)], [("Latt", 8)])

JOBS = [(name, j) for name in ("slc", "win") for j in range(2 * PAIRS)]
BESIDE = [(name, i) for name in ("gm0", "gm1", "gm2", "gm3", "lru0") for i in range(U)]


def turns_of(name, j):
    return ("win_on", j - YR_AT) if name == "win" and j >= YR_AT else (name, j)


EARLY_ACT, BESIDE_ACT = 6, 3
EARLY_DVE, BESIDE_DVE = 7, 2

DVE_LINKS = 72


class Chain:

    def __init__(self, eng, sem, per_layer):
        self.eng, self.sem, self.per_layer = eng, sem, per_layer
        self.n, self.layer, self.first = 0, None, 0

    def enter(self, layer):
        self.layer, self.first = layer, self.n

    def leave(self, layers):
        assert self.n - self.first == self.per_layer, (self.n - self.first, self.per_layer)
        self.n, self.layer = self.first + layers * self.per_layer, None

    def link(self, ins):
        self.n += 1
        ins.then_inc(self.sem, 1)
        wait(self.eng, self.sem, Count(self.n, [(self.layer, self.per_layer)]))


def heads_of(x, p):
    return x.rearrange("q (g a i d) -> q g i a d", g=KV, a=2, i=2)[:, p // 2, p % 2, :, :]


def constants():
    c = np.zeros((P, C_END), np.float32)
    i, j = np.arange(P)[:, None], np.arange(P)[None, :]
    c[:, C_ID:C_ID + P] = i == j
    causal = np.where(j <= i, 0.0, NEG)
    c[:, C_M1 + P:C_M1 + S] = causal
    c[:, C_M2:C_M2 + P] = np.where(i + P - j < WINDOW, 0.0, NEG)
    c[:, C_M2 + P:C_M2 + S] = causal
    inv = (THETA ** (-np.arange(HALF, dtype=np.float64) / HALF)).astype(np.float32)

    def rope(pos):
        ang = (pos.astype(np.float32)[:, None] * inv[None, :]).astype(np.float64)
        return np.concatenate([np.cos(ang), np.cos(ang), -np.sin(ang), np.sin(ang)], 1)

    ends = np.arange(NCMP) * CMP_STRIDE + CMP_BLOCK - 1
    for t in range(TT):
        tok = t * P + np.arange(P)
        c[:, C_ROPE + t * 2 * ROT:C_ROPE + (t + 1) * 2 * ROT] = rope(tok)
        c[:, C_CMASK + t * NCMP:C_CMASK + (t + 1) * NCMP] = np.where(ends[None, :] <= tok[:, None], 0.0, NEG)
        c[:, C_ROWOK + t] = tok >= CMP_BLOCK - 1
    c[:ROWS_C, C_ROPEC:C_ROPEC + 2 * ROT] = np.tile(rope(ends), (KV, 1))
    c[:, C_INV:C_INV + HALF] = inv
    for head in range(HEADS):
        for n in range(NCMP):
            c[(head // (HEADS // KV)) * NCMP + n, C_SEL + head * NCMP + n] = 1.0
            c[head * NCMP + n, C_SELM + head] = 1.0
    c[:, C_EPS] = EPS
    return c


def build(nc, a, consts, out, layers=LAYERS):
    ctx = ExitStack()
    with ctx:
        def sb(name, shape, dt=F32, stack=ctx):
            return stack.enter_context(nc.sbuf_tensor(name, shape, dt))

        def sem(name):
            return ctx.enter_context(nc.semaphore(name))

        def overlay(stack, *groups):
            made, free, least = [], nc.sbuf_bytes_remaining, nc.sbuf_bytes_remaining
            for group in groups:
                with ExitStack() as own:
                    made += [sb(*spec, stack=own) for spec in group]
                    least = min(least, nc.sbuf_bytes_remaining)
            sb(f"room_{groups[0][0][0]}", [P, -(-(free - least) // 4)], stack=stack)
            return made

        stage = sb("stage", [P, STAGE, UNIT_K, COLS])
        w_hi = sb("w_hi", [P, SPLIT, UNIT_K, COLS], F32R)
        w_lo = sb("w_lo", [P, SPLIT, UNIT_K, COLS], F32R)
        x_hi = sb("x_hi", [P, KD, S], F32R)
        x_lo = sb("x_lo", [P, KD, S], F32R)
        h = sb("h", [P, TT, D])
        xs = sb("xs", [P, TT, D])
        ct = sb("ct", [P, C_END])
        stat = sb("stat", [P, C_STATS])
        vec1 = sb("vec1", [P, NV1])
        vec2 = sb("vec2", [P, LAYERS, NV2])
        taps2 = sb("taps2", [P, LAYERS, TAPS2 * KC])
        sinks = sb("sinks", [P, LAYERS, HEADS])
        vcur = sb("vcur", [P, NV2])
        tcur = sb("tcur", [P, TAPS2 * KC])
        scur = sb("scur", [P, HEADS])
        pos_i = sb("pos_i", [P, TT], I32)
        pos_f = sb("pos_f", [P, TT])
        ang = sb("ang", [P, 3, TT, HALF])
        rope2 = sb("rope2", [P, TT, 2 * ROT])
        mx = sb("mx", [P, 2, 2])
        negm = sb("negm", [P, 2, 2])
        den = sb("den", [P, 2, 2])
        esink = sb("esink", [P, 2, 2])
        coef = sb("coef", [P, 2])
        ident, eps = ct[:, C_ID:C_ID + P], ct[:, C_EPS:C_EPS + 1]

        masks = sb("masks", [P, 2, S], F32R)
        ident_r = sb("ident_r", [P, P], F32R)
        x_rt, raw1, raw2, rawt, gate, x2_hi, x2_lo = overlay(
            ctx, [("x_rt", [P, KD, TAPS1 - 1 + S])],
            [("raw1", [NV1, P]), ("raw2", [LAYERS * NV2, P]), ("rawt", [TAPS2 * KC, LAYERS, P])],
            [("gate", [P, TT, 2 * D])], [("x2_hi", [P, KD, S], F32R), ("x2_lo", [P, KD, S], F32R)])

        attn, mixer, mlp, lay = ExitStack(), ExitStack(), ExitStack(), ExitStack()
        qk = sb("qk", [P, TT, 12, HD], stack=attn)
        vv = sb("vv", [P, TT, 2, P], stack=attn)
        kd = sb("kd", [P, TT, 4, 2, HD], stack=attn)
        q_t = sb("q_t", [P, PAIRS, S], stack=attn)
        k_t = sb("k_t", [P, 4, S], stack=attn)
        sm = sb("sm", [P, 2, 2, S], stack=attn)
        p_t = sb("p_t", [P, 2, TT, P], stack=attn)
        ropet = sb("ropet", [P, TT, 12, ROT], stack=attn)
        tmpo = sb("tmpo", [P, 2, HD], stack=attn)
        mixo, z = overlay(attn, [("mixo", [P, TT, 512])], [("z", [P, 4, S])])
        gy = sb("gy", [P, TT, D], stack=mixer)
        lru_r, lru_i, lru_hi, lru_lo, zj_hi, zj_lo = overlay(
            mixer, [("lru_r", [P, KD, S]), ("lru_i", [P, KD, S])],
            [("lru_hi", [P, KD, S], F32R), ("lru_lo", [P, KD, S], F32R)],
            [("zj_hi", [P, 2, KPHI, ROWS_C], F32R), ("zj_lo", [P, 2, KPHI, ROWS_C], F32R)])
        w_gates, nsa_hi, nsa_lo = overlay(
            mixer, [("w_gates", [P, 2, KD, P])], [("nsa_hi", [P, 4, S], F32R), ("nsa_lo", [P, 4, S], F32R)])
        cd, xc = overlay(mixer, [("cd", [P, TT, 4, 2, HD])], [("xc", [P, KD, S])])
        zj, pc, pc_t = overlay(mixer, [("zj", [P, KPHI, KV, NCMP])],
                               [("pc", [P, TT, HEADS, NCMP]), ("pc_t", [HEADS * NCMP, S])])
        gsig = sb("gsig", [P, TT, 3, HEADS], stack=mixer)
        softp = sb("softp", [P, 9, KD], stack=mixer)
        qk_ss = sb("qk_ss", [P, TT * 12], stack=mixer)
        w_phi2 = sb("w_phi2", [P, 2, 2, HD], stack=mixer)
        ghid = sb("ghid", [ROWS_C, 2 * PHI], stack=mixer)
        ghid_t = sb("ghid_t", [P, 4, ROWS_C], stack=mixer)
        kvc = sb("kvc", [ROWS_C, 2, HD], stack=mixer)
        kcs = sb("kcs", [ROWS_C, HD], stack=mixer)
        kcd = sb("kcd", [ROWS_C, 2, HD], stack=mixer)
        kcr = sb("kcr", [ROWS_C, ROT + 1], stack=mixer)
        knw = sb("knw", [P, HD], stack=mixer)
        qkw = sb("qkw", [P, 12, HD], stack=mixer)
        kb = sb("kb", [P, KV, 2, NCMP], stack=mixer)
        vb = sb("vb", [HEADS * NCMP, HEADS, HD], stack=mixer)
        pcs = sb("pcs", [P, 2, TT, HEADS], stack=mixer)
        mixer.close()
        u = sb("u", [P, TT, CONV], stack=attn)
        prod = u[:, :, :].rearrange("p t (n s) -> p t n s", s=S)
        y = sb("y", [P, KC, S], stack=attn)
        ysq = sb("ysq", [P, KC, S], stack=attn)
        attn.close()
        f_hi = sb("f_hi", [P, KF1, S], F32R, stack=mlp)
        f_lo = sb("f_lo", [P, KF1, S], F32R, stack=mlp)
        hid1 = sb("hid1", [P, 2, TT, COLS], stack=mlp)
        relu = sb("relu", [P, 2, TT, COLS], stack=mlp)
        mlp.close()
        g_hi = sb("g_hi", [P, KF2, S], F32R, stack=lay)
        g_lo = sb("g_lo", [P, KF2, S], F32R, stack=lay)
        hid2 = sb("hid2", [P, 2, TT, HALFW], stack=lay)
        silu = sb("silu", [P, 2, TT, HALFW], stack=lay)
        sig = sb("sig", [P, TT, COLS], stack=lay)
        u_t = sb("u_t", [P, KC, TAPS2 - 1 + S], stack=lay)
        pcur = sb("pcur", [P, TT, PLE], stack=lay)
        pl_hi = sb("pl_hi", [P, KPLE, S], F32R, stack=lay)
        pl_lo = sb("pl_lo", [P, KPLE, S], F32R, stack=lay)
        e_ple = sb("e_ple", [P, TT, D], stack=lay)
        gn = sb("gn", [P, LAYERS + 1, D], stack=lay)
        mean = masks[:, 0, 0:P].bitcast(F32)
        lay.close()
        merged, sq, th = xs, xs[:, :, 0:12 * HD], x_rt[:, :, 0:S]
        den2 = xs[:, :, :].rearrange("p t (f s) -> p (t f) s", s=S)

        acc = [ctx.enter_context(nc.psum_tensor(f"acc{i}", [P, TT, COLS], F32)) for i in range(2)]
        turn = [ctx.enter_context(nc.psum_tensor(f"turn{i}", [P, 512], F32)) for i in range(2)]
        score = ctx.enter_context(nc.psum_tensor("score", [P, 512], F32))
        outp = ctx.enter_context(nc.psum_tensor("outp", [P, 512], F32))

        s_x = sem("s_x")
        s_table = sem("s_table")
        s_const = sem("s_const")
        s_vecs2 = sem("s_vecs2")
        s_small = sem("s_small")
        s_late = sem("s_late")
        s_zero = sem("s_zero")
        s_pcur = sem("s_pcur")
        landed = [sem(f"landed{i}") for i in range(STAGE)]
        hi_done = sem("hi_done")
        lo_done = sem("lo_done")
        unit_used = sem("unit_used")
        acc_free = [sem(f"acc_free{i}") for i in range(2)]
        turn_done = sem("turn_done")
        turn_hi = sem("turn_hi")
        turn_free = [sem(f"turn_free{i}") for i in range(2)]
        score_done, score_free = sem("score_done"), sem("score_free")
        out_done, out_free = sem("out_done"), sem("out_free")
        dve_chain = sem("dve_chain")
        s_squares = sem("s_squares")
        s_rstd = sem("s_rstd")
        s_sqattn = sem("s_sqattn")
        s_rattn = sem("s_rattn")
        s_qscale = sem("s_qscale")
        s_sums, s_roots = sem("s_sums"), sem("s_roots")
        s_h = sem("s_h")
        s_vec = sem("s_vec")
        s_lam = sem("s_lam")
        s_elam = sem("s_elam")
        s_soft = sem("s_soft")
        s_xc = sem("s_xc")
        s_ab = sem("s_ab")
        s_gated = sem("s_gated")
        s_scan = sem("s_scan")
        s_olru = sem("s_olru")
        s_lruhi = sem("s_lruhi")
        s_lrulo = sem("s_lrulo")
        s_qk = sem("s_qk")
        s_kd = sem("s_kd")
        s_zj = sem("s_zj")
        s_zjhi = sem("s_zjhi")
        s_zjlo = sem("s_zjlo")
        s_kcd = sem("s_kcd")
        s_pcm = sem("s_pcm")
        s_pce = sem("s_pce")
        s_masks = sem("s_masks")
        s_negm = sem("s_negm")
        s_mixo = sem("s_mixo")
        s_merged = sem("s_merged")
        s_rl = sem("s_rl")
        s_hid = sem("s_hid")
        s_ang = sem("s_ang")
        s_rope2 = sem("s_rope2")
        s_cur = sem("s_cur")
        s_y = sem("s_y")
        s_prod = sem("s_prod")
        s_ypool = sem("s_ypool")
        s_ysq = sem("s_ysq")
        s_yn = sem("s_yn")
        s_silu = sem("s_silu")
        s_convhi = sem("s_convhi")
        s_convlo = sem("s_convlo")
        s_ple = sem("s_ple")
        s_result = sem("s_result")
        s_out = sem("s_out")

        def rows(w):
            return w.rearrange("(k p) n -> p k n", p=P)

        def layer_rows(w):
            return w.rearrange("l (k p) n -> l p k n", p=P)

        win1 = rows(a["w_in"][0])
        FIRST_COL = {"xr0": OFF_XR, "xr1": OFF_XR + COLS, "q": 0, "ks": OFF_KV, "kw": OFF_KW, "yr0": OFF_YR,
                     "yr1": OFF_YR + COLS, **{f"gm{i}": OFF_GM + i * COLS for i in range(4)}}
        view1 = {"nsa": rows(a["w_nsa_up"][0]), "lru": rows(a["w_lru_up"][0]), "o": rows(a["w_o"][0]),
                 "d": rows(a["w_ff2"][0])}
        phi1 = {"phi_k": rows(a["phi_k_w1"][0]), "phi_v": rows(a["phi_v_w1"][0])}
        ff1 = rows(a["w_ff1"][0])
        win2, wout2 = layer_rows(a["w_in_2"]), layer_rows(a["w_out_2"])
        win2_flat = a["w_in_2"].rearrange("l (k p) n -> p (l k) n", p=P)
        up2 = {"a": layer_rows(a["ffn1_w_gate_up_2"]), "b": layer_rows(a["ffn2_w_gate_up_2"])}
        dn2 = {"a": layer_rows(a["ffn1_w_down_2"]), "b": layer_rows(a["ffn2_w_down_2"])}
        wple, wpleg = layer_rows(a["w_ple_2"]), layer_rows(a["w_ple_gate_2"])
        L_COL = {"Lkv": HEADS * HD, "Lca": HEADS * HD + 2 * KV * HD,
                 "Lcg": HEADS * HD + 2 * KV * HD + CONV}

        def width(name):
            return W_KW if name == "kw" else 2 * KV * HD if name == "Lkv" else PHI if name in phi1 else COLS

        def tiles_of(name):
            return 1 if name.startswith("Lple") else UNIT_K

        def evacuated(eng, name, layer=None):
            n = CHUNKS.at(name, 0, layer)
            wait(eng, acc_free[n.slot(2)], n.lap(2) + 1)

        def turn_read(eng, name, k, layer=None):
            n = TURNS.at(name, k, layer)
            wait(eng, turn_free[n.slot(2)], n.lap(2) + 1)

        def turns_read(eng, name, count, layer=None):
            for k in range(max(0, count - 2), count):
                turn_read(eng, name, k, layer)

        block = ctx.enter_context(nc.Block())

        @block.sync
        def _(sp):
            def load(name, source, layer=None, step=None, per_step=0, k=0):
                for i in range(N_UNITS[name]):
                    n = UNITS.at(name, i + k, layer, step, per_step)
                    t = tiles_of(name)
                    src = source(i * t, t)
                    if n.const >= STAGE:
                        wait(sp, lo_done, n + (1 - STAGE))
                    sp.dma_start(stage[:, n.slot(STAGE), 0:t, 0:width(name)],
                                 src).then_inc(landed[n.slot(STAGE)], 16)

            def plain(view, c0, w=COLS):
                return lambda k0, t: view[:, k0:k0 + t, c0:c0 + w]

            def of_layer(view, layer, c0, w=COLS, k_first=0):
                return lambda k0, t: view[bass.ds(layer, 1), :, k_first + k0:k_first + k0 + t, c0:c0 + w].rearrange(
                    "o p k n -> (o p) k n")

            sp.dma_start(ct[:, :], consts).then_inc(s_table, 16)
            for t in range(TT):
                sp.dma_start(h[:, t, :], a["x"][0, t * P:(t + 1) * P, :]).then_inc(s_x, 16)
            sp.wait_ge(s_table, 16)
            sp.wait_ge(s_x, 16 * TT)
            for name in ["ks", "q", "kw", "xr0", "phi_k", "xr1", "phi_v", "yr0", "yr1", "gm0", "gm1", "gm2", "gm3"]:
                load(name, plain(phi1[name], 0, PHI) if name in phi1 else plain(win1, FIRST_COL[name], width(name)))
            for name in ["lru0", "nsa0", "lru1", "nsa1", "o0", "o1"]:
                load(name, plain(view1[name[:-1]], int(name[-1]) * COLS))
            with sp.Fori(0, NF // 2) as j:
                for i in range(2):
                    load("f0", lambda k0, t: ff1[:, k0:k0 + t, bass.ds(j * (2 * COLS) + i * COLS, COLS)],
                         step=j, per_step=2 * U, k=i * U)
            for name in ["d0", "d1"]:
                load(name, plain(view1["d"], int(name[-1]) * COLS))

            def swiglu_loads(f, layer):
                load(f"L{f}_up0", of_layer(up2[f], layer, 0), layer)
                with sp.Fori(0, (UPS - 1) // 2) as j:
                    for i in range(2):
                        load(f"L{f}_up1", lambda k0, t: up2[f][bass.ds(layer, 1), :, k0:k0 + t,
                             bass.ds(j * (2 * COLS) + (1 + i) * COLS, COLS)].rearrange("o p k n -> (o p) k n"),
                             layer, step=j, per_step=2 * U, k=i * U)
                for c in range(2):
                    load(f"L{f}_dn{c}", of_layer(dn2[f], layer, c * COLS), layer)

            with sp.Fori(0, layers) as layer:
                swiglu_loads("a", layer)
                for name in ["Lcg", "Lca", "Lkv"]:
                    load(name, of_layer(win2, layer, L_COL[name], width(name)), layer)
                load("Lq", lambda k0, t: win2_flat[:, bass.ds(layer * KD + k0, t), 0:COLS], layer)
                for part in range(2):
                    for c in range(2):
                        load(f"Lout_{'ac'[part]}{c}", of_layer(wout2, layer, c * COLS, k_first=4 * part), layer)
                swiglu_loads("b", layer)
                for c in range(2):
                    load(f"Lple{c}", of_layer(wple, layer, c * COLS), layer)
                for c in range(2):
                    load(f"Lgate{c}", of_layer(wpleg, layer, c * COLS), layer)
            for t in range(TT):
                sp.wait_ge(s_result, t + 1)
                sp.dma_start(out[0, t * P:(t + 1) * P, :], xs[:, t, :]).then_inc(s_out, 16)
            sp.wait_ge(s_out, 16 * TT)

        @block.gpsimd
        def _(pool):
            wait(pool, unit_used, Count(1))
            for i in range(2):
                w = a[["lru_wa", "lru_wx"][i]][0]
                pool.dma_start(w_gates[:, i, :, :], w.rearrange("n d e -> d n e")).then_inc(s_small, 16)
                w = a[["phi_k_w2", "phi_v_w2"][i]][0]
                pool.dma_start(w_phi2[:, i, :, :], w.rearrange("(k p) d -> p k d", p=P)).then_inc(s_small, 16)
            for i in range(12):
                w = a["q_norm_w"][0] if i < HEADS else a["k_norm_w"][0, 1 + (i - HEADS) // KV]
                pool.dma_start(qkw[:, i, :], w.partition_broadcast(P)).then_inc(s_small, 16)
            pool.dma_start(knw[:, :], a["k_norm_w"][0, 0].partition_broadcast(P)).then_inc(s_small, 16)
            pool.memset(kb[:, :, :, :], 0.0).then_inc(s_zero, 1)
            wait(pool, s_h, RESIDUAL.at("d", 2))
            for l in range(LAYERS):
                pool.dma_start(gn[:, l, :], a["ple_norm_2"][l].partition_broadcast(P)).then_inc(s_late, 16)
            pool.dma_start(gn[:, LAYERS, :], a["final_norm_2"].partition_broadcast(P)).then_inc(s_late, 16)
            pool.memset(u_t[:, :, 0:TAPS2 - 1], 0.0).then_inc(s_zero, 1)
            pool.memset(mean, 1.0 / CONV).then_inc(s_zero, 1)
            pool.wait_ge(s_late, 16 * (LAYERS + 1))
            p_rows = a["p_2"].rearrange("l o (t p) n -> p (l o t) n", p=P)
            pool.wait_ge(s_zero, 3)
            with pool.Fori(0, layers) as layer:
                pool.wait_ge(s_cur, layer + 1)
                pool.dma_start(pcur[:, :, :], p_rows[:, bass.ds(layer * TT, TT), :]).then_inc(s_pcur, 16)
                for j in range(1, TAPS2):
                    wait(pool, s_prod, Count(j + 1, [(layer, TAPS2)]))
                    if j > 1:
                        wait(pool, s_ypool, Count(j - 1, [(layer, TAPS2 - 1)]))
                    pool.tensor_tensor(y[:, KC - 2:, :], y[:, KC - 2:, :], prod[:, j % 2, :, :], ALU.add).then_inc(s_ypool, 1)
        @block.scalar
        def _(act):
            def split(name, layer=None, step=None, per_step=0, k=0, units=None):
                for i in units if units is not None else range(N_UNITS[name]):
                    n = UNITS.at(name, i + k, layer, step, per_step)
                    wait(act, landed[n.slot(STAGE)], n.lap(STAGE) + 1, 16)
                    if n.const >= SPLIT:
                        wait(act, unit_used, n + (1 - SPLIT))
                    t, w = tiles_of(name), width(name)
                    act.activation(w_hi[:, n.slot(SPLIT), 0:t, 0:w], stage[:, n.slot(STAGE), 0:t, 0:w],
                                   ACT.Copy).then_inc(hi_done, 1)

            def chunk_done(name, layer=None, step=None, k=0):
                wait(act, unit_used, UNITS.at(name, k * N_UNITS[name] + N_UNITS[name], layer, step, 2 * N_UNITS[name]))
                return CHUNKS.at(name, k, layer, step, 2).slot(2)

            def half_squares(c):
                cols, at = slice(c * COLS, (c + 1) * COLS), STATS["half"] + c * TT
                for t in range(TT):
                    ins = act.activation(xs[:, t, cols], h[:, t, cols], ACT.Square, scale=1.0 / D ** 0.5,
                                         accum_out=stat[:, at + t:at + t + 1])
                if c == 1:
                    ins.then_inc(s_squares, 1)

            def rows_scaled(dst, src, func, at="rstd"):
                for t in range(TT):
                    at_t = STATS[at] + t
                    ins = act.activation(dst(t), src(t), func, scale=stat[:, at_t:at_t + 1])
                return ins

            def rms_boundary(last, norm, dst, gain, first, residual, layer=None):
                n_last, a = N_UNITS[last], min(3, N_UNITS[last] // 2)
                split(last, layer, units=range(min(n_last, a + 3)))
                for k in (0, 1):
                    turned_hi(dst, norm, k, gain, layer)
                wait(act, s_h, RESIDUAL.at(residual, 1, layer))
                half_squares(0)
                split(last, layer, units=range(min(n_last, a + 3), n_last))
                split(first, layer, units=range(3))
                for k in (2, 3):
                    turned_hi(dst, norm, k, gain, layer)
                split(first, layer, units=range(3, U))
                wait(act, s_h, RESIDUAL.at(residual, 2, layer))
                half_squares(1)
                root(stat[:, 0:TT], norm, bias=eps, layer=layer)

            def root(dst, name, scale=1.0, bias=None, layer=None):
                n = ROOTS.at(name, 1, layer)
                wait(act, s_sums, n)
                act.activation(dst, dst, ACT.Sqrt, bias=0.0 if bias is None else bias, scale=scale).then_inc(s_roots, 1)

            def turned_hi(dst, name, k, gain=None, layer=None, step=None, per_step=0, at=None):
                n = TURNS.at(name, k, layer, step, per_step)
                wait(act, turn_done, n + 1)
                bank = turn[n.slot(2)][:, :].rearrange("p (k s) -> p k s", k=2)
                at = 2 * k if at is None else at
                if gain is None:
                    act.activation(dst[:, bass.ds(at, 2), :], bank, ACT.Copy).then_inc(turn_hi, 1)
                else:
                    for i in range(2):
                        ins = act.activation(dst[:, at + i, :], bank[:, i, :], ACT.Copy, scale=gain[:, at + i:at + i + 1])
                    ins.then_inc(turn_hi, 1)

            def turned_copy(dst, name, k, layer=None):
                n = TURNS.at(name, k, layer)
                wait(act, turn_done, n + 1)
                act.activation(dst, turn[n.slot(2)][:, :].rearrange("p (k s) -> p k s", k=2),
                               ACT.Copy).then_inc(turn_free[n.slot(2)], 1)

            def exps(name, j, sink, layer=None):
                w, b = P * (j // PAIRS + 1), j % 2
                wait(act, s_negm, HEAD_PAIRS.at(name, j + 1, layer))
                if sink:
                    act.activation(esink[:, b, :], esink[:, b, :], ACT.Exp)
                for i in range(2):
                    ins = act.activation(sm[:, b, i, 0:w], score[:, i * w:(i + 1) * w], ACT.Exp,
                                         bias=negm[:, b, i:i + 1], accum_out=den[:, b, i:i + 1])
                ins.then_inc(score_free, 1)

            def exps_t(name, j, layer=None):
                t = j // PAIRS
                n = TURNS.at(*turns_of(name, j), layer)
                wait(act, turn_done, n + 1)
                act.activation(p_t[:, :, 0:t + 1, :],
                               turn[n.slot(2)][:, 0:2 * (t + 1) * P].rearrange("p (i s q) -> p i s q", i=2, q=P),
                               ACT.Copy).then_inc(turn_free[n.slot(2)], 1)


            def vector_rows(dst, row, v, done):
                act.dma_start(dst[row:row + v.shape[-1] // P, :], v.rearrange("(r p) -> r p", p=P)).then_inc(done, 16)

            for name, v in [("norm1", a["norm1_w"][0]), ("norm2", a["norm2_w"][0]), ("conv_b", a["conv_b"][0]),
                            ("lam", a["lru_lambda"][0])]:
                vector_rows(raw1, V1[name], v, s_const)
            act.dma_start(raw1[V1["conv_w"]:V1["conv_w"] + TAPS1 * KD, :],
                          a["conv_w"][0].rearrange("j (r p) -> (j r) p", p=P)).then_inc(s_const, 16)
            act.dma_start(raw1[V1["ba"]:V1["ba"] + KD, :], a["lru_ba"][0]).then_inc(s_const, 16)
            act.dma_start(raw1[V1["bx"]:V1["bx"] + KD, :], a["lru_bx"][0]).then_inc(s_const, 16)
            for name in ["k", "v"]:
                act.dma_start(raw1[V1["pos_" + name]:V1["pos_" + name] + KPHI, :],
                              a[f"phi_{name}_pos"][0].rearrange("(j l) d -> j (l d)", l=2)).then_inc(s_const, 16)
            act.wait_ge(s_x, 16 * TT)
            act.wait_ge(s_vec, 1)
            for k in range(4):
                turned_hi(x_hi, "norm1", k, vec1[:, V1["norm1"]:V1["norm1"] + KD])
            split("ks")
            for c in range(2):
                half_squares(c)
            root(stat[:, 0:TT], "norm1", bias=eps)
            for l in range(LAYERS):
                for name, v in [("ffn1", "ffn1_norm_2"), ("mix", "mix_norm_2"), ("ffn2", "ffn2_norm_2"),
                                ("attn", "attn_out_norm_2"), ("conv", "conv_out_norm_2"), ("conv_b", "conv_b_2"),
                                ("ln_g", "conv_ln_g_2"), ("ln_b", "conv_ln_b_2")]:
                    vector_rows(raw2, l * NV2 + V2[name], a[v][l], s_vecs2)
                act.dma_start(rawt[:, l, :], a["conv_w_2"][l].rearrange("j (r p) -> (j r) p", p=P)).then_inc(s_vecs2, 16)
            act.dma_start(sinks[:, :, :], a["sinks_2"].partition_broadcast(P)).then_inc(s_vecs2, 16)
            for t in range(TT):
                act.dma_start(pos_i[:, t:t + 1], a["positions_2"][0, t * P:(t + 1) * P].unsqueeze(1)).then_inc(s_vecs2, 16)
            split("q")
            act.wait_ge(s_lam, 1)
            act.activation(softp[:, 3, :], softp[:, 2, :], ACT.Exp).then_inc(s_elam, 1)
            for i, at in enumerate([C_M1, C_M2]):
                act.activation(masks[:, i, :], ct[:, at:at + S], ACT.Copy)
            act.activation(ident_r[:, :], ident, ACT.Copy).then_inc(s_masks, 1)

            def heads(b, lo, hi):
                return lambda t: acc[b][:, t, lo:hi].rearrange("p (n d) -> p n d", d=HD)

            b = chunk_done("ks")
            act.wait_ge(s_rstd, 1)
            for i in range(2):
                rows_scaled(lambda t: cd[:, t, :, i, :], heads(b, 0, 2 * P), ACT.Copy)
            rows_scaled(lambda t: qk[:, t, HEADS:HEADS + KV, :], heads(b, 2 * P, 3 * P), ACT.Copy)
            rows_scaled(lambda t: vv[:, t, 0, :], lambda t: acc[b][:, t, 3 * P:], ACT.Copy).then_inc(acc_free[b], 1)
            split("kw")
            b = chunk_done("q")
            rows_scaled(lambda t: qk[:, t, 0:HEADS, :], heads(b, 0, COLS), ACT.Copy).then_inc(acc_free[b], 1)
            for k in range(2):
                n = TURNS.at("z", k)
                wait(act, turn_done, n + 1)
                bank = turn[n.slot(2)][:, :].rearrange("p (k s) -> p k s", k=2)
                act.activation(z[0:HD, 2 * k:2 * k + 2, :], bank[0:HD, :, :], ACT.Copy)
                act.activation(z[HD:P, 2 * k:2 * k + 2, 0:S - 1], bank[HD:P, :, 1:S],
                               ACT.Copy).then_inc(turn_free[n.slot(2)], 1)
            split("xr0")
            b = chunk_done("kw")
            rows_scaled(lambda t: qk[:, t, HEADS + KV:, :], heads(b, 0, P), ACT.Copy)
            rows_scaled(lambda t: vv[:, t, 1, :], lambda t: acc[b][:, t, P:2 * P], ACT.Copy)
            rows_scaled(lambda t: gsig[:, t, :, :], lambda t: acc[b][:, t, 2 * P:W_KW].rearrange("p (b n) -> p b n", b=3),
                        ACT.Sigmoid).then_inc(acc_free[b], 1)
            for i in range(2):
                act.wait_ge(s_zj, i + 1)
                act.activation(zj_hi[:, i, :, :], zj[:, :, :, :].rearrange("p j g n -> p j (g n)"),
                               ACT.Copy).then_inc(s_zjhi, 1)
            root(qk_ss[:, :], "qk", bias=eps)
            split("phi_k")

            def xr_rows(c):
                b = chunk_done(f"xr{c}")
                rows_scaled(lambda t: gy[:, t, c * COLS:(c + 1) * COLS], lambda t: acc[b][:, t, :],
                            ACT.Copy).then_inc(acc_free[b], 1)

            xr_rows(0)
            split("xr1")
            split("phi_v")
            xr_rows(1)
            split("yr0")
            wait(act, unit_used, UNITS.at("phi_v", units_of(KPHI)))
            act.activation(ghid[:, :], score[0:ROWS_C, :], ACT.Gelu_apprx_tanh).then_inc(score_free, 1)
            split("yr1")
            for k in range(2):
                turned_copy(q_t[:, 2 * k:2 * k + 2, :], "q", k)
            for k in range(2):
                turned_copy(k_t[:, 2 * k:2 * k + 2, :], "k", k)
            n = TURNS.at("hid")
            wait(act, turn_done, n + 1)
            act.activation(ghid_t[:, :, :],
                           turn[n.slot(2)][:, 0:4 * ROWS_C].rearrange("p (k s) -> p k s", k=4),
                           ACT.Copy).then_inc(turn_free[n.slot(2)], 1)
            act.wait_ge(s_vec, 4)
            for k in range(4):
                turned_copy(x_rt[:, 2 * k:2 * k + 2, TAPS1 - 1:], "xr", k)
            root(kcr[:, ROT:ROT + 1], "kc", bias=eps[0:ROWS_C, :])

            def yr_rows(c):
                b = chunk_done(f"yr{c}")
                rows_scaled(lambda t: gy[:, t, c * COLS:(c + 1) * COLS], lambda t: acc[b][:, t, :],
                            ACT.Gelu_apprx_tanh).then_inc(acc_free[b], 1)

            yr_rows(0)
            split("gm0")
            yr_rows(1)
            for k in range(4):
                for plan, done, free, bank, dst, bias in [
                        (SCORES, score_done, score_free, score, lru_r, "ba"), (OUTS, out_done, out_free, outp, lru_i, "bx")]:
                    wait(act, done, plan.at("gates", k + 1))
                    for m in range(2):
                        f = 2 * k + m
                        ins = act.activation(dst[:, f, :], bank[:, m * S:(m + 1) * S], ACT.Sigmoid,
                                             bias=vec1[:, V1[bias] + f:V1[bias] + f + 1])
                    ins.then_inc(free, 1)
            act.wait_ge(s_pcm, 1)
            act.activation(pc[:, :, :, :], pc[:, :, :, :], ACT.Exp).then_inc(s_pce, 1)
            n = TURNS.at("pc")
            wait(act, turn_done, n + 1)
            act.activation(pc_t[:, :], turn[n.slot(2)][0:HEADS * NCMP, 0:S], ACT.Copy).then_inc(turn_free[n.slot(2)], 1)

            def decay(step):
                half = range(step % 2 * KD // 2, (step % 2 + 1) * KD // 2)
                if step == 0:
                    wait(act, score_free, SCORES.at("gates", 4))
                    act.wait_ge(s_soft, 1)
                if step < 2:
                    for f in half:
                        act.activation(th[:, f, :], lru_r[:, f, :], ACT.Tanh, scale=softp[:, 0, f:f + 1])
                elif step < 4:
                    for f in half:
                        ins = act.activation(lru_r[:, f, :], lru_r[:, f, :], ACT.Exp, scale=softp[:, 1, f:f + 1])
                    if step == 3:
                        ins.then_inc(s_ab, 1)
                elif step == 6:
                    root(den2, "lru")

            def gate_chunk(c):
                b = chunk_done(f"gm{c}")
                rows_scaled(lambda t: gate[:, t, c * COLS:(c + 1) * COLS], lambda t: acc[b][:, t, :],
                            ACT.Sigmoid).then_inc(acc_free[b], 1)

            exps("slc", 0, False)
            for i, (name, j) in enumerate(JOBS):
                if i + 1 < len(JOBS):
                    exps(*JOBS[i + 1], False)
                exps_t(name, j)
                split(BESIDE[i + SPLIT][0], units=[BESIDE[i + SPLIT][1]])
                decay(i)
                if i == U + 2:
                    gate_chunk(0)
                elif i > U + 2 and i % U == 0:
                    gate_chunk(i // U - 1)
                if (name, j) == ("win", YR_AT - 1):
                    for k in range(4):
                        act.wait_ge(s_olru, k + 1)
                        act.activation(lru_hi[:, 2 * k:2 * k + 2, :], xc[:, 2 * k:2 * k + 2, :],
                                       ACT.Copy).then_inc(s_lruhi, 1)
            gate_chunk(3)
            split("nsa0")
            for k in range(2):
                turned_hi(nsa_hi, "nsa", k)
            split("lru1")
            for k in range(2):
                turned_hi(x_hi, "merged", k)
            split("nsa1")
            split("o0", units=range(3))
            for k in range(2, 4):
                turned_hi(x_hi, "merged", k)
            split("o0", units=range(3, U))
            rms_boundary("o1", "norm2", x2_hi, vec1[:, V1["norm2"]:V1["norm2"] + KD], "f0", "o")

            def relu_chunk(i, step=None):
                b = chunk_done("f0", None, step, i)
                rows_scaled(lambda t: relu[:, i % 2, t, :], lambda t: acc[b][:, t, :], ACT.Relu).then_inc(s_rl, 1)

            def ff_hi(i, step=None):
                for m in range(2):
                    k = 2 * i + m
                    turned_hi(f_hi, "ff", k, None, None, step, 4, 2 * k if step is None else step * 8 + 2 * k)

            split("f1")
            act.wait_ge(s_rstd, 2)
            relu_chunk(0)
            with act.Fori(0, NF // 2 - 1) as j:
                for i in (1, 2):
                    split("f0", None, j, 2 * U, (i + 1) * U)
                    relu_chunk(i, j)
                    ff_hi(i - 1, j)
            ff_hi(NF - 2)
            split("d0", units=range(U))
            relu_chunk(NF - 1)
            ff_hi(NF - 1)
            split("d0", units=range(U, N_UNITS["d0"]))
            split("d1")
            act.wait_ge(s_ang, 1)
            for m in range(2):
                act.activation(rope2[:, :, m * HALF:(m + 1) * HALF], ang[:, 1, :, :], ACT.Sin)
            act.activation(rope2[:, :, 2 * HALF:3 * HALF], ang[:, 0, :, :], ACT.Sin, scale=-1.0)
            act.activation(rope2[:, :, 3 * HALF:4 * HALF], ang[:, 0, :, :], ACT.Sin).then_inc(s_rope2, 1)

            def swiglu(f, after, layer):

                def silu_chunk(i, step=None):
                    b = chunk_done(f"L{f}_up0", layer, step, i)
                    rows_scaled(lambda t: silu[:, i % 2, t, :], lambda t: acc[b][:, t, 0:HALFW],
                                ACT.Silu).then_inc(s_rl, 1)

                def hid_hi(i, step=None):
                    turned_hi(g_hi, f"L{f}_hid", i, None, layer, step, 2, 2 * i if step is None else step * 4 + 2 * i)

                split(f"L{f}_up1", layer)
                wait(act, s_rstd, RSTD.at(f"L{f}_norm", 1, layer))
                silu_chunk(0)
                with act.Fori(0, (UPS - 1) // 2 - 1) as j:
                    for i in (1, 2):
                        split(f"L{f}_up0", layer, j, 2 * U, (i + 1) * U)
                        silu_chunk(i, j)
                        hid_hi(i - 1, j)
                split(f"L{f}_up{UPS - 1}", layer)
                silu_chunk(UPS - 2)
                hid_hi(UPS - 3)
                hid_hi(UPS - 2)
                split(f"L{f}_dn0", layer, units=range(U))
                silu_chunk(UPS - 1)
                hid_hi(UPS - 1)
                split(f"L{f}_dn0", layer, units=range(U, N_UNITS[f"L{f}_dn0"]))
                after()

            def mix_boundary():
                rms_boundary("La_dn1", "Lmix", x_hi, vcur[:, V2["mix"]:V2["mix"] + KD], "Lcg", "La_dn", layer)

            def raw_boundary():
                split("Lb_dn1", layer, units=range(3))
                turned_hi(pl_hi, "Lp", 0, None, layer)
                split("Lb_dn1", layer, units=range(3, 6))
                for k in (0, 1):
                    turned_hi(x_hi, "Lraw", k, None, layer)
                split("Lb_dn1", layer, units=range(6, N_UNITS["Lb_dn1"]))
                split("Lple0", layer)
                split("Lple1", layer)
                for k in (2, 3):
                    turned_hi(x_hi, "Lraw", k, None, layer)

            with act.Fori(0, layers) as layer:
                split("La_up0", layer, units=range(2))
                act.wait_ge(s_cur, layer + 1)
                for k in range(4):
                    turned_hi(x2_hi, "La_norm", k, vcur[:, V2["ffn1"]:V2["ffn1"] + KD], layer)
                    if k % 2:
                        split("La_up0", layer, units=[2 + k // 2])
                wait(act, s_h, RESIDUAL.at("La_dn", 0, layer))
                for c in range(2):
                    half_squares(c)
                root(stat[:, 0:TT], "La_norm", bias=eps, layer=layer)
                swiglu("a", mix_boundary, layer)
                split("Lca", layer)
                b = chunk_done("Lcg", layer)
                wait(act, s_rstd, RSTD.at("Lmix", 1, layer))
                rows_scaled(lambda t: sig[:, t, :], lambda t: acc[b][:, t, :], ACT.Sigmoid).then_inc(acc_free[b], 1)
                split("Lkv", layer)
                split("Lq", layer, units=range(2))
                bk = chunk_done("Lkv", layer)
                rows_scaled(lambda t: qk[:, t, HEADS:HEADS + KV, :], heads(bk, 0, P), ACT.Copy)
                rows_scaled(lambda t: vv[:, t, 0, :], lambda t: acc[bk][:, t, P:2 * P], ACT.Copy).then_inc(acc_free[bk], 1)
                act.wait_ge(s_zero, 3)
                for k in range(2):
                    turned_copy(u_t[:, 2 * k:2 * k + 2, TAPS2 - 1:], "Lu", k, layer)
                split("Lq", layer, units=range(2, U))

                def tap_products(lo, hi):
                    for j in range(lo, hi):
                        if j > 2:
                            wait(act, s_ypool, Count(j - 2, [(layer, TAPS2 - 1)]))
                        for n in (KC - 2, KC - 1):
                            w = tcur[:, j * KC + n:j * KC + n + 1]
                            if j == 0:
                                ins = act.activation(y[:, n, :], u_t[:, n, 0:S], ACT.Identity, scale=w,
                                                     bias=vcur[:, V2["conv_b"] + n:V2["conv_b"] + n + 1])
                            else:
                                ins = act.activation(prod[:, j % 2, n - KC + 2, :], u_t[:, n, j:j + S], ACT.Copy, scale=w)
                        ins.then_inc(s_prod, 1)

                for n in TURNS.at("Lu", 0, layer), TURNS.at("Lu", 1, layer):
                    wait(act, turn_free[n.slot(2)], n.lap(2) + 1)
                tap_products(0, EARLY_ACT)
                bq = chunk_done("Lq", layer)
                act.wait_ge(s_qscale, layer + 1)
                rows_scaled(lambda t: qk[:, t, 0:HEADS, :], heads(bq, 0, COLS), ACT.Copy, "q").then_inc(acc_free[bq], 1)
                split("Lout_a0", layer)
                turned_copy(k_t[:, 0:2, :], "Lk", 0, layer)
                for k in range(2):
                    turned_copy(q_t[:, 2 * k:2 * k + 2, :], "Lq", k, layer)
                for j in range(2):
                    exps("Latt", j, True, layer)
                exps_t("Latt", 0, layer)
                for j in range(2 * PAIRS):
                    if j + 2 < 2 * PAIRS:
                        exps("Latt", j + 2, True, layer)
                    if j + 1 < 2 * PAIRS:
                        wait(act, out_done, OUTS.at("Latt", j + 1, layer))
                        exps_t("Latt", j + 1, layer)
                    tap_products(EARLY_ACT + BESIDE_ACT * j, EARLY_ACT + BESIDE_ACT * (j + 1))
                tap_products(EARLY_ACT + BESIDE_ACT * 2 * PAIRS, TAPS2)
                wait(act, s_mixo, Count(2, [(layer, 1)]))
                for k in range(2):
                    turned_hi(x_hi, "Lmixed", k, vcur[:, V2["attn"]:V2["attn"] + 4], layer)
                for t in range(TT):
                    at = STATS["attn"] + t
                    ins = act.activation(xs[:, t, 0:CONV], mixo[:, t, :], ACT.Square, scale=1.0 / CONV ** 0.5,
                                         accum_out=stat[:, at:at + 1])
                ins.then_inc(s_sqattn, 1)
                split("Lout_a1", layer)
                wait(act, score_free, SCORES.at("Lsum", 1, layer))
                act.activation(ysq[:, :, :], y[:, :, :], ACT.Square).then_inc(s_ysq, 1)
                wait(act, score_done, SCORES.at("Lsum", 2, layer))
                act.activation(sig[:, 0, 0:S], score[:, 0:S], ACT.Sqrt, bias=eps).then_inc(score_free, 1)
                act.wait_ge(s_sqattn, layer + 1)
                rows = stat[:, STATS["attn"]:STATS["attn"] + TT]
                act.activation(rows, rows, ACT.Sqrt, bias=eps).then_inc(s_rattn, 1)
                split("Lout_c0", layer)
                wait(act, s_yn, Count(1, [(layer, 1)]))
                for n in range(KC):
                    act.activation(y[:, n, :], y[:, n, :], ACT.Silu, scale=vcur[:, V2["ln_g"] + n:V2["ln_g"] + n + 1],
                                   bias=vcur[:, V2["ln_b"] + n:V2["ln_b"] + n + 1]).then_inc(s_silu, 1)
                wait(act, s_silu, Count(KC, [(layer, KC)]))
                for n in range(KC):
                    ins = act.activation(x_hi[:, 4 + n, :], y[:, n, :], ACT.Copy,
                                         scale=vcur[:, V2["conv"] + n:V2["conv"] + n + 1])
                ins.then_inc(s_convhi, 1)
                act.activation(ysq[:, :, :], y[:, :, :], ACT.Square).then_inc(s_ysq, 1)
                wait(act, score_done, SCORES.at("Lsum", 3, layer))
                act.activation(stat[:, STATS["conv"]:STATS["conv"] + TT], score[:, 0:TT], ACT.Sqrt,
                               bias=eps).then_inc(score_free, 1)
                rms_boundary("Lout_c1", "Lb_norm", x2_hi, vcur[:, V2["ffn2"]:V2["ffn2"] + KD], "Lb_up0", "Lout_c", layer)
                swiglu("b", raw_boundary, layer)
                split("Lgate0", layer, units=range(2))
                for c in range(2):
                    b = chunk_done(f"Lple{c}", layer)
                    for t in range(TT):
                        squared = sig[:, t, :] if c == 0 else ysq[:, 2 * t:2 * t + 2, :].rearrange("p k s -> p (k s)")
                        act.activation(squared, acc[b][:, t, :], ACT.Square, scale=1.0 / D ** 0.5,
                                       accum_out=stat[:, STATS["ple"] + c * TT + t:STATS["ple"] + c * TT + t + 1]).then_inc(s_ple, 1)
                root(stat[:, STATS["e"]:STATS["e"] + TT], "Lple", bias=eps, layer=layer)
                split("Lgate0", layer, units=range(2, 4))
                split("Lgate1", layer)
                for c in range(2):
                    b = chunk_done(f"Lgate{c}", layer)
                    if c == 1:
                        wait(act, s_h, RESIDUAL.at("Lgate", 1, layer))
                    act.activation(sig[:, :, :], acc[b][:, :, :], ACT.Sigmoid).then_inc(acc_free[b], 1)
            act.wait_ge(s_h, 4 + RESIDUAL.per_layer * layers)
            for c in range(2):
                half_squares(c)
            act.wait_ge(s_sums, 5 + ROOTS.per_layer * layers + 1)
            act.activation(stat[:, 0:TT], stat[:, 0:TT], ACT.Sqrt, bias=eps).then_inc(s_roots, 1)

        @block.vector
        def _(dve):
            chain = Chain(dve, dve_chain, DVE_LINKS)
            link = chain.link

            def split(name, layer=None, step=None, per_step=0, k=0, units=None):
                for i in units if units is not None else range(N_UNITS[name]):
                    n = UNITS.at(name, i + k, layer, step, per_step)
                    wait(dve, hi_done, n + 1)
                    t, w = tiles_of(name), width(name)
                    dve.tensor_tensor(w_lo[:, n.slot(SPLIT), 0:t, 0:w], stage[:, n.slot(STAGE), 0:t, 0:w],
                                      w_hi[:, n.slot(SPLIT), 0:t, 0:w].bitcast(F32), ALU.subtract).then_inc(lo_done, 1)

            def chunk_done(name, layer=None):
                wait(dve, unit_used, UNITS.at(name, N_UNITS[name], layer))
                return CHUNKS.at(name, 0, layer).slot(2)

            def rooted(ins, name, layer=None):
                ins.then_inc(s_sums, 1)
                wait(dve, s_roots, ROOTS.at(name, 1, layer))

            def row_factors(name, layer=None):
                wait(dve, s_squares, RSTD.at(name, 1, layer))
                at = STATS["half"]
                rooted(dve.tensor_tensor(stat[:, 0:TT], stat[:, at:at + TT], stat[:, at + TT:at + 2 * TT], ALU.add),
                       name, layer)
                dve.reciprocal(stat[:, 0:TT], stat[:, 0:TT]).then_inc(s_rstd, 1)
                wait(dve, s_rstd, RSTD.at(name, 1, layer))

            def rms_boundary(parts, norm, hi, lo, gain, first, layer=None, at=None, before=lambda: None):
                n_last, a = N_UNITS[parts[1]], min(3, N_UNITS[parts[1]] // 2)
                scale = 0.5 if "dn" in parts[1] else 1.0
                if at is not None:
                    scale = stat[:, STATS[at]:STATS[at] + TT]
                split(parts[1], layer, units=range(min(n_last, 3)))
                before()
                add_residual(parts[0], 0, scale, layer)
                split(parts[1], layer, units=range(3, min(n_last, a + 3)))
                for k in (0, 1):
                    turned_lo(hi, lo, norm, k, gain, layer)
                split(parts[1], layer, units=range(min(n_last, a + 3), n_last))
                split(first, layer, units=range(2))
                add_residual(parts[1], 1, scale, layer)
                split(first, layer, units=range(2, 3))
                for k in (2, 3):
                    turned_lo(hi, lo, norm, k, gain, layer)
                split(first, layer, units=range(3, U))
                row_factors(norm, layer)

            def turned_lo(hi, lo, name, k, gain=None, layer=None, step=None, per_step=0, at=None):
                n = TURNS.at(name, k, layer, step, per_step)
                wait(dve, turn_hi, HI_TURNS.at(name, k + 1, layer, step, per_step))
                bank = turn[n.slot(2)][:, :].rearrange("p (k s) -> p k s", k=2)
                at = 2 * k if at is None else at
                if gain is None:
                    dve.tensor_tensor(lo[:, bass.ds(at, 2), :], bank, hi[:, bass.ds(at, 2), :].bitcast(F32),
                                      ALU.subtract).then_inc(turn_free[n.slot(2)], 1)
                else:
                    for i in range(2):
                        ins = dve.scalar_tensor_tensor(lo[:, at + i, :], bank[:, i, :], gain[:, at + i:at + i + 1],
                                                       hi[:, at + i, :].bitcast(F32), ALU.mult, ALU.subtract)
                    ins.then_inc(turn_free[n.slot(2)], 1)

            def add_residual(name, c, scale, layer=None):
                b = chunk_done(name, layer)
                hc = h[:, :, c * COLS:(c + 1) * COLS]
                if isinstance(scale, float):
                    ins = dve.scalar_tensor_tensor(hc, acc[b][:, :, :], scale, hc, ALU.mult, ALU.add)
                else:
                    for t in range(TT):
                        ins = dve.scalar_tensor_tensor(hc[:, t, :], acc[b][:, t, :], scale[:, t:t + 1], hc[:, t, :],
                                                       ALU.mult, ALU.add)
                ins.then_inc(acc_free[b], 1)
                evacuated(dve, name, layer)
                dve.sem_inc(s_h, 1)

            def rotate(x, table, tmp, x1_x2):
                lo, hi = x1_x2
                dve.tensor_tensor(tmp[0], hi, table(2), ALU.mult)
                link(dve.tensor_tensor(tmp[1], lo, table(3), ALU.mult))
                dve.tensor_tensor(lo, lo, table(0), ALU.mult)
                link(dve.tensor_tensor(hi, hi, table(1), ALU.mult))
                dve.tensor_tensor(lo, lo, tmp[0], ALU.add)
                return dve.tensor_tensor(hi, hi, tmp[1], ALU.add)

            def rotate_heads(first, end, table):
                x, heads = qk[:, :, first:end, :], end - first

                def part(i):
                    return table[:, :, i * HALF:(i + 1) * HALF].unsqueeze(2).to_broadcast([P, TT, heads, HALF])
                return rotate(x, part, [ropet[:, :, first:end, 0:HALF], ropet[:, :, first:end, HALF:ROT]],
                              (x[:, :, :, 0:HALF], x[:, :, :, HALF:ROT]))

            def maxima(name, j, sink, layer=None):
                t, p, b, w = j // PAIRS, j % PAIRS, j % 2, P * (j // PAIRS + 1)
                wait(dve, score_done, SCORES.at(name, j + 1, layer))
                link(dve.tensor_reduce(mx[:, b, :], score[:, 0:2 * w].rearrange("p (i s) -> p i s", i=2), AX_X, ALU.max))
                if sink:
                    of_pair = heads_of(scur[:, :], p).rearrange("q a d -> q (a d)")
                    link(dve.tensor_tensor(mx[:, b, :], mx[:, b, :], of_pair, ALU.max))
                    dve.tensor_tensor(esink[:, b, :], of_pair, mx[:, b, :], ALU.subtract)
                dve.tensor_scalar(negm[:, b, :], mx[:, b, :], -1.0, None, ALU.mult).then_inc(s_negm, 1)

            def output_factors(name, j, branch, sink, layer=None):
                t, p, b = j // PAIRS, j % PAIRS, j % 2
                wait(dve, score_free, SCORES.at(name, j + 1, layer))
                if sink:
                    link(dve.tensor_tensor(den[:, b, :], den[:, b, :], esink[:, b, :], ALU.add))
                link(dve.reciprocal(coef[:, :], den[:, b, :]))
                if branch is not None:
                    link(dve.tensor_tensor(coef[:, :], coef[:, :],
                                           heads_of(gsig[:, t, branch, :], p).rearrange("q a d -> q (a d)"), ALU.mult))

            def weigh_output(name, j, branch, layer=None):
                t, p = j // PAIRS, j % PAIRS
                n = OUTS.at(name, j, layer)
                wait(dve, out_done, n + 1)
                o = heads_of(mixo[:, t, :], p)
                res = outp[:, 0:2 * HD].rearrange("p (n d) -> p n d", d=HD)
                cb = coef[:, :].unsqueeze(2).to_broadcast([P, 2, HD])
                dve.tensor_tensor(o if branch is None else tmpo[:, :, :], res, cb, ALU.mult).then_inc(out_free, 1)
                wait(dve, out_free, n + 1)
                if branch is not None:
                    link(dve.tensor_tensor(o, o, tmpo[:, :, :], ALU.add))

            def vector_in(k, plan, done, free, bank, dst, cols):
                wait(dve, done, plan.at("vec", k + 1))
                dve.tensor_copy(dst, bank[:, 0:cols]).then_inc(free, 1)
                wait(dve, free, plan.at("vec", k + 1))
                dve.sem_inc(s_vec, 1)

            vector_in(0, SCORES, score_done, score_free, score, vec1[:, :], NV1)
            for k in range(4):
                turned_lo(x_hi, x_lo, "norm1", k, vec1[:, V1["norm1"]:V1["norm1"] + KD])
            split("ks")
            row_factors("norm1")
            lam = vec1[:, V1["lam"]:V1["lam"] + KD]
            dve.scalar_tensor_tensor(softp[:, 2, :], lam, -1.0, lam, ALU.mult, ALU.min).then_inc(s_lam, 1)
            split("q")
            dve.wait_ge(s_elam, 1)
            e, z1, z2, s = (softp[:, i, :] for i in (3, 4, 5, 6))
            link(dve.tensor_scalar(z2, e, 2.0, None, ALU.add))
            link(dve.reciprocal(z2, z2))
            link(dve.tensor_tensor(z1, e, z2, ALU.mult))
            link(dve.tensor_tensor(z2, z1, z1, ALU.mult))
            link(dve.tensor_scalar(s, z2, 1.0 / 19, None, ALU.mult))
            for odd in range(17, 1, -2):
                link(dve.scalar_tensor_tensor(s, s, 1.0 / odd, z2, ALU.add, ALU.mult))
            link(dve.scalar_tensor_tensor(s, s, 1.0, z1, ALU.add, ALU.mult))
            link(dve.tensor_scalar(z1, lam, -8.0, 0.0, ALU.mult, ALU.max))
            link(dve.scalar_tensor_tensor(softp[:, 0, :], s, 16.0, z1, ALU.mult, ALU.add))
            dve.tensor_scalar(softp[:, 1, :], softp[:, 0, :], -1.0, None, ALU.mult).then_inc(s_soft, 1)
            split("kw")
            vector_in(0, OUTS, out_done, out_free, outp, vec2[:, :, :].rearrange("p l v -> p (l v)"), LAYERS * NV2)
            vector_in(1, SCORES, score_done, score_free, score, taps2[:, 0, :], TAPS2 * KC)
            vector_in(1, OUTS, out_done, out_free, outp, taps2[:, 1, :], TAPS2 * KC)
            dve.memset(x_rt[:, :, 0:TAPS1 - 1], 0.0)
            split("xr0")
            for i in range(2):
                turn_read(dve, "z", i)
                if i == 1:
                    dve.wait_ge(s_zjlo, 1)
                zi = z[:, 2 * i:2 * i + 2, :]
                src = bass.AP(zi.tensor, zi.offset, [zi.ap[0], [2, KPHI], [S, KV], [CMP_STRIDE, NCMP]])
                pos = vec1[:, V1["pos_" + "kv"[i]]:V1["pos_" + "kv"[i]] + KPHI]
                dve.tensor_tensor(zj[:, :, :, :], src, pos.unsqueeze(2).unsqueeze(3).to_broadcast([P, KPHI, KV, NCMP]),
                                  ALU.add).then_inc(s_zj, 1)
                dve.wait_ge(s_zjhi, i + 1)
                dve.tensor_tensor(zj_lo[:, i, :, :], zj[:, :, :, :].rearrange("p j g n -> p j (g n)"),
                                  zj_hi[:, i, :, :].bitcast(F32), ALU.subtract).then_inc(s_zjlo, 1)
            for name in ["q", "ks", "kw"]:
                evacuated(dve, name)
            dve.wait_ge(s_small, 16 * 17)
            turns_read(dve, "norm1", 4)
            qk_flat = qk[:, :, :, :].rearrange("p t n d -> p t (n d)")
            heads = qk[:, :, :, :].rearrange("p t n d -> p (t n) d")
            ss = qk_ss[:, :]
            link(dve.scalar_tensor_tensor(sq, qk_flat, 1.0 / HD, qk_flat, ALU.mult, ALU.mult))
            rooted(dve.tensor_reduce(ss.rearrange("p (t n) -> p t n", t=TT), sq.rearrange("p t (n d) -> p t n d", d=HD),
                                     AX_X, ALU.add), "qk")
            link(dve.reciprocal(ss, ss))
            ssq = ss.rearrange("p (t n) -> p t n", t=TT)[:, :, 0:HEADS]
            link(dve.tensor_scalar(ssq, ssq, HD ** -0.5, None, ALU.mult))
            link(dve.tensor_tensor(heads, heads, ss.unsqueeze(2).to_broadcast([P, TT * 12, HD]), ALU.mult))
            for t in range(TT):
                ins = dve.tensor_tensor(qk[:, t, :, :], qk[:, t, :, :], qkw[:, :, :], ALU.mult)
            link(ins)
            rotate_heads(0, 12, ct[:, C_ROPE:C_ROPE + TT * 2 * ROT].rearrange("p (t r) -> p t r", t=TT)).then_inc(s_qk, 1)
            dve.wait_ge(s_qk, 1)
            for i in range(2):
                ins = dve.tensor_copy(kd[:, :, :, i, :], qk[:, :, HEADS:, :])
            ins.then_inc(s_kd, 1)
            for name in ["phi_k", "xr1", "phi_v", "yr0", "yr1"]:
                split(name)
            wait(dve, out_done, OUTS.at("kvc", 1))
            dve.tensor_copy(kvc[:, :, :], outp[0:ROWS_C, 0:2 * HD].rearrange("p (i d) -> p i d", i=2)).then_inc(out_free, 1)
            wait(dve, out_free, OUTS.at("kvc", 1))
            kc, rt = kvc[:, 0, :], kcr[:, ROT:ROT + 1]
            link(dve.scalar_tensor_tensor(kcs[:, :], kc, 1.0 / HD, kc, ALU.mult, ALU.mult))
            rooted(dve.tensor_reduce(rt, kcs[:, :], AX_X, ALU.add), "kc")
            link(dve.reciprocal(rt, rt))
            link(dve.scalar_tensor_tensor(kc, kc, rt, knw[0:ROWS_C, :], ALU.mult, ALU.mult))
            link(rotate(kc, lambda i: ct[0:ROWS_C, C_ROPEC + i * HALF:C_ROPEC + (i + 1) * HALF],
                        [kcr[:, 0:HALF], kcr[:, HALF:ROT]], (kc[:, 0:HALF], kc[:, HALF:ROT])))
            for i in range(2):
                ins = dve.tensor_copy(kcd[:, i, :], kc)
            ins.then_inc(s_kcd, 1)
            for k in range(4):
                turn_read(dve, "xr", k)
            for j in range(TAPS1):
                for f in range(KD):
                    wj = vec1[:, V1["conv_w"] + j * KD + f:V1["conv_w"] + j * KD + f + 1]
                    if j == 0:
                        ins = dve.tensor_scalar(xc[:, f, :], x_rt[:, f, 0:S], wj,
                                                vec1[:, V1["conv_b"] + f:V1["conv_b"] + f + 1], ALU.mult, ALU.add)
                    else:
                        ins = dve.scalar_tensor_tensor(xc[:, f, :], x_rt[:, f, j:j + S], wj, xc[:, f, :],
                                                       ALU.mult, ALU.add)
                if j < TAPS1 - 1:
                    link(ins)
            ins.then_inc(s_xc, 1)
            dve.wait_ge(s_zero, 1)
            n = TURNS.at("kc")
            wait(dve, turn_done, n + 1)
            for i in range(2):
                ins = dve.tensor_copy(kb[i * HD:(i + 1) * HD, :, i, :],
                                      turn[n.slot(2)][i * HD:(i + 1) * HD, 0:ROWS_C].rearrange("p (g n) -> p g n", g=KV))
            ins.then_inc(turn_free[n.slot(2)], 1)
            wait(dve, out_done, OUTS.at("vb", 1))
            dve.tensor_tensor(vb[:, :, :], outp[0:HEADS * NCMP, 0:HD].unsqueeze(1).to_broadcast([HEADS * NCMP, HEADS, HD]),
                              ct[0:HEADS * NCMP, C_SELM:C_SELM + HEADS].unsqueeze(2).to_broadcast([HEADS * NCMP, HEADS, HD]),
                              ALU.mult).then_inc(out_free, 1)
            wait(dve, score_done, SCORES.at("cmp", 1))
            mask = ct[:, C_CMASK:C_CMASK + TT * NCMP].rearrange("p (t n) -> p t n", t=TT)
            for t in range(TT):
                ins = dve.tensor_tensor(pc[:, t, :, :], score[:, t * HEADS * NCMP:(t + 1) * HEADS * NCMP].rearrange("p (h n) -> p h n", n=NCMP),
                                        mask[:, t, :].unsqueeze(1).to_broadcast([P, HEADS, NCMP]), ALU.add)
            ins.then_inc(score_free, 1)
            wait(dve, score_free, SCORES.at("cmp", 1))
            pcf = pc[:, :, :, :].rearrange("p t h n -> p (t h) n")
            pmx, pco = (pcs[:, i, :, :].rearrange("p t h -> p (t h)") for i in range(2))
            link(dve.tensor_reduce(pmx, pcf, AX_X, ALU.max))
            dve.tensor_tensor(pcf, pcf, pmx.unsqueeze(2).to_broadcast([P, TT * HEADS, NCMP]), ALU.subtract).then_inc(s_pcm, 1)
            dve.wait_ge(s_pce, 1)
            link(dve.tensor_reduce(pmx, pcf, AX_X, ALU.add))
            link(dve.reciprocal(pco, pmx))
            for t in range(TT):
                ins = dve.scalar_tensor_tensor(pcs[:, 1, t, :], pcs[:, 1, t, :], ct[:, C_ROWOK + t:C_ROWOK + t + 1],
                                               gsig[:, t, 0, :], ALU.mult, ALU.mult)
            link(ins)
            split("gm0")
            for t in range(TT):
                n = OUTS.at("cmp", t)
                wait(dve, out_done, n + 1)
                dve.tensor_tensor(mixo[:, t, :].rearrange("p (h d) -> p h d", d=HD),
                                  outp[:, :].rearrange("p (h d) -> p h d", d=HD),
                                  pcs[:, 1, t, :].unsqueeze(2).to_broadcast([P, HEADS, HD]), ALU.mult).then_inc(out_free, 1)
            def recurrence(step):
                if step == 0:
                    wait(dve, out_free, OUTS.at("gates", 4))
                    dve.tensor_tensor(lru_i[:, :, :], lru_i[:, :, :], xc[:, :, :], ALU.mult).then_inc(s_gated, 1)
                elif step == 4:
                    dve.wait_ge(s_ab, 1)
                    dve.tensor_tensor(den2, lru_r[:, :, :], lru_r[:, :, :], ALU.mult).then_inc(s_gated, 1)
                elif step == 5:
                    dve.wait_ge(s_gated, 2)
                    dve.scalar_tensor_tensor(den2, den2, 1.0, th, ALU.add, ALU.mult).then_inc(s_sums, 1)
                elif step == 7:
                    wait(dve, s_roots, ROOTS.at("lru", 1))
                    dve.tensor_tensor(lru_i[:, :, :], lru_i[:, :, :], den2, ALU.mult).then_inc(s_gated, 1)
                elif step in (8, 9):
                    dve.wait_ge(s_gated, 3)
                    for f in range((step - 8) * KD // 2, (step - 7) * KD // 2):
                        dve.tensor_tensor_scan(xc[:, f, :], lru_r[:, f, :], lru_i[:, f, :], 0.0, ALU.mult,
                                               ALU.add).then_inc(s_scan, 1)

            maxima("slc", 0, False)
            for i, (name, j) in enumerate(JOBS):
                if i + 1 < len(JOBS):
                    maxima(*JOBS[i + 1], False)
                recurrence(i)
                branch = 1 if name == "slc" else 2
                output_factors(name, j, branch, False)
                weigh_output(name, j, branch)
                split(BESIDE[i + SPLIT][0], units=[BESIDE[i + SPLIT][1]])
                if (name, j) == ("win", YR_AT - 1):
                    dve.wait_ge(s_scan, KD)
                    for k in range(4):
                        n = TURNS.at("yr", k)
                        wait(dve, turn_done, n + 1)
                        xk = xc[:, 2 * k:2 * k + 2, :]
                        dve.tensor_tensor(xk, turn[n.slot(2)][:, :].rearrange("p (k s) -> p k s", k=2), xk,
                                          ALU.mult).then_inc(turn_free[n.slot(2)], 1)
                        turn_read(dve, "yr", k)
                        dve.sem_inc(s_olru, 1)
                        dve.wait_ge(s_lruhi, k + 1)
                        dve.tensor_tensor(lru_lo[:, 2 * k:2 * k + 2, :], xk, lru_hi[:, 2 * k:2 * k + 2, :].bitcast(F32),
                                          ALU.subtract).then_inc(s_lrulo, 1)
            dve.sem_inc(s_mixo, 1)
            split("nsa0")
            for k in range(2):
                turned_lo(nsa_hi, nsa_lo, "nsa", k)

            def merge(name, c):
                b = chunk_done(f"{name}{c}")
                side = ["nsa", "lru"].index(name)
                evacuated(dve, f"gm{2 * side + c}")
                gc = gate[:, :, (2 * side + c) * COLS:(2 * side + c + 1) * COLS]
                mc = merged[:, :, c * COLS:(c + 1) * COLS]
                dve.tensor_tensor(mc if name == "lru" else gc, acc[b][:, :, :], gc, ALU.mult).then_inc(acc_free[b], 1)
                evacuated(dve, f"{name}{c}")
                if name == "nsa":
                    dve.tensor_tensor(mc, mc, gc, ALU.add).then_inc(s_merged, 1)

            split("lru1", units=range(2))
            merge("lru", 0)
            split("lru1", units=range(2, U))
            merge("nsa", 0)
            split("nsa1")
            for k in range(2):
                turned_lo(x_hi, x_lo, "merged", k)
            split("o0", units=range(2))
            merge("lru", 1)
            split("o0", units=range(2, 3))
            merge("nsa", 1)
            for k in range(2, 4):
                turned_lo(x_hi, x_lo, "merged", k)
            split("o0", units=range(3, U))
            rms_boundary(["o0", "o1"], "norm2", x2_hi, x2_lo, vec1[:, V1["norm2"]:V1["norm2"] + KD], "f0")

            def square_chunk(i, step=None):
                wait(dve, s_rl, HIDDEN.at("ff", i + 1, None, step, 2))
                n = CHUNKS.at("f0", i, None, step, 2)
                b = n.slot(2)
                for t in range(TT):
                    ins = dve.scalar_tensor_tensor(hid1[:, i % 2, t, :], acc[b][:, t, :], stat[:, t:t + 1],
                                                   relu[:, i % 2, t, :], ALU.mult, ALU.mult)
                ins.then_inc(acc_free[b], 1)

            def ff_lo(i, step=None):
                for m in range(2):
                    k = 2 * i + m
                    turned_lo(f_hi, f_lo, "ff", k, None, None, step, 4, 2 * k if step is None else step * 8 + 2 * k)

            split("f1")
            square_chunk(0)
            with dve.Fori(0, NF // 2 - 1) as j:
                for i in (1, 2):
                    split("f0", None, j, 2 * U, (i + 1) * U)
                    square_chunk(i, j)
                    ff_lo(i - 1, j)
            ff_lo(NF - 2)
            split("d0", units=range(U))
            square_chunk(NF - 1)
            ff_lo(NF - 1)
            split("d0", units=range(U, N_UNITS["d0"]))
            TURN = [float(np.float32(6.28125)), float(np.float32(2 * np.pi - 6.28125)),
                    float(2 * np.pi - 6.28125 - np.float32(2 * np.pi - 6.28125))]
            a0, a1, a2 = (ang[:, i, :, :] for i in range(3))
            link(dve.tensor_copy(pos_f[:, :], pos_i[:, :]))
            link(dve.tensor_tensor(a0, pos_f[:, :].unsqueeze(2).to_broadcast([P, TT, HALF]),
                                   ct[:, C_INV:C_INV + HALF].unsqueeze(1).to_broadcast([P, TT, HALF]), ALU.mult))
            link(dve.tensor_scalar(a1, a0, 0.5 / np.pi, None, ALU.mult))
            link(dve.tensor_scalar(a1, a1, 1.5 * 2 ** 23, None, ALU.add))
            link(dve.tensor_scalar(a1, a1, 1.5 * 2 ** 23, None, ALU.subtract))
            for part in TURN:
                link(dve.scalar_tensor_tensor(a0, a1, -part, a0, ALU.mult, ALU.add))
            link(dve.tensor_scalar(a0, a0, float(np.float32(3.1415925)), -float(np.float32(3.1415925)), ALU.min, ALU.max))
            link(dve.scalar_tensor_tensor(a2, a0, -1.0, a0, ALU.mult, ALU.max))
            dve.tensor_scalar(a1, a2, -1.0, float(np.float32(np.pi / 2)), ALU.mult, ALU.add).then_inc(s_ang, 1)
            split("d1", units=range(U))
            add_residual("d0", 0, 1.0)
            split("d1", units=range(U, N_UNITS["d1"]))

            def swiglu(f, layer):

                def hid_chunk(i, step=None):
                    wait(dve, s_rl, HIDDEN.at(f"L{f}_hid", i + 1, layer, step, 2))
                    b = CHUNKS.at(f"L{f}_up0", i, layer, step, 2).slot(2)
                    for t in range(TT):
                        ins = dve.scalar_tensor_tensor(hid2[:, i % 2, t, :], acc[b][:, t, HALFW:COLS], stat[:, t:t + 1],
                                                       silu[:, i % 2, t, :], ALU.mult, ALU.mult)
                    ins.then_inc(acc_free[b], 1)

                def hid_lo(i, step=None):
                    turned_lo(g_hi, g_lo, f"L{f}_hid", i, None, layer, step, 2, 2 * i if step is None else step * 4 + 2 * i)

                split(f"L{f}_up1", layer)
                hid_chunk(0)
                with dve.Fori(0, (UPS - 1) // 2 - 1) as j:
                    for i in (1, 2):
                        split(f"L{f}_up0", layer, j, 2 * U, (i + 1) * U)
                        hid_chunk(i, j)
                        hid_lo(i - 1, j)
                split(f"L{f}_up{UPS - 1}", layer)
                hid_chunk(UPS - 2)
                hid_lo(UPS - 3)
                hid_lo(UPS - 2)
                split(f"L{f}_dn0", layer, units=range(U))
                hid_chunk(UPS - 1)
                hid_lo(UPS - 1)
                split(f"L{f}_dn0", layer, units=range(U, N_UNITS[f"L{f}_dn0"]))

            def vectors_of(layer):
                dve.tensor_copy(vcur[:, :], vec2[:, bass.ds(layer, 1), :].rearrange("p o v -> p (o v)"))
                dve.tensor_copy(scur[:, :], sinks[:, bass.ds(layer, 1), :].rearrange("p o v -> p (o v)"))
                dve.tensor_copy(tcur[:, :], taps2[:, bass.ds(layer, 1), :].rearrange("p o v -> p (o v)")).then_inc(s_cur, 1)
                dve.wait_ge(s_cur, layer + 1)

            add_residual("d1", 1, 1.0)
            with dve.Fori(0, layers) as layer:
                chain.enter(layer)
                vectors_of(layer)
                split("La_up0", layer, units=range(2))
                for k in range(4):
                    turned_lo(x2_hi, x2_lo, "La_norm", k, vcur[:, V2["ffn1"]:V2["ffn1"] + KD], layer)
                    if k % 2:
                        split("La_up0", layer, units=[2 + k // 2])
                row_factors("La_norm", layer)
                swiglu("a", layer)
                rms_boundary(["La_dn0", "La_dn1"], "Lmix", x_hi, x_lo, vcur[:, V2["mix"]:V2["mix"] + KD], "Lcg", layer)
                at = STATS["q"]
                dve.tensor_scalar(stat[:, at:at + TT], stat[:, 0:TT], HD ** -0.5, None, ALU.mult).then_inc(s_qscale, 1)
                split("Lca", layer)
                split("Lkv", layer)
                b = chunk_done("Lca", layer)
                evacuated(dve, "Lcg", layer)
                for t in range(TT):
                    ins = dve.scalar_tensor_tensor(u[:, t, :], acc[b][:, t, :], stat[:, t:t + 1], sig[:, t, :],
                                                   ALU.mult, ALU.mult)
                ins.then_inc(acc_free[b], 1)
                split("Lq", layer, units=range(2))
                turns_read(dve, "Lu", 2, layer)

                def taps(lo, hi):
                    for j in range(lo, hi):
                        for n in range(KC - 2):
                            w = tcur[:, j * KC + n:j * KC + n + 1]
                            if j == 0:
                                ins = dve.tensor_scalar(y[:, n, :], u_t[:, n, 0:S], w,
                                                        vcur[:, V2["conv_b"] + n:V2["conv_b"] + n + 1], ALU.mult, ALU.add)
                            else:
                                ins = dve.scalar_tensor_tensor(y[:, n, :], u_t[:, n, j:j + S], w, y[:, n, :],
                                                               ALU.mult, ALU.add)
                        if j < TAPS2 - 1:
                            link(ins)
                    return ins

                split("Lq", layer, units=range(2, U))
                evacuated(dve, "Lkv", layer)
                dve.wait_ge(s_rope2, 1)
                rotate_heads(HEADS, HEADS + KV, rope2).then_inc(s_qk, 1)
                wait(dve, s_qk, Count(2, [(layer, 2)]))
                for i in range(2):
                    ins = dve.tensor_copy(kd[:, :, 0:KV, i, :], qk[:, :, HEADS:HEADS + KV, :])
                ins.then_inc(s_kd, 1)
                taps(0, EARLY_DVE)
                evacuated(dve, "Lq", layer)
                rotate_heads(0, HEADS, rope2).then_inc(s_qk, 1)
                split("Lout_a0", layer)
                for j in range(2):
                    maxima("Latt", j, True, layer)
                for j in range(2 * PAIRS):
                    output_factors("Latt", j, None, True, layer)
                    if j + 2 < 2 * PAIRS:
                        maxima("Latt", j + 2, True, layer)
                    weigh_output("Latt", j, None, layer)
                    if j + 1 < 2 * PAIRS:
                        taps(EARLY_DVE + BESIDE_DVE * j, EARLY_DVE + BESIDE_DVE * (j + 1))
                dve.sem_inc(s_mixo, 1)
                taps(EARLY_DVE + BESIDE_DVE * (2 * PAIRS - 1), TAPS2).then_inc(s_y, 1)
                for k in range(2):
                    turned_lo(x_hi, x_lo, "Lmixed", k, vcur[:, V2["attn"]:V2["attn"] + 4], layer)
                rs = sig[:, 0, 0:S]
                over = [P, KC, S]
                wait(dve, score_done, SCORES.at("Lsum", 1, layer))
                dve.scalar_tensor_tensor(y[:, :, :], score[:, 0:S].unsqueeze(1).to_broadcast(over), -1.0, y[:, :, :],
                                         ALU.mult, ALU.add).then_inc(score_free, 1)
                split("Lout_a1", layer)
                wait(dve, score_free, SCORES.at("Lsum", 2, layer))
                link(dve.reciprocal(rs, rs))
                dve.tensor_tensor(y[:, :, :], y[:, :, :], rs.unsqueeze(1).to_broadcast(over), ALU.mult).then_inc(s_yn, 1)
                wait(dve, s_rattn, Count(1, [(layer, 1)]))
                at = STATS["attn"]
                link(dve.reciprocal(stat[:, at:at + TT], stat[:, at:at + TT]))
                split("Lout_c0", layer)
                for c in range(2):
                    add_residual(f"Lout_a{c}", c, stat[:, at:at + TT], layer)
                dve.wait_ge(s_convhi, layer + 1)
                for n in range(KC):
                    ins = dve.scalar_tensor_tensor(x_lo[:, 4 + n, :], y[:, n, :], vcur[:, V2["conv"] + n:V2["conv"] + n + 1],
                                                   x_hi[:, 4 + n, :].bitcast(F32), ALU.mult, ALU.subtract)
                ins.then_inc(s_convlo, 1)

                def conv_factors():
                    at = STATS["conv"]
                    wait(dve, score_free, SCORES.at("Lsum", 3, layer))
                    link(dve.reciprocal(stat[:, at:at + TT], stat[:, at:at + TT]))

                rms_boundary(["Lout_c0", "Lout_c1"], "Lb_norm", x2_hi, x2_lo, vcur[:, V2["ffn2"]:V2["ffn2"] + KD], "Lb_up0",
                             layer, "conv", conv_factors)
                swiglu("b", layer)
                split("Lb_dn1", layer, units=range(3))
                turned_lo(pl_hi, pl_lo, "Lp", 0, None, layer)
                add_residual("Lb_dn0", 0, 0.5, layer)
                split("Lb_dn1", layer, units=range(3, 6))
                for k in (0, 1):
                    turned_lo(x_hi, x_lo, "Lraw", k, None, layer)
                split("Lb_dn1", layer, units=range(6, N_UNITS["Lb_dn1"]))
                split("Lple0", layer)
                add_residual("Lb_dn1", 1, 0.5, layer)
                split("Lple1", layer)
                for k in (2, 3):
                    turned_lo(x_hi, x_lo, "Lraw", k, None, layer)
                split("Lgate0", layer, units=range(2))
                wait(dve, s_ple, Count(4, [(layer, 4)]))
                at, e = STATS["ple"], STATS["e"]
                rooted(dve.tensor_tensor(stat[:, e:e + TT], stat[:, at:at + TT], stat[:, at + TT:at + 2 * TT], ALU.add),
                       "Lple", layer)
                link(dve.reciprocal(stat[:, e:e + TT], stat[:, e:e + TT]))
                for c in range(2):
                    b = chunk_done(f"Lple{c}", layer)
                    for t in range(TT):
                        ins = dve.scalar_tensor_tensor(
                            e_ple[:, t, c * COLS:(c + 1) * COLS], acc[b][:, t, :], stat[:, e + t:e + t + 1],
                            gn[:, bass.ds(layer, 1), c * COLS:(c + 1) * COLS].rearrange("p o n -> p (o n)"),
                            ALU.mult, ALU.mult)
                    ins.then_inc(acc_free[b], 1)
                split("Lgate0", layer, units=range(2, 4))
                split("Lgate1", layer)
                for c in range(2):
                    evacuated(dve, f"Lgate{c}", layer)
                    evacuated(dve, f"Lple{c}", layer)
                    link(dve.tensor_tensor(sig[:, :, :], sig[:, :, :], e_ple[:, :, c * COLS:(c + 1) * COLS], ALU.mult))
                    hc = h[:, :, c * COLS:(c + 1) * COLS]
                    dve.tensor_tensor(hc, hc, sig[:, :, :], ALU.add).then_inc(s_h, 1)
                    wait(dve, s_h, RESIDUAL.at("Lgate", c + 1, layer))
                chain.leave(layers)
            dve.wait_ge(s_squares, 2 + RSTD.per_layer * layers + 1)
            at = STATS["half"]
            dve.tensor_tensor(stat[:, 0:TT], stat[:, at:at + TT], stat[:, at + TT:at + 2 * TT], ALU.add).then_inc(s_sums, 1)
            dve.wait_ge(s_roots, 5 + ROOTS.per_layer * layers + 1)
            link(dve.reciprocal(stat[:, 0:TT], stat[:, 0:TT]))
            for t in range(TT):
                dve.scalar_tensor_tensor(xs[:, t, :], h[:, t, :], stat[:, t:t + 1], gn[:, LAYERS, :],
                                         ALU.mult, ALU.mult).then_inc(s_result, 1)
        @block.tensor
        def _(pe):
            def chunk(name, hi, lo, layer=None, step=None, k=0, ready=lambda kt: None, bank=None,
                      units=None):
                c = CHUNKS.at(name, k, layer, step, 2) if bank is None else None
                w, tiles = width(name), tiles_of(name)
                if bank is None and c.const >= 2 and (units is None or 0 in units):
                    wait(pe, acc_free[c.slot(2)], c.lap(2))
                last = N_UNITS[name] * tiles - 1
                for i in range(N_UNITS[name]) if units is None else units:
                    n = UNITS.at(name, i + k * N_UNITS[name], layer, step, 2 * N_UNITS[name])
                    wait(pe, lo_done, n + 1)
                    for q in range(tiles):
                        kt = i * tiles + q
                        ready(kt)
                        wh, wl = w_hi[:, n.slot(SPLIT), q, 0:w], w_lo[:, n.slot(SPLIT), q, 0:w]
                        for t in range(TT if bank is None else 1):
                            if bank is None:
                                dst = acc[c.slot(2)][:, t, 0:w]
                                xh, xl = hi[:, kt, t * P:(t + 1) * P], lo[:, kt, t * P:(t + 1) * P]
                            else:
                                dst, xh, xl = bank, hi[:, kt, :], lo[:, kt, :]
                            pe.matmul(dst, xh, wh, start=kt == 0, stop=False)
                            pe.matmul(dst, xh, wl, start=False, stop=False)
                            mm = pe.matmul(dst, xl, wh, start=False, stop=kt == last)
                    mm.then_inc(unit_used, 1)

            def turned(name, k, pieces, layer=None, step=None, per_step=0):
                n = TURNS.at(*turns_of(name, k), layer, step, per_step)
                if n.const >= 2:
                    wait(pe, turn_free[n.slot(2)], n.lap(2))
                at = 0
                for src in pieces:
                    rows_in, cols_in = src.shape
                    mm = pe.transpose(turn[n.slot(2)][0:cols_in, at:at + rows_in], src, ident[0:rows_in, 0:rows_in])
                    at += rows_in
                mm.then_inc(turn_done, 1)

            def pieces(src, k):
                return [src[:, t, f * P:(f + 1) * P] for f in (2 * k, 2 * k + 1) for t in range(TT)]

            def turn_rows(name, src, count, layer=None):
                for k in range(count):
                    turned(name, k, pieces(src, k), layer)

            def free(plan, sem_free, name, k, layer=None):
                wait(pe, sem_free, plan.at(name, k, layer))

            def scores(name, j, kbase, mask, layer=None):
                t, p = j // PAIRS, j % PAIRS
                w = P * (t + 1)
                free(SCORES, score_free, name, j, layer)
                half = slice(p % 2 * HD, (p % 2 + 1) * HD)
                for i in range(2):
                    pe.matmul(score[:, i * w:(i + 1) * w], q_t[half, p // 2 * 2 + i, t * P:(t + 1) * P],
                              k_t[half, kbase + p // 2, 0:w], start=True, stop=False)
                    mm = pe.matmul(score[:, i * w:(i + 1) * w], ident_r[:, :], masks[:, mask, S - w:S], start=False, stop=True)
                mm.then_inc(score_done, 1)

            def turn_exps(name, j, layer=None):
                t, b = j // PAIRS, j % 2
                wait(pe, score_free, SCORES.at(name, j + 1, layer))
                turned(name, j, [sm[:, b, i, s * P:(s + 1) * P] for i in range(2) for s in range(t + 1)], layer)

            def values(name, j, branch, layer=None):
                t, g = j // PAIRS, j % PAIRS // 2
                free(OUTS, out_free, name, j, layer)
                turn_read(pe, *turns_of(name, j), layer)
                for i in range(2):
                    for s in range(t + 1):
                        mm = pe.matmul(outp[:, i * HD:(i + 1) * HD], p_t[:, i, s, :],
                                       vv[:, s, branch, g * HD:(g + 1) * HD], start=s == 0, stop=s == t)
                mm.then_inc(out_done, 1)

            pe.wait_ge(s_table, 16)
            pe.wait_ge(s_const, 16 * 9)
            pe.transpose(score[:, 0:NV1], raw1[:, :], ident[0:NV1, 0:NV1]).then_inc(score_done, 1)
            pe.wait_ge(s_x, 16 * TT)
            turn_rows("norm1", h, 4)
            chunk("ks", x_hi, x_lo, ready=lambda kt: turn_read(pe, "norm1", kt // 2) if kt % 2 == 0 else None)
            chunk("q", x_hi, x_lo)
            evacuated(pe, "ks")
            turn_rows("z", cd[:, :, :, :, :].rearrange("p t b i d -> p t (b i d)"), 2)
            pe.wait_ge(s_vecs2, 16 * (9 * LAYERS + 1 + TT))
            pe.transpose(outp[:, 0:LAYERS * NV2], raw2[:, :], ident[0:LAYERS * NV2, 0:LAYERS * NV2]).then_inc(out_done, 1)
            rows_t = TAPS2 * KC
            pe.wait_ge(score_free, 1)
            pe.transpose(score[:, 0:rows_t], rawt[:, 0, :], ident[0:rows_t, 0:rows_t]).then_inc(score_done, 1)
            pe.wait_ge(out_free, 1)
            pe.transpose(outp[:, 0:rows_t], rawt[:, 1, :], ident[0:rows_t, 0:rows_t]).then_inc(out_done, 1)
            chunk("kw", x_hi, x_lo)
            chunk("xr0", x_hi, x_lo)
            free(SCORES, score_free, "hid", 0)
            for i, name in enumerate(phi1):
                pe.wait_ge(s_zjlo, i + 1)
                chunk(name, zj_hi[:, i, :, :], zj_lo[:, i, :, :], bank=score[0:ROWS_C, i * PHI:(i + 1) * PHI])
                if i == 0:
                    chunk("xr1", x_hi, x_lo)
            chunk("yr0", x_hi, x_lo)
            pe.wait_ge(s_qk, 1)
            turn_rows("q", qk[:, :, 0:HEADS, :].rearrange("p t n d -> p t (n d)"), 2)
            pe.wait_ge(s_kd, 1)
            turn_rows("k", kd[:, :, :, :, :].rearrange("p t b i d -> p t (b i d)"), 2)
            wait(pe, score_free, SCORES.at("hid", 1))
            pe.sem_inc(score_done, 1)
            turned("hid", 0, [ghid[:, i * P:(i + 1) * P] for i in range(4)])
            turn_read(pe, "hid", 0)
            free(OUTS, out_free, "kvc", 0)
            for i in range(2):
                for m in range(2):
                    mm = pe.matmul(outp[0:ROWS_C, i * HD:(i + 1) * HD], ghid_t[:, 2 * i + m, :], w_phi2[:, i, m, :],
                                   start=m == 0, stop=m == 1)
            mm.then_inc(out_done, 1)
            for c in range(2):
                evacuated(pe, f"xr{c}")
            turn_rows("xr", gy, 4)
            chunk("yr1", x_hi, x_lo)
            pe.wait_ge(s_kcd, 1)
            turned("kc", 0, [kcd[:, :, :].rearrange("p i d -> p (i d)")])
            free(OUTS, out_free, "vb", 0)
            pe.matmul(outp[0:HEADS * NCMP, 0:HD], ct[0:ROWS_C, C_SEL:C_SEL + HEADS * NCMP], kvc[:, 1, :],
                      start=True, stop=True).then_inc(out_done, 1)
            turn_read(pe, "kc", 0)
            turns_read(pe, "q", 2)
            for t in range(TT):
                for p in range(PAIRS):
                    at = t * HEADS * NCMP + p * 2 * NCMP
                    mm = pe.matmul(score[:, at:at + 2 * NCMP], q_t[:, p, t * P:(t + 1) * P],
                                   kb[:, p // KV, :, :].rearrange("p i n -> p (i n)"), start=True, stop=True)
            mm.then_inc(score_done, 1)
            pe.wait_ge(s_xc, 1)
            pe.wait_ge(s_small, 16 * 17)
            for k in range(4):
                for i, (plan, done, sem_free, bank) in enumerate([(SCORES, score_done, score_free, score),
                                                                  (OUTS, out_done, out_free, outp)]):
                    free(plan, sem_free, "gates", k)
                    for m in range(2):
                        f = 2 * k + m
                        mm = pe.matmul(bank[:, m * S:(m + 1) * S], w_gates[:, i, f, :], xc[:, f, :], start=True, stop=True)
                    mm.then_inc(done, 1)
            pe.wait_ge(s_pce, 1)
            turned("pc", 0, [pc[:, t, :, :].rearrange("p h n -> p (h n)") for t in range(TT)])
            turn_read(pe, "pc", 0)
            for t in range(TT):
                free(OUTS, out_free, "cmp", t)
                pe.matmul(outp[:, :], pc_t[:, t * P:(t + 1) * P], vb[:, :, :].rearrange("p h d -> p (h d)"),
                          start=True, stop=True).then_inc(out_done, 1)
            pe.wait_ge(s_masks, 1)
            turns_read(pe, "k", 2)

            def branch_of(name):
                return 0 if name == "slc" else 1

            scores("slc", 0, 0, 0)
            for i, (name, j) in enumerate(JOBS):
                if i + 1 < len(JOBS):
                    following, k = JOBS[i + 1]
                    scores(following, k, KV * branch_of(following), 0)
                turn_exps(name, j)
                chunk(BESIDE[i][0], x_hi, x_lo, units=[BESIDE[i][1]])
                values(name, j, branch_of(name))
                if (name, j) == ("win", YR_AT - 1):
                    for c in range(2):
                        evacuated(pe, f"yr{c}")
                    turn_rows("yr", gy, 4)
            pe.wait_ge(s_lrulo, 4)

            def attention_in(kt):
                if kt == UNIT_K:
                    pe.wait_ge(s_mixo, 1)
                    turn_rows("nsa", mixo, 2)

            def merged_first(kt):
                if kt == KD // 2:
                    pe.wait_ge(s_merged, 1)
                    for k in (0, 1):
                        turned("merged", k, pieces(merged, k))

            def merged_second(kt):
                if kt == 0:
                    turns_read(pe, "merged", 2)
                elif kt == UNIT_K:
                    pe.wait_ge(s_merged, 2)
                    for k in (2, 3):
                        turned("merged", k, pieces(merged, k))
                elif kt >= KD // 2 and kt % 2 == 0:
                    turn_read(pe, "merged", kt // 2)

            chunk("lru0", lru_hi, lru_lo, ready=attention_in)
            turns_read(pe, "nsa", 2)
            chunk("nsa0", nsa_hi, nsa_lo)
            chunk("lru1", lru_hi, lru_lo, ready=merged_first)
            chunk("nsa1", nsa_hi, nsa_lo)

            def first_half(name, residual, last, layer=None):
                def ready(kt):
                    if kt == UNIT_K * min(3, N_UNITS[last] // 2):
                        wait(pe, s_h, RESIDUAL.at(residual, 1, layer))
                        for k in (0, 1):
                            turned(name, k, pieces(h, k), layer)
                return ready

            def second_half(name, residual, layer=None, count=2):
                def ready(kt):
                    if kt == UNIT_K:
                        wait(pe, s_h, RESIDUAL.at(residual, count, layer))
                        for k in (2, 3):
                            turned(name, k, pieces(h, k), layer)
                    if kt == 0:
                        turns_read(pe, name, 2, layer)
                    elif kt >= KD // 2 and kt % 2 == 0:
                        turn_read(pe, name, kt // 2, layer)
                return ready

            chunk("o0", x_hi, x_lo, ready=merged_second)
            chunk("o1", x_hi, x_lo, ready=first_half("norm2", "o", "o1"))

            def ff_turns(i, step=None):
                n = CHUNKS.at("f0", i, None, step, 2)
                wait(pe, acc_free[n.slot(2)], n.lap(2) + 1)
                for m in range(2):
                    turned("ff", 2 * i + m, pieces(hid1[:, i % 2, :, :], m), None, step, 4)

            chunk("f0", x2_hi, x2_lo, ready=second_half("norm2", "o"))
            with pe.Fori(0, NF // 2 - 1) as j:
                for i in (1, 2):
                    chunk("f0", x2_hi, x2_lo, None, j, i)
                    ff_turns(i - 1, j)
            chunk(f"f{NF - 1}", x2_hi, x2_lo, ready=lambda kt: ff_turns(NF - 2) if kt == KD // 2 else None)

            def last_ff(kt):
                if kt == 0:
                    for m in range(2):
                        turn_read(pe, "ff", 2 * (NF - 2) + m)
                elif kt == UNIT_K:
                    ff_turns(NF - 1)
                elif kt == KF1 - COLS // P:
                    for m in range(2):
                        turn_read(pe, "ff", 2 * (NF - 1) + m)

            chunk("d0", f_hi, f_lo, ready=last_ff)
            chunk("d1", f_hi, f_lo)

            def swiglu(f, layer, first=lambda kt: None, last=lambda kt: None):

                def hid_turns(i, step=None):
                    n = CHUNKS.at(f"L{f}_up0", i, layer, step, 2)
                    wait(pe, acc_free[n.slot(2)], n.lap(2) + 1)
                    turned(f"L{f}_hid", i, pieces(hid2[:, i % 2, :, :], 0), layer, step, 2)

                chunk(f"L{f}_up0", x2_hi, x2_lo, layer, ready=first)
                with pe.Fori(0, (UPS - 1) // 2 - 1) as j:
                    for i in (1, 2):
                        chunk(f"L{f}_up0", x2_hi, x2_lo, layer, j, i)
                        hid_turns(i - 1, j)
                chunk(f"L{f}_up{UPS - 2}", x2_hi, x2_lo, layer)
                hid_turns(UPS - 3)
                chunk(f"L{f}_up{UPS - 1}", x2_hi, x2_lo, layer,
                      ready=lambda kt: hid_turns(UPS - 2) if kt == KD // 2 else None)

                def last_hid(kt):
                    if kt == 0:
                        turn_read(pe, f"L{f}_hid", UPS - 2, layer)
                    elif kt == UNIT_K:
                        hid_turns(UPS - 1)
                    elif kt == KF2 - HALFW // P:
                        turn_read(pe, f"L{f}_hid", UPS - 1, layer)

                chunk(f"L{f}_dn0", g_hi, g_lo, layer, ready=last_hid)
                chunk(f"L{f}_dn1", g_hi, g_lo, layer, ready=last)

            with pe.Fori(0, layers) as layer:
                wait(pe, s_h, RESIDUAL.at("La_dn", -1, layer))
                for k in (0, 1):
                    turned("La_norm", k, pieces(h, k), layer)
                swiglu("a", layer, second_half("La_norm", "La_dn", layer, 0), first_half("Lmix", "La_dn", "La_dn1", layer))
                chunk("Lcg", x_hi, x_lo, layer, ready=second_half("Lmix", "La_dn", layer))
                chunk("Lca", x_hi, x_lo, layer)
                chunk("Lkv", x_hi, x_lo, layer)

                def conv_in(kt):
                    if kt == UNIT_K:
                        evacuated(pe, "Lca", layer)
                        turn_rows("Lu", u, 2, layer)

                chunk("Lq", x_hi, x_lo, layer, ready=conv_in)
                wait(pe, s_kd, Count(2, [(layer, 1)]))
                turned("Lk", 0, pieces(kd[:, :, 0:KV, :, :].rearrange("p t b i d -> p t (b i d)"), 0), layer)
                wait(pe, s_qk, Count(3, [(layer, 2)]))
                turn_rows("Lq", qk[:, :, 0:HEADS, :].rearrange("p t n d -> p t (n d)"), 2, layer)
                turns_read(pe, "Lq", 2, layer)
                turn_read(pe, "Lk", 0, layer)
                for j in range(2):
                    scores("Latt", j, 0, 1, layer)
                turn_exps("Latt", 0, layer)
                for j in range(2 * PAIRS):
                    if j + 2 < 2 * PAIRS:
                        scores("Latt", j + 2, 0, 1, layer)
                    if j + 1 < 2 * PAIRS:
                        turn_exps("Latt", j + 1, layer)
                    values("Latt", j, 0, layer)
                def feature_means(i, src):
                    free(SCORES, score_free, "Lsum", i, layer)
                    for n in range(KC):
                        mm = pe.matmul(score[:, 0:S], mean, src[:, n, :], start=n == 0, stop=n == KC - 1)
                    mm.then_inc(score_done, 1)

                wait(pe, s_mixo, Count(2, [(layer, 1)]))
                turn_rows("Lmixed", mixo, 2, layer)
                pe.wait_ge(s_zero, 3)
                wait(pe, s_y, Count(1, [(layer, 1)]))
                wait(pe, s_ypool, Count(TAPS2 - 1, [(layer, TAPS2 - 1)]))
                feature_means(0, y)
                turns_read(pe, "Lmixed", 2, layer)
                chunk("Lout_a0", x_hi, x_lo, layer)
                wait(pe, s_ysq, Count(1, [(layer, 2)]))
                feature_means(1, ysq)
                chunk("Lout_a1", x_hi, x_lo, layer)
                wait(pe, s_convlo, Count(1, [(layer, 1)]))
                chunk("Lout_c0", x_hi[:, 4:, :], x_lo[:, 4:, :], layer)
                wait(pe, s_ysq, Count(2, [(layer, 2)]))
                free(SCORES, score_free, "Lsum", 2, layer)
                for t in range(TT):
                    for n in range(KC):
                        mm = pe.matmul(score[:, t:t + 1], ysq[:, n, t * P:(t + 1) * P], mean[:, 0:1], start=n == 0,
                                       stop=n == KC - 1)
                mm.then_inc(score_done, 1)
                chunk("Lout_c1", x_hi[:, 4:, :], x_lo[:, 4:, :], layer, ready=first_half("Lb_norm", "Lout_c", "Lout_c1", layer))

                def embedding_in(kt):
                    if kt == 0:
                        wait(pe, s_pcur, Count(1, [(layer, 1)]), 16)
                        turned("Lp", 0, pieces(pcur, 0), layer)
                    half(kt)

                half = first_half("Lraw", "Lb_dn", "Lb_dn1", layer)
                swiglu("b", layer, second_half("Lb_norm", "Lout_c", layer), embedding_in)
                turn_read(pe, "Lp", 0, layer)
                chunk("Lple0", pl_hi, pl_lo, layer)
                wait(pe, s_h, RESIDUAL.at("Lb_dn", 2, layer))
                for k in (2, 3):
                    turned("Lraw", k, pieces(h, k), layer)
                chunk("Lple1", pl_hi, pl_lo, layer)
                turns_read(pe, "Lraw", 2, layer)
                chunk("Lgate0", x_hi, x_lo, layer,
                      ready=lambda kt: turn_read(pe, "Lraw", kt // 2, layer) if kt >= KD // 2 and kt % 2 == 0 else None)
                chunk("Lgate1", x_hi, x_lo, layer)


def kernel(**inputs):
    from concourse import bacc
    from concourse.bass_utils import run_bass_kernel_spmd

    nc = bacc.Bacc("TRN2", target_bir_lowering=False, num_devices=1)
    arrays, aps = {}, {}
    for name, value in inputs.items():
        if name.endswith("w_gate_up_2"):
            value = np.asarray(value).reshape(LAYERS, D, 2, UPS, HALFW).transpose(0, 1, 3, 2, 4).reshape(value.shape)
        arrays[f"in_{name}"] = np.ascontiguousarray(value)
    arrays["in_tables"] = constants()
    for name, value in arrays.items():
        aps[name[3:]] = nc.dram_tensor(name, value.shape, mybir.dt.from_np(value.dtype), kind="ExternalInput").ap()
    out = nc.dram_tensor("out", (1, S, D), F32, kind="ExternalOutput").ap()
    build(nc, aps, aps.pop("tables"), out)
    return run_bass_kernel_spmd(nc, [arrays], core_ids=[0]).results[0]["out"]
```
